# Optimizing a Trainium2 kernel written in Bass

```python
import math
import jax, jax.numpy as jnp
from jax import lax
import numpy as np

D_MODEL = 1024
BATCH = 1
SEQ = 512
DEPTH = 1
DEC_BATCH = 8
DEC_SEQ = 8
PAST_LEN = 256
PAGE_SIZE = 128

SSM_WIDTH = D_MODEL // 2
SSM_GROUP = 16
N_SSM_GROUPS = SSM_WIDTH // SSM_GROUP
SSM_STATE = 64
DT_MIN = 1e-3
DT_MAX = 1e-1
HEAD_DIM = 64
N_Q_HEADS = (D_MODEL // 2) // HEAD_DIM
N_KV_HEADS = 2
GQA = N_Q_HEADS // N_KV_HEADS
CMP_LEN = 32
CMP_STRIDE = 16
SLC_BLOCK = 64
TOP_N = 8
WINDOW = 512
Q_BLOCK = 128
NEG_INF = -1e30
FORCE_BONUS = 1e4
Q_W = N_Q_HEADS * HEAD_DIM
KV_W = 2 * N_KV_HEADS * HEAD_DIM
NSA_GATE_W = 3 * N_Q_HEADS
D_IN_PROJ = SSM_WIDTH + Q_W + 3 * KV_W + NSA_GATE_W + 2 * D_MODEL
N_EXPERT_GROUPS = 4
EXPERTS_PER_GROUP = 4
N_EXPERTS = N_EXPERT_GROUPS * EXPERTS_PER_GROUP
TOP_K_INNER = 2
D_FF_EXPERT = 256
MOE_CHUNK = 2048
PLE_DIM = 256
RMS_EPS = 1e-6

kernel_name = "hybrid_s5_nsa_hmoe_decode_step"

def rms_norm(x, g):
    xf = x.astype(jnp.float32)
    inv = lax.rsqrt(jnp.mean(xf * xf, axis=-1, keepdims=True) + RMS_EPS)
    return (xf * inv * g.astype(jnp.float32)).astype(x.dtype)

def gather_pages(pool, page_table):
    rows = pool[page_table]
    return rows.reshape((rows.shape[0], rows.shape[1] * rows.shape[2]) + rows.shape[3:])

def s5_scan(u, h0, lam_re, lam_im, log_dt, b_re, b_im, c_re, c_im, d_skip):
    f32 = jnp.float32
    n, t, _ = u.shape
    lam = lax.complex(lam_re.astype(f32), lam_im.astype(f32))
    dt = jnp.exp(log_dt.astype(f32))[:, None]
    a_bar = jnp.exp(lam * dt)
    b = lax.complex(b_re.astype(f32), b_im.astype(f32))
    b_bar = ((a_bar - 1.0) / lam)[..., None] * b
    uf = u.astype(f32)
    ug = uf.reshape(n, t, N_SSM_GROUPS, SSM_GROUP)
    bu = lax.complex(jnp.einsum('ntgc,gpc->ntgp', ug, b_bar.real),
                     jnp.einsum('ntgc,gpc->ntgp', ug, b_bar.imag))
    a_seq = jnp.broadcast_to(a_bar, bu.shape)

    def combine(left, right):
        return (left[0] * right[0], right[0] * left[1] + right[1])

    a_cum, h = lax.associative_scan(combine, (a_seq, bu), axis=1)
    if h0 is not None:
        h = h + a_cum * lax.complex(h0[..., 0].astype(f32), h0[..., 1].astype(f32))[:, None]
    y = (jnp.einsum('ntgp,gcp->ntgc', h.real, c_re.astype(f32))
         - jnp.einsum('ntgp,gcp->ntgc', h.imag, c_im.astype(f32)))
    y = y.reshape(n, t, SSM_WIDTH) + d_skip.astype(f32) * uf
    h_last = h[:, -1]
    return y, jnp.stack([h_last.real, h_last.imag], axis=-1)

def compress_blocks(kv, pe, w1, w2):
    n, tp = kv.shape[:2]
    r = CMP_LEN // CMP_STRIDE
    n_chunk = tp // CMP_STRIDE
    n_cmp = n_chunk - r + 1
    chunks = kv.reshape(n, n_chunk, CMP_STRIDE, 2, N_KV_HEADS, HEAD_DIM)
    pre = None
    for s in range(r):
        sl = slice(s * CMP_STRIDE, (s + 1) * CMP_STRIDE)
        pe_s = jnp.swapaxes(pe[:, sl], 0, 1)[:, :, None, :].astype(kv.dtype)
        part = jnp.einsum('ncikhd,kide->nckhe', chunks + pe_s, w1[:, sl].astype(kv.dtype))
        part = part[:, s:s + n_cmp]
        pre = part if pre is None else pre + part
    return jnp.einsum('njkhe,kef->njkhf', jax.nn.gelu(pre), w2.astype(kv.dtype))

def nsa_attention(q, gates, kv_cmp, kv_slc, win_ext, q_pos0, n_pre, cmp_pe, cmp_w1, cmp_w2):
    f32 = jnp.float32
    n, tq = q.shape[:2]
    tk = kv_cmp.shape[1]
    tpad = -(-tk // SLC_BLOCK) * SLC_BLOCK
    padw = ((0, 0), (0, tpad - tk), (0, 0), (0, 0), (0, 0))
    kv_cmp = jnp.pad(kv_cmp.astype(f32), padw)
    kv_slc = jnp.pad(kv_slc.astype(f32), padw)
    cmp = compress_blocks(kv_cmp, cmp_pe, cmp_w1, cmp_w2)
    kc, vc = cmp[:, :, 0], cmp[:, :, 1]
    n_cmp = cmp.shape[1]
    n_slc = tpad // SLC_BLOCK
    ks = kv_slc[:, :, 0].reshape(n, n_slc, SLC_BLOCK, N_KV_HEADS, HEAD_DIM).transpose(0, 3, 1, 2, 4)
    vs = kv_slc[:, :, 1].reshape(n, n_slc, SLC_BLOCK, N_KV_HEADS, HEAD_DIM).transpose(0, 3, 1, 2, 4)
    cmp_start = jnp.arange(n_cmp, dtype=jnp.int32) * CMP_STRIDE
    cmp_end = cmp_start + (CMP_LEN - 1)
    slc_start = jnp.arange(n_slc, dtype=jnp.int32) * SLC_BLOCK
    overlap = ((cmp_start[:, None] <= slc_start[None, :] + (SLC_BLOCK - 1))
               & (cmp_end[:, None] >= slc_start[None, :])).astype(f32)
    k_sel = min(TOP_N, n_slc)
    qb = min(Q_BLOCK, tq)
    n_blk = tq // qb
    lw = n_pre + qb
    win_ext = win_ext.astype(f32)
    b_idx = jnp.arange(n)[:, None, None, None]
    h_idx = jnp.arange(N_KV_HEADS)[None, :, None, None]
    sid = jnp.arange(n_slc, dtype=jnp.int32)

    def block(args):
        q_b, g_b, pos, i = args
        qf = q_b.astype(f32) * (HEAD_DIM ** -0.5)
        s_c = jnp.einsum('nqhgd,njhd->nhgqj', qf, kc)
        m_c = cmp_end[None, :] <= pos[:, None]
        p_c = jax.nn.softmax(jnp.where(m_c, s_c, NEG_INF), axis=-1) * m_c
        o_c = jnp.einsum('nhgqj,njhd->nqhgd', p_c, vc)
        imp = jnp.einsum('nhgqj,js->nhqs', p_c, overlap)
        cur = pos // SLC_BLOCK
        forced = (sid[None, :] == 0) | (sid[None, :] == cur[:, None]) | (sid[None, :] == cur[:, None] - 1)
        imp = jnp.where(forced, imp + FORCE_BONUS, imp)
        imp = jnp.where(slc_start[None, :] <= pos[:, None], imp, NEG_INF)
        _, idx = lax.top_k(imp, k_sel)
        k_g = ks[b_idx, h_idx, idx]
        v_g = vs[b_idx, h_idx, idx]
        kpos = slc_start[idx][..., None] + jnp.arange(SLC_BLOCK, dtype=jnp.int32)
        m_s = (kpos <= pos[None, None, :, None, None]).reshape(n, N_KV_HEADS, 1, qb, k_sel * SLC_BLOCK)
        s_s = jnp.einsum('nqhgd,nhqkld->nhgqkl', qf, k_g).reshape(n, N_KV_HEADS, GQA, qb, k_sel * SLC_BLOCK)
        p_s = jax.nn.softmax(jnp.where(m_s, s_s, NEG_INF), axis=-1)
        p_s = p_s.reshape(n, N_KV_HEADS, GQA, qb, k_sel, SLC_BLOCK)
        o_s = jnp.einsum('nhgqkl,nhqkld->nqhgd', p_s, v_g)
        kw = lax.dynamic_slice_in_dim(win_ext, i * qb, lw, axis=1)
        wpos = q_pos0 - n_pre + i * qb + jnp.arange(lw, dtype=jnp.int32)
        dlt = pos[:, None] - wpos[None, :]
        m_w = (dlt >= 0) & (dlt < WINDOW) & (wpos[None, :] >= 0)
        s_w = jnp.einsum('nqhgd,nkhd->nhgqk', qf, kw[:, :, 0])
        p_w = jax.nn.softmax(jnp.where(m_w, s_w, NEG_INF), axis=-1)
        o_w = jnp.einsum('nhgqk,nkhd->nqhgd', p_w, kw[:, :, 1])
        return g_b[..., 0:1] * o_c + g_b[..., 1:2] * o_s + g_b[..., 2:3] * o_w

    xs = (q.reshape(n, n_blk, qb, N_KV_HEADS, GQA, HEAD_DIM).swapaxes(0, 1),
          gates.reshape(n, n_blk, qb, N_KV_HEADS, GQA, 3).swapaxes(0, 1),
          (q_pos0 + jnp.arange(tq, dtype=jnp.int32)).reshape(n_blk, qb),
          jnp.arange(n_blk, dtype=jnp.int32))
    out = lax.map(block, xs)
    return out.swapaxes(0, 1).reshape(n, tq, N_KV_HEADS, GQA, HEAD_DIM)

def token_mixer(h, q_pos0, past_cmp, past_slc, past_win, h0,
                w_in, lam_re, lam_im, log_dt, b_re, b_im, c_re, c_im, d_skip, w_glu, b_glu,
                cmp_pe, cmp_w1, cmp_w2, w_ssm_out, w_nsa_out, w_o):
    n, t, _ = h.shape
    z = h @ w_in
    cuts = np.cumsum([SSM_WIDTH, Q_W, KV_W, KV_W, KV_W, NSA_GATE_W, D_MODEL]).tolist()
    u, q, kvc, kvs, kvw, g_nsa, g_a, g_b = jnp.split(z, cuts, axis=-1)
    y_ssm, ssm_state = s5_scan(u, h0, lam_re, lam_im, log_dt, b_re, b_im, c_re, c_im, d_skip)
    zg = jax.nn.gelu(y_ssm)
    glu = zg * jax.nn.sigmoid(zg @ w_glu.astype(jnp.float32) + b_glu.astype(jnp.float32))
    kv_shape = (n, t, 2, N_KV_HEADS, HEAD_DIM)
    kvc = kvc.reshape(kv_shape)
    kvs = kvs.reshape(kv_shape)
    kvw = kvw.reshape(kv_shape)
    full_c = kvc if past_cmp is None else jnp.concatenate([past_cmp.astype(kvc.dtype), kvc], axis=1)
    full_s = kvs if past_slc is None else jnp.concatenate([past_slc.astype(kvs.dtype), kvs], axis=1)
    if past_win is None:
        n_pre = WINDOW
        win_ext = jnp.concatenate([jnp.zeros((n, WINDOW, 2, N_KV_HEADS, HEAD_DIM), kvw.dtype), kvw], axis=1)
        new_win = kvw[:, t - min(WINDOW, t):]
    else:
        n_pre = past_win.shape[1]
        win_ext = jnp.concatenate([past_win.astype(kvw.dtype), kvw], axis=1)
        keep = min(WINDOW, n_pre + t)
        new_win = win_ext[:, n_pre + t - keep:]
    qh = q.reshape(n, t, N_KV_HEADS, GQA, HEAD_DIM)
    gh = jax.nn.sigmoid(g_nsa.astype(jnp.float32)).reshape(n, t, N_KV_HEADS, GQA, 3)
    o_nsa = nsa_attention(qh, gh, full_c, full_s, win_ext, q_pos0, n_pre, cmp_pe, cmp_w1, cmp_w2)
    o_nsa = o_nsa.reshape(n, t, Q_W).astype(h.dtype)
    a_br = glu.astype(h.dtype) @ w_ssm_out
    b_br = o_nsa @ w_nsa_out
    merged = jax.nn.sigmoid(g_a) * a_br + jax.nn.sigmoid(g_b) * b_br
    return merged @ w_o, kvc, kvs, new_win, ssm_state

def hier_moe(h, w_rg, b_rg, w_re, b_re, w_gate, w_up, w_down):
    f32 = jnp.float32
    n, t, dm = h.shape
    m = n * t
    c = math.gcd(m, MOE_CHUNK)

    def chunk(hf):
        glog = (hf @ w_rg + b_rg).astype(f32)
        gsel = jnp.argmax(glog, axis=-1)
        gw = jnp.take_along_axis(jax.nn.softmax(glog, axis=-1), gsel[:, None], axis=-1)
        elog = (hf @ w_re + b_re).astype(f32).reshape(c, N_EXPERT_GROUPS, EXPERTS_PER_GROUP)
        elog = jnp.take_along_axis(elog, gsel[:, None, None], axis=1)[:, 0]
        top_v, top_i = lax.top_k(elog, TOP_K_INNER)
        wts = jax.nn.softmax(top_v, axis=-1) * gw
        eid = gsel[:, None] * EXPERTS_PER_GROUP + top_i
        comb = jnp.einsum('cke,ck->ce', jax.nn.one_hot(eid, N_EXPERTS, dtype=f32), wts)
        a = jnp.einsum('cd,edf->cef', hf, w_gate)
        b = jnp.einsum('cd,edf->cef', hf, w_up)
        act = jax.nn.silu(a) * b * comb[..., None].astype(hf.dtype)
        return jnp.einsum('cef,efd->cd', act, w_down)

    return lax.map(chunk, h.reshape(m // c, c, dm)).reshape(n, t, dm)

def setup_inputs(seed: int = 0) -> dict:
    key = jax.random.key(seed)
    keys = iter(jax.random.split(key, 48))

    def nrm(shape, scale):
        return jax.random.normal(next(keys), shape, jnp.float32) * scale

    n_pages = PAST_LEN // PAGE_SIZE
    n_used = DEC_BATCH * n_pages
    n_pool = n_used + n_used // 4
    win_buf = min(WINDOW, PAST_LEN)
    kvt = (2, N_KV_HEADS, HEAD_DIM)
    x_prompt = nrm((BATCH, SEQ, D_MODEL), 1.0)
    x_sample = nrm((DEC_BATCH, DEC_SEQ, D_MODEL), 1.0)
    p_prompt = nrm((DEPTH, BATCH, SEQ, PLE_DIM), 1.0)
    p_sample = nrm((DEPTH, DEC_BATCH, DEC_SEQ, PLE_DIM), 1.0)
    cache_cmp_kv = nrm((DEPTH, n_pool, PAGE_SIZE) + kvt, 1.0)
    cache_slc_kv = nrm((DEPTH, n_pool, PAGE_SIZE) + kvt, 1.0)
    cache_win_kv = nrm((DEPTH, DEC_BATCH, win_buf) + kvt, 1.0)
    state_ssm = nrm((DEPTH, DEC_BATCH, N_SSM_GROUPS, SSM_STATE, 2), 1.0)
    page_table = jax.random.permutation(next(keys), n_pool)[:n_used].reshape(DEC_BATCH, n_pages).astype(jnp.int32)
    norm1_g = 1.0 + nrm((DEPTH, D_MODEL), 0.02)
    w_in = nrm((DEPTH, D_MODEL, D_IN_PROJ), D_MODEL ** -0.5)
    ssm_lam_re = -0.5 + nrm((DEPTH, N_SSM_GROUPS, SSM_STATE), 0.01)
    ssm_lam_im = jnp.pi * jnp.arange(SSM_STATE, dtype=jnp.float32) + nrm((DEPTH, N_SSM_GROUPS, SSM_STATE), 0.01)
    ssm_log_dt = jax.random.uniform(next(keys), (DEPTH, N_SSM_GROUPS), jnp.float32, math.log(DT_MIN), math.log(DT_MAX))
    ssm_b_re = nrm((DEPTH, N_SSM_GROUPS, SSM_STATE, SSM_GROUP), (2 * SSM_GROUP) ** -0.5)
    ssm_b_im = nrm((DEPTH, N_SSM_GROUPS, SSM_STATE, SSM_GROUP), (2 * SSM_GROUP) ** -0.5)
    ssm_c_re = nrm((DEPTH, N_SSM_GROUPS, SSM_GROUP, SSM_STATE), (2 * SSM_STATE) ** -0.5)
    ssm_c_im = nrm((DEPTH, N_SSM_GROUPS, SSM_GROUP, SSM_STATE), (2 * SSM_STATE) ** -0.5)
    ssm_d = nrm((DEPTH, SSM_WIDTH), 1.0)
    w_glu = nrm((DEPTH, SSM_WIDTH, SSM_WIDTH), SSM_WIDTH ** -0.5)
    b_glu = nrm((DEPTH, SSM_WIDTH), 0.02)
    cmp_pe = nrm((DEPTH, 2, CMP_LEN, HEAD_DIM), 0.1)
    cmp_w1 = nrm((DEPTH, 2, CMP_LEN, HEAD_DIM, HEAD_DIM), (CMP_LEN * HEAD_DIM) ** -0.5)
    cmp_w2 = nrm((DEPTH, 2, HEAD_DIM, HEAD_DIM), HEAD_DIM ** -0.5)
    w_ssm_out = nrm((DEPTH, SSM_WIDTH, D_MODEL), SSM_WIDTH ** -0.5)
    w_nsa_out = nrm((DEPTH, Q_W, D_MODEL), Q_W ** -0.5)
    w_o = nrm((DEPTH, D_MODEL, D_MODEL), D_MODEL ** -0.5)
    norm2_g = 1.0 + nrm((DEPTH, D_MODEL), 0.02)
    w_route_group = nrm((DEPTH, D_MODEL, N_EXPERT_GROUPS), D_MODEL ** -0.5)
    b_route_group = nrm((DEPTH, N_EXPERT_GROUPS), 0.01)
    w_route_expert = nrm((DEPTH, D_MODEL, N_EXPERTS), D_MODEL ** -0.5)
    b_route_expert = nrm((DEPTH, N_EXPERTS), 0.01)
    w_exp_gate = nrm((DEPTH, N_EXPERTS, D_MODEL, D_FF_EXPERT), D_MODEL ** -0.5)
    w_exp_up = nrm((DEPTH, N_EXPERTS, D_MODEL, D_FF_EXPERT), D_MODEL ** -0.5)
    w_exp_down = nrm((DEPTH, N_EXPERTS, D_FF_EXPERT, D_MODEL), D_FF_EXPERT ** -0.5)
    w_ple = nrm((DEPTH, PLE_DIM, D_MODEL), PLE_DIM ** -0.5)
    w_ple_gate = nrm((DEPTH, D_MODEL, D_MODEL), D_MODEL ** -0.5)
    final_norm_g = 1.0 + nrm((D_MODEL,), 0.02)
    return {"x_prompt": x_prompt, "x_sample": x_sample, "p_prompt": p_prompt, "p_sample": p_sample,
            "cache_cmp_kv": cache_cmp_kv, "cache_slc_kv": cache_slc_kv, "cache_win_kv": cache_win_kv,
            "state_ssm": state_ssm, "page_table": page_table,
            "norm1_g": norm1_g, "w_in": w_in, "ssm_lam_re": ssm_lam_re, "ssm_lam_im": ssm_lam_im,
            "ssm_log_dt": ssm_log_dt, "ssm_b_re": ssm_b_re, "ssm_b_im": ssm_b_im, "ssm_c_re": ssm_c_re,
            "ssm_c_im": ssm_c_im, "ssm_d": ssm_d, "w_glu": w_glu, "b_glu": b_glu,
            "cmp_pe": cmp_pe, "cmp_w1": cmp_w1, "cmp_w2": cmp_w2,
            "w_ssm_out": w_ssm_out, "w_nsa_out": w_nsa_out, "w_o": w_o, "norm2_g": norm2_g,
            "w_route_group": w_route_group, "b_route_group": b_route_group,
            "w_route_expert": w_route_expert, "b_route_expert": b_route_expert,
            "w_exp_gate": w_exp_gate, "w_exp_up": w_exp_up, "w_exp_down": w_exp_down,
            "w_ple": w_ple, "w_ple_gate": w_ple_gate, "final_norm_g": final_norm_g}

def reference(x_prompt, x_sample, p_prompt, p_sample, cache_cmp_kv, cache_slc_kv, cache_win_kv, state_ssm,
              page_table, norm1_g, w_in, ssm_lam_re, ssm_lam_im, ssm_log_dt, ssm_b_re, ssm_b_im, ssm_c_re,
              ssm_c_im, ssm_d, w_glu, b_glu, cmp_pe, cmp_w1, cmp_w2, w_ssm_out, w_nsa_out, w_o, norm2_g,
              w_route_group, b_route_group, w_route_expert, b_route_expert, w_exp_gate, w_exp_up, w_exp_down,
              w_ple, w_ple_gate, final_norm_g):
    past_len = page_table.shape[1] * PAGE_SIZE

    def layer(x, p_l, l, q_pos0, past_cmp, past_slc, past_win, h0):
        h = rms_norm(x, norm1_g[l])
        mix, kvc, kvs, new_win, ssm_st = token_mixer(
            h, q_pos0, past_cmp, past_slc, past_win, h0,
            w_in[l], ssm_lam_re[l], ssm_lam_im[l], ssm_log_dt[l], ssm_b_re[l], ssm_b_im[l],
            ssm_c_re[l], ssm_c_im[l], ssm_d[l], w_glu[l], b_glu[l], cmp_pe[l], cmp_w1[l], cmp_w2[l],
            w_ssm_out[l], w_nsa_out[l], w_o[l])
        x = x + mix
        x = x + hier_moe(rms_norm(x, norm2_g[l]), w_route_group[l], b_route_group[l], w_route_expert[l],
                         b_route_expert[l], w_exp_gate[l], w_exp_up[l], w_exp_down[l])
        x = x + jax.nn.sigmoid(x @ w_ple_gate[l]) * (p_l @ w_ple[l])
        return x, kvc, kvs, new_win, ssm_st

    xp = x_prompt
    st_p = []
    for l in range(DEPTH):
        xp, *st = layer(xp, p_prompt[l], l, 0, None, None, None, None)
        st_p.append(st)
    xs = x_sample
    st_s = []
    for l in range(DEPTH):
        xs, *st = layer(xs, p_sample[l], l, past_len,
                        gather_pages(cache_cmp_kv[l], page_table),
                        gather_pages(cache_slc_kv[l], page_table),
                        cache_win_kv[l], state_ssm[l])
        st_s.append(st)
    y_prompt = rms_norm(xp, final_norm_g)
    y_sample = rms_norm(xs, final_norm_g)
    new_cmp_kv_prompt = jnp.stack([s[0] for s in st_p])
    new_slc_kv_prompt = jnp.stack([s[1] for s in st_p])
    new_win_kv_prompt = jnp.stack([s[2] for s in st_p])
    new_ssm_prompt = jnp.stack([s[3] for s in st_p])
    new_cmp_kv_sample = jnp.stack([s[0] for s in st_s])
    new_slc_kv_sample = jnp.stack([s[1] for s in st_s])
    new_win_kv_sample = jnp.stack([s[2] for s in st_s])
    new_ssm_sample = jnp.stack([s[3] for s in st_s])
    return (y_prompt, y_sample, new_cmp_kv_prompt, new_slc_kv_prompt, new_win_kv_prompt, new_ssm_prompt,
            new_cmp_kv_sample, new_slc_kv_sample, new_win_kv_sample, new_ssm_sample)


_drawn_inputs = setup_inputs


def setup_inputs(seed=0):
    import zlib

    import numpy as np

    out = dict(_drawn_inputs(seed))
    spreads = {}
    factors = {'norm1_g': 2.837,
     'ssm_lam_re': 19.285,
     'b_glu': 8.0,
     'b_route_expert': 5.267,
     'final_norm_g': 7.394,
     'norm2_g': 3.612,
     'b_route_group': 5.769}
    for name, (base, spread) in spreads.items():
        noise = np.random.default_rng([zlib.crc32(name.encode()), seed]).standard_normal(out[name].shape)
        drawn = base * np.exp(spread * noise) if base else spread * noise
        out[name] = __import__('jax').numpy.asarray(drawn.astype(out[name].dtype))
    for name, factor in factors.items():
        out[name] = (out[name] * factor).astype(out[name].dtype)
    return out
```

```python
from contextlib import ExitStack
import math

import numpy as np

import concourse.bass as bass
from concourse import mybir

F32 = mybir.dt.float32
BF16 = mybir.dt.bfloat16
I32 = mybir.dt.int32
ALU = mybir.AluOpType
ACT = mybir.ActivationFunctionType
X = mybir.AxisListType.X

P = 128
D = 1024
KD = D // P
NP_, NSEQ, NDEC = 512, 8, 8
ROWS = NP_ + NSEQ * NDEC
HALF = ROWS // 2
TILES = [128, 128, 128, 128, 64]
NT = len(TILES)
PAST, PAGE = 256, 128
SSM_W, GRP, NG, NST = 512, 16, 32, 64
CH = 8
NCH = ROWS // CH
NPC = NP_ // CH
NS = NG // 2
HD, NH, NKV, GQA = 64, 8, 2, 4
KVW = 256
COL_Q, COL_KV, COL_GA, COL_GB = 512, 1024, 1816, 2840
NKVG = 3 * KVW + 3 * NH
SCALE = HD ** -0.5
NEG = -1e30
CL, CS = 32, 16
CT0 = CL
CTOK = CT0 + NP_ + NSEQ * PAST
NBLK = CTOK // CS - 1
CJ_P = CT0 // CS
CJ_S = CJ_P + NP_ // CS
SJ = PAST // CS
NE, FF = 16, 256
PLE = 256
EPS = 1e-6
RING = 6
GELU = ACT.Gelu_apprx_tanh


class Plan:

    def __init__(self):
        self.at, self.by, self.count, self.order = {}, {}, {}, []

    def add(self, key, engine):
        self.at[key] = len(self.order)
        self.order.append(key)
        self.count[engine] = self.count.get(engine, 0) + 1
        self.by[key] = (engine, self.count[engine])

    def done(self, key):
        return self.at[key] + 1


def attention_items():
    items = []
    for b in range(4):
        items += [("c", b, 0, 0)]
        items += [("p", b, r, h) for r in (1, 2) for h in range(NH)]
    for t in range(NSEQ // 2):
        items += [("sc", t, 0, 0), ("s", t, 1, 0), ("s", t, 2, 0)]
    return items


ITEMS = attention_items()
GROUPS = []
for _i, _it in enumerate(ITEMS):
    if GROUPS and (ITEMS[GROUPS[-1][-1]][:3] == _it[:3]):
        GROUPS[-1].append(_i)
    else:
        GROUPS.append([_i])
GROUP_OF = {i: g for g, m in enumerate(GROUPS) for i in m}
T_LAG, V_LAG, O_LAG = 2, 3, 2


def item_keys(it):
    kind, b = it[0], it[1]
    if kind == "p":
        return [128] * (b + 1)
    if kind == "c":
        return [128, 128]
    return [32] if kind == "sc" else [128, 128, 64]


def attention_steps():
    steps, late = [], []
    n = len(ITEMS)
    for i in range(n + V_LAG + O_LAG):
        if i < n:
            steps.append(("score", i))
        if 0 <= i - T_LAG < n:
            steps.append(("turn", i - T_LAG))
        if 0 <= i - V_LAG < n:
            j = i - V_LAG
            steps.append(("value", j))
            if j == GROUPS[GROUP_OF[j]][-1]:
                steps.append(("gather", GROUP_OF[j]))
                if ITEMS[j][2] == 2:
                    late.append((i + O_LAG, GROUP_OF[j]))
        if late and late[0][0] == i:
            steps.append(("out", late.pop(0)[1]))
    return steps


def make_plan():
    p = Plan()
    for t in range(NT):
        for k in range(2):
            p.add(("hT", t, k), "dve")
    for t in range(NT):
        p.add(("u", t), "act")
    for t in range(NT):
        for c in range(2):
            p.add(("kv", t, c), "act")
    p.add(("lam",), "dve")
    p.add(("c", 0), "dve")
    p.add(("c", 1), "dve")
    p.add(("h0",), "dve")
    for i in range(5):
        p.add(("x", i), "dve")
    for i in range(8):
        p.add(("vt", i), "act")
    for i in range(8):
        p.add(("k", i), "act")
    for i in range(6):
        p.add(("d", i), "act")
    for m in range(4):
        for h in range(2):
            p.add(("q", m, h), "act")
    for i in range(8):
        p.add(("y", i), "dve")
    p.add(("fin",), "act")
    for t in range(CH):
        p.add(("zg", t), "dve")
    for m in range(4):
        for h in range(2):
            p.add(("glu", m, h), "act")
    p.add(("pe",), "act")
    for i in range(10):
        p.add(("ct", i), "act")
    for k in range(2):
        p.add(("pre", k), "dve")
    p.add(("kc",), "dve")
    p.add(("vcp",), "dve")
    p.add(("vcs",), "dve")
    for r in range(2):
        p.add(("ktp", r), "act")
    p.add(("ktn",), "act")
    for r in range(2):
        for i in range(4):
            p.add(("kts", r, i), "act")
    for what, i in attention_steps():
        if what == "score":
            p.add(("s", i), "act")
        elif what == "turn":
            p.add(("t", i), "dve" if i % 2 else "act")
        elif what == "out":
            p.add(("o", i), "dve")
    for m in range(KD):
        for h in range(2):
            for w, e in (("ga", "act"), ("ab", "dve"), ("gb", "act"), ("bb", "dve")):
                p.add((w, m, h), e)
    for t in range(NT):
        for c in range(2):
            p.add(("wo", t, c), "dve")
    for t in range(NT):
        for k in range(2):
            p.add(("h2T", t, k), "dve")
        p.add(("rt", t), "dve")
    for t in range(NT):
        p.add(("pT", t), "act")
    for t in range(NT):
        for k in range(2):
            p.add(("x2T", t, k), "dve" if k else "act")
        for c in range(2):
            p.add(("pg", t, c), "act")
            p.add(("pp", t, c), "dve")
    return p


PLAN = make_plan()

WEIGHTS = [("u", ("u", NT - 1)), ("kv0", ("kv", NT - 1, 0)), ("kv1", ("kv", NT - 1, 1)), ("q", ("q", 3, 1)),
           ("glu", ("glu", 3, 1))]
WEIGHTS += [(f"m{m}", ("bb", m, 1)) for m in range(KD)]
WEIGHTS += [("wo0", ("wo", NT - 1, 0)), ("wo1", ("wo", NT - 1, 1)), ("ple", ("pp", NT - 1, 1)),
            ("pg0", ("pg", NT - 1, 0)), ("pg1", ("pg", NT - 1, 1))]
NW = 3
W_AT = {name: i for i, (name, _) in enumerate(WEIGHTS)}


def build(nc, I, O):
    (y_prompt, y_sample, o_cmp_p, o_slc_p, o_win_p, o_ssm_p, o_cmp_s, o_slc_s, o_win_s, o_ssm_s) = O
    u_dram = nc.dram_tensor("u_rows", (ROWS, SSM_W), F32).ap()
    g_dram = nc.dram_tensor("gate_rows", (NSEQ * NDEC, 3 * NH), F32).ap()
    k_dram = nc.dram_tensor("kernel_taps", (GRP, NG, P), F32).ap()
    w_in = I["w_in"][0]
    n_pool = I["cache_cmp_kv"].shape[1]
    PARS = 16 * 13

    with ExitStack() as ctx:
        def sem(name):
            return ctx.enter_context(nc.semaphore(name))

        def sb(name, shape, dt=F32, stack=ctx):
            return stack.enter_context(nc.sbuf_tensor(name, shape, dt))

        def flat(t):
            return (t if isinstance(t, bass.AP) else t[:]).rearrange("p a b -> p (a b)")

        ps = ctx.enter_context(nc.psum_tensor("ps", [P, 8, 512], F32))
        ident = sb("ident", [P, P])
        ident_b = sb("ident_b", [P, P], BF16)
        causal = sb("causal", [P, P], BF16)
        new_mask = sb("new_mask", [P, 4, 64], BF16)
        g_cols = sb("g_cols", [P, 2, KD])
        halfneg = sb("halfneg", [P, 1])
        stat = sb("stat", [P, 4, 8])
        b_glu = sb("b_glu", [P, 4])
        ptab = sb("ptab", [1, 2 * NSEQ], I32)
        ring = [sb(f"w_slot{i}", [P, 4096]) for i in range(NW)]
        hT = sb("hT", [P, KD, ROWS])
        kv = sb("kv", [P, NT, NKVG])
        tgate = sb("tgate", [P, NT, 3 * NH])
        tgate_s = sb("tgate_s", [P, 4, 3])
        qg_t = sb("qg", [P, 2 * 4 * ROWS])
        qT = qg_t[:, 0:4 * ROWS].rearrange("p (g n) -> p g n", g=GQA)
        gluT = qg_t[:, 4 * ROWS:].rearrange("p (k n) -> p k n", k=4)
        ucg = qg_t[0:NCH, 0:CH * SSM_W].rearrange("p (g n) -> p g n", g=NG)

        with ExitStack() as s5:
            x_in = sb("x_in", [P, NT, D], stack=s5)
        with ExitStack() as s5:
            pw = sb("pw", [P, CH + 1, 2, NS], stack=s5)
            pwr = sb("pwr", [P, CH, 2, NS], stack=s5)
            sm = sb("sm", [P, 24, NS], stack=s5)
            bbar = sb("bbar", [P, 2, NS, GRP], stack=s5)
            vt = sb("vt", [P, NS * 2, P], stack=s5)
            zgT = vt[:].rearrange("p a b -> p (a b)")[:, 0:4 * ROWS].rearrange("p (k n) -> p k n", k=4)
            gm = sb("gm", [P, 2, NS, CH + 1, GRP], stack=s5)
            xg_t = sb("xg", [P, NT * SSM_W], stack=s5)
            u_rows = xg_t[:].rearrange("p (t n) -> p t n", t=NT)
            xg = xg_t[:, 0:NG * NCH].rearrange("p (g n) -> p g n", g=NG)
            hst = sb("hst", [P, 2, NS, NCH], stack=s5)
            fin = sb("fin", [P, 2, 1 + NSEQ, NS], stack=s5)
            walk = sb("walk", [P, 4, 2, NS], stack=s5)
            vn_t = sb("vn", [P, NS * 2 * P], stack=s5)
            vn = vn_t[:].rearrange("p (s r n) -> p s r n", s=NS, r=2)
            wt = vn_t[:].rearrange("p (g n) -> p g n", g=NG)
            uc_t = sb("uc", [P, 2 * NS * (CH + 1) * GRP], stack=s5)
            uc = uc_t[0:NCH, 0:CH * SSM_W].rearrange("p (t n) -> p t n", t=CH)
            tmp_v = uc_t[:, 0:NS * (CH + 1) * GRP]
            tmp_g = uc_t[:, NS * (CH + 1) * GRP:]
            lam_r = sb("lam_r", [NS, 2, P], stack=s5)
            raw = sb("raw", [P, 1024], stack=s5)
            c_r = hst[:].rearrange("p r s c -> p (r s c)")[:, 0:1024].rearrange("p (r b u n) -> p r b u n", r=2, b=4, u=2)
            b_r = raw[:, 512:1024].rearrange("p (r s c) -> p r s c", r=2, s=NS)
            ks = raw[0:GRP, :].rearrange("p (u g n) -> p u g n", u=2, g=4)
            cst = sb("cst", [P, 2, NS, GRP], stack=s5)
            tmp9 = cst[:].rearrange("p r s c -> p (r s c)")[:, 0:2 * 9 * NS].rearrange("p (r q s) -> p r q s", r=2, q=9)
            h0_r = sb("h0_r", [P, 2 * P], stack=s5)
            fo = h0_r[:].rearrange("p (n r) -> p n r", r=2)
            fo_p = sb("fo_p", [NS, P, 2], stack=s5)
            d_b = sb("d_b", [NCH, SSM_W], stack=s5)
            ldt = sb("ldt", [P, NS], stack=s5)

        with ExitStack() as late:
            onsaT = sb("onsaT", [P, 4, ROWS], stack=late)
            with ExitStack() as at:
                w1_t = sb("w1", [P, 2 * CL * P], stack=at)
                w1 = w1_t[:].rearrange("p (k i e) -> p k i e", k=2, i=CL)
                caches = w1_t[:].rearrange("p (r s h n) -> p r s h n", r=2, s=NSEQ, h=2)
                kvct_t = sb("kvct", [P, 2 * CTOK], stack=at)
                kvct = kvct_t[:].rearrange("p (k n) -> p k n", k=2)
                kts = kvct_t[:, 0:2 * NSEQ * PAST].rearrange("p (r s n) -> p r s n", r=2, s=NSEQ)
                w2 = sb("w2", [P, 2, P], stack=at)
                pe_r = sb("pe_r", [2 * CL, 2, HD], stack=at)
                cxr = sb("cxr", [P, 4, 32], stack=at)
                rawc = sb("rawc", [P, 4, 2, KVW], stack=at)
                cx = sb("cx", [P, 2, 2, NBLK], stack=at)
                cc = sb("cc", [P, 2], stack=at)
                kc = sb("kc", [P, NBLK], stack=at)
                vcbd = sb("vcbd", [P, NKV, GQA, HD], stack=at)
                vcs = sb("vcs", [32, 4, P], stack=at)
                kt = sb("kt", [P, 2, ROWS], stack=at)
                qpad = sb("qpad", [P, NSEQ, P], stack=at)
                pb = rawc[:].rearrange("p b t n -> p (b t n)")[:, 0:3 * 512].rearrange("p (b n) -> p b n", b=3)
                pt = sb("pt", [P, 2, 512], stack=at)
                ob = sb("ob", [P, 2, 512], stack=at)
                tmp_o = sb("tmp_o", [P, 512], stack=at)
                sct = sb("sct", [P, 256], stack=at)
                osd = sb("osd", [P, 2, 2, HD], stack=at)
                nm = sb("nm", [P, len(ITEMS)], stack=at)
                rs = sb("rs", [P, len(ITEMS)], stack=at)
                mx8 = sb("mx8", [P, NH], stack=at)
                rs8 = sb("rs8", [P, NH], stack=at)
                w8 = sb("w8", [P, 2, NH], stack=at)
                cm01 = sb("cm01", [P, 4, 32], stack=at)
                cmneg = sb("cmneg", [P, 4, 32], stack=at)
                csneg = sb("csneg", [P, 3, 32], stack=at)
                sel4 = sb("sel4", [P, 4], stack=at)
                rowi = sb("rowi", [P, 3], I32, stack=at)
                rowf = sb("rowf", [P, 4], stack=at)
                nmk = sb("nmk", [P, 3, 4, 64], stack=at)
            with ExitStack() as fin_s:
                merged = sb("merged", [P, KD, ROWS], stack=fin_s)
                x = sb("x", [P, NT, D], stack=fin_s)
                tg = sb("tg", [P, 4, HALF], stack=fin_s)
                mt = sb("mt", [P, 2, HALF], stack=fin_s)
                hn = sb("hn", [P, 2, D], stack=fin_s)
                w_rt = sb("w_rt", [P, KD, 20], stack=fin_s)
                b_rt = sb("b_rt", [P, 20], stack=fin_s)
                lg = sb("lg", [P, NT, 20], stack=fin_s)
                rtmp = sb("rtmp", [P, 12, NT, 4], stack=fin_s)
                r16 = sb("r16", [P, NT, 16], stack=fin_s)
                comb = sb("comb", [P, NT, NE], stack=fin_s)
                wgu = sb("wgu", [P, 2, 2, KD, FF], stack=fin_s)
                wdn = flat(merged)[:, 0:4 * D].rearrange("p (u k n) -> p u k n", u=2, k=2)
                th = sb("th", [P, 2, HALF], stack=fin_s)
                si = sb("si", [P, 2, HALF], stack=fin_s)
                actT = flat(onsaT).rearrange("p (u f n) -> p u f n", u=2, f=2)
                p_in = flat(kv)[:, 0:NT * PLE].rearrange("p (t n) -> p t n", t=NT)
                pT = flat(kv)[:, NT * PLE:NT * PLE + 2 * ROWS].rearrange("p (k n) -> p k n", k=2)
                gf = flat(kv)[:, NT * PLE + 2 * ROWS:NT * PLE + 2 * ROWS + D]
                tpg = flat(qT)[:, 0:1024].rearrange("p (u n) -> p u n", u=2)

        pe_done = sem("pe_done")
        drained = {"dve": sem("dve_drained"), "act": sem("act_drained")}
        dve_step, act_step, pool_step = sem("dve_step"), sem("act_step"), sem("pool_step")
        x_ld = [sem(f"x_loaded{t}") for t in range(NT)]
        w_ld = [sem(f"w_loaded{i}") for i in range(NW)]
        gains_ld, par_ld, rt_ld, gf_ld, p_ld = sem("gains_loaded"), sem("s5_params_loaded"), sem("router_loaded"), sem("final_gain_loaded"), sem("ple_rows_loaded")
        consts = sem("constants_made")
        sq_done, rstd_done = sem("sum_squares"), sem("rstd_made")
        u_out, uc_ld, k_out, w_toep = sem("u_written"), sem("u_by_chunks"), [sem(f"taps_written{u}") for u in range(2)], sem("toeplitz_loaded")
        dt_done, angles, trig = sem("dt_made"), sem("angles_made"), sem("sin_cos_made")
        powers, v_made, g_made = sem("powers_made"), sem("v_made"), sem("g_made")
        half_done = sem("first_kv_head_done")
        ucg_made = sem("u_by_groups")
        w_zero, ud_made, walked, y_gelu = sem("toeplitz_zeroed"), sem("skip_made"), sem("states_walked"), sem("y_activated")
        glu_made, fin_out, outs = sem("glu_made"), sem("states_written"), sem("outputs_written")
        gates_made, gd_out, gs_ld = sem("gates_made"), sem("gates_written"), sem("sample_gates_loaded")
        pt_ld = sem("page_table_loaded")
        w1_zero, w1_ld, pe_ld, raw_ld = sem("w1_zeroed"), sem("w1_loaded"), sem("embeddings_loaded"), [sem(f"raw_pages{i}") for i in range(4)]
        cache_ld = sem("caches_loaded")
        cmp_g = sem("cmp_gelu")
        masks, row_masks, qpad_made = sem("masks_made"), sem("row_masks_made"), sem("qpad_made")
        bglu_half, si_made = sem("glu_bias_halved"), sem("silu_made")
        s_max, s_prob, s_val, s_gath = sem("score_max"), sem("probabilities"), sem("values_done"), sem("values_taken")
        osd_made = sem("sample_outputs")
        merged_made = sem("merged_made")
        x_res, hn_made = sem("x_reloaded"), sem("hn_made")
        lg_made, lg_exp, comb_made = sem("logit_diffs"), sem("logit_exps"), sem("combine_weights")
        e_ld = [sem(f"expert_loaded{u}") for u in range(2)]
        up_done, th_made, act_made = sem("gate_up_done"), sem("gate_tanh"), sem("act_made")
        dn_done, dn_free = sem("down_done"), sem("down_used")
        x3_made, y_made = sem("x3_made"), sem("y_made")

        def bank(key):
            return ps[:, PLAN.at[key] % RING, :]

        def freed(key):
            last = PLAN.order[PLAN.at[key] - RING]
            return drained[PLAN.by[last][0]], PLAN.by[last][1]

        def emptied(key):
            return drained[PLAN.by[key][0]], PLAN.by[key][1]

        w_parts = {"m%d" % m: 4 for m in range(KD)} | {"q": KD * NKV}
        w_need, total = {}, [0] * NW
        for i, (name, _) in enumerate(WEIGHTS):
            total[i % NW] += 16 * w_parts.get(name, 1)
            w_need[name] = (w_ld[i % NW], total[i % NW])

        def slot(name):
            return ring[W_AT[name] % NW]

        def wk(name, n, at=0, k=KD):
            return slot(name)[:, at:at + k * n].rearrange("p (k n) -> p k n", k=k)

        block = ctx.enter_context(nc.Block())

        @block.sync
        def _(sp):
            xp = I["x_prompt"][0].rearrange("(t p) d -> p t d", p=P)
            xs = I["x_sample"].rearrange("s q d -> (s q) d")

            def rows(src, t, dst):
                a = src[0][:, t, :] if t < 4 else src[1]
                return sp.dma_start(dst[0:TILES[t], t, :], a)

            def load_weights(name):
                i = W_AT[name]
                if i >= NW:
                    sp.wait_ge(pe_done, PLAN.done(WEIGHTS[i - NW][1]))
                s = w_ld[i % NW]

                def one(src, at, n, k=KD):
                    sp.dma_start(slot(name)[:, at:at + k * n].rearrange("p (k n) -> p k n", k=k),
                                 src.rearrange("(k p) n -> p k n", p=P)).then_inc(s, 16)
                if name == "u":
                    one(w_in[:, 0:512], 0, 512)
                elif name == "kv0":
                    one(w_in[:, COL_KV:COL_KV + 396], 0, 396)
                elif name == "kv1":
                    one(w_in[:, COL_KV + 396:COL_GA], 0, 396)
                elif name == "q":
                    for k in range(KD):
                        for h in range(NKV):
                            sp.dma_start(slot(name)[:, 512 * k:512 * k + 512].rearrange("p (m h n) -> p h m n", m=GQA, h=NKV)[:, h],
                                         w_in[P * k:P * k + P, COL_Q + 256 * h:COL_Q + 256 * h + 256].rearrange("p (m n) -> p m n", m=GQA)
                                         ).then_inc(s, 16)
                elif name == "glu":
                    one(I["w_glu"][0], 0, 512, 4)
                elif name[:2] == "wo":
                    c = int(name[2:])
                    one(I["w_o"][0][:, 512 * c:512 * c + 512], 0, 512)
                elif name == "ple":
                    one(I["w_ple"][0], 0, D, 2)
                elif name[:2] == "pg":
                    c = int(name[2:])
                    one(I["w_ple_gate"][0][:, 512 * c:512 * c + 512], 0, 512)
                else:
                    m = int(name[1:])
                    one(w_in[:, COL_GA + P * m:COL_GA + P * m + P], 0, P)
                    one(w_in[:, COL_GB + P * m:COL_GB + P * m + P], 1024, P)
                    one(I["w_ssm_out"][0][:, P * m:P * m + P], 2048, P, 4)
                    one(I["w_nsa_out"][0][:, P * m:P * m + P], 2560, P, 4)

            for t in range(NT):
                rows((xp, xs), t, x_in).then_inc(x_ld[t], 16)
            for name in ("u", "kv0", "kv1"):
                load_weights(name)
            for t in range(NT):
                sp.wait_ge(*emptied(("u", t)))
                sp.dma_start(u_dram[P * t:P * t + TILES[t], :], u_rows[0:TILES[t], t, :]).then_inc(u_out, 16)
            load_weights("q")
            sp.wait_ge(*emptied(("kv", NT - 1, 1)))
            for n, (op, os) in enumerate(((o_cmp_p, o_cmp_s), (o_slc_p, o_slc_s), (o_win_p, None))):
                sp.dma_start(op[0, 0].rearrange("(t p) a h d -> p t (a h d)", p=P),
                             kv[:, 0:4, KVW * n:KVW * n + KVW]).then_inc(outs, 16)
                if os is not None:
                    sp.dma_start(os[0].rearrange("s q a h d -> (s q) (a h d)"),
                                 kv[0:64, 4, KVW * n:KVW * n + KVW]).then_inc(outs, 16)
            for s in range(NSEQ):
                sp.dma_start(o_win_s[0, s, PAST:PAST + NDEC].rearrange("q a h d -> q (a h d)"),
                             kv[NDEC * s:NDEC * s + NDEC, 4, 2 * KVW:3 * KVW]).then_inc(outs, 16)
            sp.dma_start(o_win_s[0, :, 0:PAST].rearrange("s p a h d -> s (p a h d)"),
                         I["cache_win_kv"][0].rearrange("s p a h d -> s (p a h d)")).then_inc(outs, 16)
            n_outs = 16 * (3 + 2 + NSEQ + 1)
            sp.wait_ge(u_out, 16 * NT)
            sp.wait_ge(v_made, 1)
            sp.wait_ge(g_made, 1)
            sp.dma_start(uc, u_dram.rearrange("(c t) n -> c t n", t=CH)).then_inc(uc_ld, 16)
            sp.wait_ge(gates_made, NT + 2)
            sp.dma_start(g_dram, tgate[0:64, NT - 1, :]).then_inc(gd_out, 16)
            sp.wait_ge(gd_out, 16)
            gv = g_dram.rearrange("(t a q) (k g r) -> a k g q t r", a=2, q=NDEC, k=NKV, g=GQA)
            for a in range(2):
                for k in range(NKV):
                    for g in range(GQA):
                        row = 64 * a + 32 * k + NDEC * g
                        sp.dma_start(tgate_s[row:row + NDEC], gv[a, k, g]).then_inc(gs_ld, 16)
            load_weights("glu")
            for i in range(8):
                sp.wait_ge(*emptied(("k", i)))
                sp.dma_start(k_dram[:, 8 * (i // 2) + i % 2:8 * (i // 2) + i % 2 + 7:2, :], ks[:, i % 2, :, :]).then_inc(k_out[i % 2], 16)
            for u in range(2):
                sp.wait_ge(k_out[u], 16 * 4)
            sp.wait_ge(w_zero, 1)
            for t in range(CH):
                sp.dma_start(wt[GRP * t:GRP * t + GRP, :, GRP * t:P], k_dram[:, :, 0:P - GRP * t]).then_inc(w_toep, 16)
            load_weights("m0")
            sp.wait_ge(*emptied(("fin",)))
            sp.dma_start(o_ssm_s[0].rearrange("q (s g) n r -> (q s) (g n r)", g=2),
                         fo.rearrange("p n r -> p (n r)")).then_inc(fin_out, 16)
            sp.dma_start(o_ssm_p[0, 0].rearrange("(s g) n r -> s (g n r)", g=2),
                         fo_p[:].rearrange("p n r -> p (n r)")).then_inc(fin_out, 16)

            sp.wait_ge(fin_out, 32)
            sp.wait_ge(glu_made, 8)
            for u in range(2):
                sp.dma_start(pe_r[:, u], I["cmp_pe"][0].rearrange("k i d -> (k i) d")).then_inc(pe_ld, 16)
            sp.wait_ge(pt_ld, 16)
            pages = [[None] * 2 for _ in range(NSEQ)]

            def page(s, u):
                return sp.value_load(ptab[0:1, 2 * s + u:2 * s + u + 1], min_val=0, max_val=n_pool - 1)

            def load_raw(s):
                for u in range(2):
                    sp.dma_start(rawc[:, s % 4, u, :],
                                 I["cache_cmp_kv"][0, bass.ds(page(s, u), 1)].rearrange("o p a h d -> (o p) (a h d)")
                                 ).then_inc(raw_ld[s % 4], 16)
            for s in range(4):
                load_raw(s)
            sp.wait_ge(w1_zero, 1)
            for h in range(NKV):
                for k in range(2):
                    sp.dma_start(w1[HD * h:HD * h + HD, k, :, HD * h:HD * h + HD],
                                 I["cmp_w1"][0][k].rearrange("i d e -> d i e")).then_inc(w1_ld, 16)
                sp.dma_start(w2[HD * h:HD * h + HD, :, HD * h:HD * h + HD],
                             I["cmp_w2"][0].rearrange("k d e -> d k e")).then_inc(w1_ld, 16)
            for s in range(4, NSEQ):
                sp.wait_ge(pe_done, PLAN.done(("ct", 2 + s - 4)))
                load_raw(s)
            load_weights("m1")
            sp.wait_ge(pe_done, PLAN.done(("pre", 1)))
            sp.dma_start(caches[:, 1], I["cache_win_kv"][0].rearrange("s (h p) a b d -> p s h (a b d)", p=P)
                         ).then_inc(cache_ld, 16)
            for s in range(NSEQ):
                for u in range(2):
                    sp.dma_start(caches[:, 0, s, u, :],
                                 I["cache_slc_kv"][0, bass.ds(page(s, u), 1)].rearrange("o p a h d -> (o p) (a h d)")
                                 ).then_inc(cache_ld, 16)
            load_weights("m2")
            for m in range(3, KD):
                load_weights(f"m{m}")
                if m == 3:
                    sp.wait_ge(pe_done, PLAN.done(("o", len(GROUPS) - 1)))
                    sp.wait_ge(*emptied(("o", len(GROUPS) - 1)))
                    for t in range(NT):
                        rows((xp, xs), t, x).then_inc(x_res, 16)
                    sp.dma_start(w_rt[:, :, 0:4], I["w_route_group"][0].rearrange("(k p) n -> p k n", p=P)).then_inc(rt_ld, 16)
                    sp.dma_start(w_rt[:, :, 4:20], I["w_route_expert"][0].rearrange("(k p) n -> p k n", p=P)).then_inc(rt_ld, 16)
                    sp.dma_start(b_rt[:, 0:4], I["b_route_group"].broadcast_to([P, 4])).then_inc(rt_ld, 16)
                    sp.dma_start(b_rt[:, 4:20], I["b_route_expert"].broadcast_to([P, 16])).then_inc(rt_ld, 16)
            load_weights("wo0")
            load_weights("wo1")

            def load_gate_up(e, u):
                one = bass.ds(e, 1) if not isinstance(e, int) else slice(e, e + 1)
                sp.dma_start(wgu[:, u, 0], I["w_exp_gate"][0, one].rearrange("o (k p) n -> p (o k) n", p=P)).then_inc(e_ld[u], 16)
                sp.dma_start(wgu[:, u, 1], I["w_exp_up"][0, one].rearrange("o (k p) n -> p (o k) n", p=P)).then_inc(e_ld[u], 16)

            def load_down(e, u):
                one = bass.ds(e, 1) if not isinstance(e, int) else slice(e, e + 1)
                sp.dma_start(wdn[:, u], I["w_exp_down"][0, one].rearrange("o (k p) n -> p (o k) n", p=P)).then_inc(e_ld[u], 16)
            for u in range(2):
                load_gate_up(u, u)
            sp.wait_ge(outs, n_outs)
            sp.dma_start(gf, I["final_norm_g"].rearrange("(o n) -> o n", o=1).broadcast_to([P, D])).then_inc(gf_ld, 16)
            sp.dma_start(p_in[:, 0:4], I["p_prompt"][0, 0].rearrange("(t p) n -> p t n", p=P)).then_inc(p_ld, 16)
            sp.dma_start(p_in[0:64, 4], I["p_sample"][0].rearrange("s q n -> (s q) n")).then_inc(p_ld, 16)
            load_weights("ple")
            sp.wait_ge(pe_done, PLAN.done(("wo", NT - 1, 1)))
            for u in range(2):
                load_down(u, u)
            load_weights("pg0")
            load_weights("pg1")
            with sp.Fori(1, NE // 2) as i:
                for u in range(2):
                    sp.wait_ge(dn_done, i * 20 + 10 * (u - 1))
                    load_gate_up(i * 2 + u, u)
                    load_down(i * 2 + u, u)
            ysm = y_sample.rearrange("s q d -> (s q) d")
            for t in range(NT):
                sp.wait_ge(y_made, t + 1)
                dst = y_prompt[0][P * t:P * t + P, :] if t < 4 else ysm
                sp.dma_start(dst, x[0:TILES[t], t, :]).then_inc(outs, 16)
            sp.wait_ge(outs, n_outs + 16 * NT)

        @block.gpsimd
        def _(pool):
            count = [0]

            def link(ins):
                count[0] += 1
                ins.then_inc(pool_step, 1)
                pool.wait_ge(pool_step, count[0])

            link(pool.memset(ident[:], 0.0))
            link(pool.affine_select(out=ident[:], in_=ident[:], compare_op=ALU.not_equal, fill=1.0, base=0,
                                    pattern=[[-1, P]], channel_multiplier=1))
            pool.tensor_copy(ident_b[:], ident[:]).then_inc(consts, 1)
            link(pool.memset(causal[:], 0.0))
            pool.affine_select(out=causal[:], in_=causal[:], compare_op=ALU.is_ge, fill=NEG, base=0,
                               pattern=[[-1, P]], channel_multiplier=1).then_inc(consts, 1)
            link(pool.memset(halfneg[:], -0.5))

            def rstd(t, at):
                p = TILES[t]
                link(pool.tensor_scalar(stat[0:p, 1, t:t + 1], stat[0:p, 0, t:t + 1], 1.0 / D, EPS, ALU.mult, ALU.add))
                pool.tensor_tensor(stat[0:p, 2, t:t + 1], stat[0:p, 1, t:t + 1], halfneg[0:p], ALU.pow).then_inc(rstd_done, 1)

            for t in range(NT):
                pool.wait_ge(sq_done, t + 1)
                rstd(t, 0)

            pool.wait_ge(powers, 1)
            pool.wait_ge(*emptied(("c", 1)))
            n9 = [P, NS, CH + 1, GRP]
            pr = pw[:, :, 0, :].rearrange("p t s -> p s t").unsqueeze(3).broadcast_to(n9)
            pi = pw[:, :, 1, :].rearrange("p t s -> p s t").unsqueeze(3).broadcast_to(n9)
            cr = cst[:, 0].unsqueeze(2).broadcast_to(n9)
            ci = cst[:, 1].unsqueeze(2).broadcast_to(n9)
            tg9 = tmp_g.rearrange("p (s t c) -> p s t c", s=NS, t=CH + 1)
            link(pool.tensor_tensor(gm[:, 0], pr, cr, ALU.mult))
            link(pool.tensor_tensor(tg9, pi, ci, ALU.mult))
            link(pool.tensor_tensor(gm[:, 0], gm[:, 0], tg9, ALU.subtract))
            link(pool.tensor_tensor(gm[:, 1], pi, cr, ALU.mult))
            link(pool.tensor_tensor(tg9, pr, ci, ALU.mult))
            link(pool.tensor_tensor(gm[:, 1], gm[:, 1], tg9, ALU.add))
            pool.tensor_scalar(gm[:, 1], gm[:, 1], -1.0, None, ALU.mult).then_inc(g_made, 1)
            pool.wait_ge(pe_done, PLAN.done(("vt", 7)))
            pool.memset(vn_t[:], 0.0).then_inc(w_zero, 1)
            pool.wait_ge(pe_done, PLAN.done(("x", 4)))
            pool.wait_ge(par_ld, PARS)
            pool.tensor_tensor(uc, uc, d_b[:].unsqueeze(1).broadcast_to([NCH, CH, SSM_W]), ALU.mult).then_inc(ud_made, 1)
            pool.wait_ge(*emptied(("d", 5)))
            pool.wait_ge(*emptied(("h0",)))
            link(pool.tensor_scalar(walk[:, 0, 0], pw[:, CH, 0], 1.0, None, ALU.mult))
            link(pool.tensor_scalar(walk[:, 0, 1], pw[:, CH, 0], 1.0, None, ALU.mult))
            link(pool.tensor_scalar(walk[:, 1, 0], pw[:, CH, 1], -1.0, None, ALU.mult))
            link(pool.tensor_scalar(walk[:, 1, 1], pw[:, CH, 1], 1.0, None, ALU.mult))
            base = count[0]
            with pool.Fori(0, NPC - 1) as c:
                now, nxt = bass.ds(c, 1), bass.ds(c + 1, 1)

                def h(r, at):
                    return (hst[:, r, :, at] if r is not None else hst[:, :, :, at])
                pool.tensor_tensor(walk[:, 2].unsqueeze(3), walk[:, 0].unsqueeze(3), hst[:, :, :, now], ALU.mult)
                pool.tensor_tensor(walk[:, 3, 0].unsqueeze(2), walk[:, 1, 0].unsqueeze(2), hst[:, 1, :, now], ALU.mult)
                pool.tensor_tensor(walk[:, 3, 1].unsqueeze(2), walk[:, 1, 1].unsqueeze(2), hst[:, 0, :, now], ALU.mult
                                   ).then_inc(pool_step, 1)
                pool.wait_ge(pool_step, c * 3 + (base + 1))
                pool.tensor_tensor(walk[:, 2], walk[:, 2], walk[:, 3], ALU.add).then_inc(pool_step, 1)
                pool.wait_ge(pool_step, c * 3 + (base + 2))
                pool.tensor_tensor(hst[:, :, :, nxt], hst[:, :, :, nxt], walk[:, 2].unsqueeze(3), ALU.add
                                   ).then_inc(pool_step, 1)
                pool.wait_ge(pool_step, c * 3 + (base + 3))
            count[0] = base + 3 * (NPC - 1)
            nine = [P, 1 + NSEQ, NS]
            hv = [hst[:, r, :, NPC - 1:NCH].rearrange("p s c -> p c s") for r in range(2)]
            a8 = [pw[:, CH, r].unsqueeze(1).broadcast_to(nine) for r in range(2)]
            t9 = [tmp9[:, j] for j in range(2)]
            for r, (p0, p1, op) in enumerate(((0, 1, ALU.subtract), (1, 0, ALU.add))):
                pool.tensor_tensor(t9[0], hv[p0], a8[0], ALU.mult)
                link(pool.tensor_tensor(t9[1], hv[p1], a8[1], ALU.mult))
                link(pool.tensor_tensor(t9[0], t9[0], t9[1], op))
                link(pool.tensor_tensor(fin[:, r], fin[:, r], t9[0], ALU.add))
            pool.memset(walk[:, 0, 0, 0:1], 0.0).then_inc(walked, 1)

            pool.wait_ge(fin_out, 32)
            pool.wait_ge(glu_made, 8)
            pool.memset(w2[:], 0.0)
            pool.memset(w1_t[:], 0.0).then_inc(w1_zero, 1)
            link(pool.memset(cm01[:], 1.0))
            link(pool.affine_select(out=cm01[:], in_=cm01[:], compare_op=ALU.is_ge, fill=0.0, base=-(CL - 1),
                                    pattern=[[P, 4], [-CS, 32]], channel_multiplier=1))
            pool.tensor_scalar(cmneg[:], cm01[:], -NEG, NEG, ALU.mult, ALU.add)
            link(pool.memset(sel4[:], 1.0))
            link(pool.affine_select(out=sel4[:], in_=sel4[:], compare_op=ALU.is_ge, fill=0.0, base=0,
                                    pattern=[[-32, 4]], channel_multiplier=1))
            link(pool.affine_select(out=sel4[:], in_=sel4[:], compare_op=ALU.is_ge, fill=0.0, base=31,
                                    pattern=[[32, 4]], channel_multiplier=-1))
            link(pool.iota(rowi[:, 0:1], [[0, 1]], base=0, channel_multiplier=1))
            link(pool.iota(csneg[:, 0, :], [[1, 32]], base=0, channel_multiplier=0, allow_small_or_imprecise_dtypes=True))
            pool.iota(nmk[:, 0], [[-16, 4], [1, 64]], base=0, channel_multiplier=0,
                      allow_small_or_imprecise_dtypes=True).then_inc(masks, 1)
            pool.memset(vcbd[:], 0.0).then_inc(masks, 1)
            link(pool.memset(qpad[:], 0.0))
            pool.wait_ge(*emptied(("q", 3, 1)))
            for k in range(NKV):
                for par in range(2):
                    dstq = qpad[HD * k:HD * k + HD].rearrange("p (s two) n -> p s two n", two=2)[:, :, par,
                                64 * par + 32 * k:64 * par + 32 * k + 32].rearrange("p s (g q) -> p s g q", g=GQA)
                    srcq = qT[HD * k:HD * k + HD, :, NP_:ROWS].rearrange("p g (s two q) -> p s two g q", two=2, q=NDEC)[:, :, par]
                    pool.tensor_copy(dstq, srcq).then_inc(qpad_made, 1)
            for t in range(NT):
                pool.wait_ge(sq_done, NT + t + 1)
                rstd(t, 1)
            for t in range(NT):
                pool.wait_ge(sq_done, 2 * NT + t + 1)
                rstd(t, 2)

        @block.tensor
        def _(pe):
            def begin(key):
                if PLAN.at[key] >= RING:
                    pe.wait_ge(*freed(key))
                return bank(key)

            def finish(ins):
                ins.then_inc(pe_done, 1)

            def product(out, pairs):
                for n, (a, b) in enumerate(pairs):
                    ins = pe.matmul(out, a, b, start=(n == 0), stop=(n == len(pairs) - 1))
                return ins

            pe.wait_ge(consts, 1)
            for t in range(NT):
                p = TILES[t]
                pe.wait_ge(hn_made, t + 1)
                for k in range(2):
                    o = begin(("hT", t, k))
                    for j in range(4):
                        ins = pe.transpose(o[:, j * P:j * P + p], x_in[0:p, t, (4 * k + j) * P:(4 * k + j + 1) * P], ident[0:p, 0:p])
                    finish(ins)
            for t in range(NT):
                p = TILES[t]
                o = begin(("u", t))
                pe.wait_ge(*emptied(("hT", t, 1)))
                pe.wait_ge(*w_need["u"])
                finish(product(o[0:p, :], [(hT[:, k, P * t:P * t + p], wk("u", 512)[:, k]) for k in range(KD)]))
            for t in range(NT):
                p = TILES[t]
                for c in range(2):
                    o = begin(("kv", t, c))
                    pe.wait_ge(*w_need[f"kv{c}"])
                    finish(product(o[0:p, 0:396], [(hT[:, k, P * t:P * t + p], wk(f"kv{c}", 396)[:, k]) for k in range(KD)]))
            pe.wait_ge(par_ld, PARS)
            o = begin(("lam",))
            pe.transpose(o[:, 0:NS], lam_r[:, 0, :], ident[0:NS, 0:NS])
            finish(pe.transpose(o[:, NS:2 * NS], lam_r[:, 1, :], ident[0:NS, 0:NS]))
            for r in range(2):
                o = begin(("c", r))
                for b in range(4):
                    ins = pe.transpose(o[:, P * b:P * b + P], c_r[:, r, b].rearrange("p u n -> p (u n)"), ident[:])
                finish(ins)
            o = begin(("h0",))
            h0v = h0_r[:].rearrange("p (n r) -> p r n", r=2)
            for r in range(2):
                ins = pe.transpose(o[:, P * r:P * r + P], h0v[:, r], ident[:])
            finish(ins)
            pe.wait_ge(ucg_made, 1)
            for i in range(5):
                o = begin(("x", i))
                for j, g in enumerate(range(7 * i, min(7 * i + 7, NG))):
                    ins = pe.transpose(o[:, NCH * j:NCH * j + NCH], ucg[:, g], ident[0:NCH, 0:NCH])
                finish(ins)
            for i in range(8):
                o = begin(("vt", i))
                for j in range(4):
                    q = 4 * i + j
                    ins = pe.transpose(o[:, P * j:P * j + P], vn[:, q // 2, q % 2], ident[:])
                finish(ins)
            for i in range(8):
                o = begin(("k", i))
                for j in range(4):
                    s, lo = 4 * (i // 2) + j, 64 * (i % 2)
                    ins = product(o[0:GRP, P * j:P * j + P],
                                  [(bbar[lo:lo + 64, r, s], gm[lo:lo + 64, r, s, 0:CH]) for r in range(2)])
                finish(ins)
            pe.wait_ge(*emptied(("x", 4)))
            pe.wait_ge(*emptied(("vt", 7)))
            for i in range(6):
                o = begin(("d", i))
                for s in range(3 * i, min(3 * i + 3, NS)):
                    for r in range(2):
                        at = ((s - 3 * i) * 2 + r) * NCH
                        for g2 in range(2):
                            ins = pe.matmul(o[64 * g2:64 * g2 + 64, at:at + NCH], vt[:, 2 * s + r, 64 * g2:64 * g2 + 64],
                                            xg[:, 2 * s + g2], start=True, stop=True)
                finish(ins)
            pe.wait_ge(*w_need["q"])
            for m in range(GQA):
                wq = wk("q", 512)[:, :, P * m:P * m + P]
                for h in range(2):
                    o = begin(("q", m, h))
                    finish(product(o[:, 0:HALF], [(wq[:, k], hT[:, k, HALF * h:HALF * h + HALF]) for k in range(KD)]))
            pe.wait_ge(walked, 1)
            pe.wait_ge(w_toep, 16 * CH)
            for i in range(8):
                o = begin(("y", i))
                for j in range(4):
                    s, lo = 4 * (i // 2) + j, 64 * (i % 2)
                    g = 2 * s + i % 2
                    ins = product(o[0:NCH, P * j:P * j + P],
                                  [(xg[:, g], wt[:, g])]
                                  + [(hst[lo:lo + 64, r, s], gm[lo:lo + 64, r, s, 1:CH + 1]) for r in range(2)])
                finish(ins)
            o = begin(("fin",))
            for r in range(2):
                pe.transpose(o[:, P * r:P * r + P], fin[:, r, 1:1 + NSEQ], ident[:])
            for r in range(2):
                ins = pe.transpose(o[0:NS, 256 + P * r:256 + P * r + P], fin[:, r, 0], ident[:])
            finish(ins)
            pe.wait_ge(y_gelu, 8)
            for t in range(CH):
                o = begin(("zg", t))
                for b in range(4):
                    ins = pe.transpose(o[:, NCH * b:NCH * b + NCH], uc[:, t, P * b:P * b + P], ident[0:NCH, 0:NCH])
                finish(ins)
            pe.wait_ge(*emptied(("zg", CH - 1)))
            pe.wait_ge(*w_need["glu"])
            for m in range(4):
                for h in range(2):
                    o = begin(("glu", m, h))
                    finish(product(o[:, 0:HALF], [(wk("glu", 512, k=4)[:, k, P * m:P * m + P],
                                                   zgT[:, k, HALF * h:HALF * h + HALF]) for k in range(4)]))
            o = begin(("pe",))
            pe.wait_ge(pe_ld, 32)
            finish(pe.transpose(o[:, 0:2 * CL], pe_r[:].rearrange("p u n -> p (u n)"), ident[0:64, 0:64]))
            for i in range(10):
                o = begin(("ct", i))
                if i >= 2:
                    pe.wait_ge(raw_ld[(i - 2) % 4], 32 * ((i - 2) // 4 + 1))
                for u in range(2):
                    for k in range(2):
                        src = kv[:, 2 * i + u, P * k:P * k + P] if i < 2 else rawc[:, (i - 2) % 4, u, P * k:P * k + P]
                        ins = pe.transpose(o[:, (2 * u + k) * P:(2 * u + k + 1) * P], src, ident[:])
                finish(ins)
            pe.wait_ge(*emptied(("ct", 9)))
            pe.wait_ge(w1_ld, 16 * 6)
            for k in range(2):
                o = begin(("pre", k))
                finish(product(o[:, 0:NBLK], [(w1[:, k, i], kvct[:, k, i:i + CS * (NBLK - 1) + 1:CS]) for i in range(CL)]))
            o = begin(("kc",))
            pe.wait_ge(cmp_g, 1)
            finish(pe.matmul(o[:, 0:NBLK], w2[:, 0], cx[:, 0, 1], start=True, stop=True))
            o = begin(("vcp",))
            pe.wait_ge(cmp_g, 3)
            finish(pe.matmul(o[:, 0:P], cxr[:].rearrange("p g j -> p (g j)"), w2[:, 1],
                             start=True, stop=True))
            o = begin(("vcs",))
            for t in range(4):
                j = CJ_S + 2 * SJ * t
                if t < 3:
                    ins = pe.matmul(o[0:32, P * t:P * t + P], cx[:, 1, 1, j:j + 32], w2[:, 1], start=True, stop=True)
                else:
                    ins = pe.matmul(o[0:31, P * t:P * t + P], cx[:, 1, 1, j:j + 31], w2[:, 1], start=True, stop=True)
            finish(ins)
            for r in range(2):
                o = begin(("ktp", r))
                for t in range(4):
                    ins = pe.transpose(o[:, P * t:P * t + P], kv[:, t, KVW * (r + 1):KVW * (r + 1) + P], ident[:])
                finish(ins)
            o = begin(("ktn",))
            for r in range(2):
                ins = pe.transpose(o[:, 64 * r:64 * r + 64], kv[0:64, 4, KVW * (r + 1):KVW * (r + 1) + P], ident[0:64, 0:64])
            finish(ins)
            pe.wait_ge(cache_ld, 16 * 17)
            for r in range(2):
                for i in range(4):
                    o = begin(("kts", r, i))
                    for j in range(4):
                        ins = pe.transpose(o[:, P * j:P * j + P], caches[:, r, 2 * i + j // 2, j % 2, 0:P], ident[:])
                    finish(ins)

            pe.wait_ge(*emptied(("kts", 1, 3)))
            pe.wait_ge(consts, 2)
            pe.wait_ge(row_masks, 1)
            pe.wait_ge(qpad_made, 4)
            pe.wait_ge(*emptied(("vcs",)))
            for what, i in attention_steps():
                kind, b, r, h = ITEMS[i] if what in ("score", "turn", "value") else ITEMS[GROUPS[i][0]]
                kh, m = h // GQA, h % GQA
                lo = HD * kh
                if what == "score":
                    o = begin(("s", i))
                    if kind == "p":
                        n = P * (b + 1)
                        pe.matmul(o[:, 0:n], qT[lo:lo + HD, m, P * b:P * b + P], kt[lo:lo + HD, r - 1, 0:n], start=True, stop=False)
                        finish(pe.matmul(o[:, n - P:n], ident_b[:], causal[:], start=False, stop=True))
                    elif kind == "c":
                        for hh in range(NH):
                            if hh == GQA:
                                ins.then_inc(half_done, 1)
                                pe.wait_ge(half_done, b + 1)
                            l = HD * (hh // GQA)
                            ins = pe.matmul(o[:, 32 * hh:32 * hh + 32], qT[l:l + HD, hh % GQA, P * b:P * b + P],
                                            kc[l:l + HD, CJ_P:CJ_P + 32], start=True, stop=True)
                        finish(ins)
                    elif kind == "s":
                        product(o[:, 0:PAST], [(qpad[:, 2 * b + u], kts[:, r - 1, 2 * b + u]) for u in range(2)])
                        for u in range(2):
                            pe.matmul(o[:, PAST:PAST + 64], qpad[:, 2 * b + u], kt[:, r - 1, NP_:ROWS], start=(u == 0), stop=False)
                        finish(pe.matmul(o[:, PAST:PAST + 64], ident_b[:], new_mask[:, b], start=False, stop=True))
                    else:
                        j = CJ_S + 2 * SJ * b
                        n = min(32, NBLK - j)
                        finish(product(o[:, 0:n], [(qpad[:, 2 * b + u], kc[:, j:j + n]) for u in range(2)]))
                elif what == "turn":
                    o = begin(("t", i))
                    pe.wait_ge(*emptied(("s", i)))
                    if kind == "c":
                        pe.wait_ge(s_prob, b + 1)
                    at = 0
                    for c, n in enumerate(item_keys(ITEMS[i])):
                        ins = pe.transpose(o[0:n, P * c:P * c + P], pb[:, i % 3, at:at + n], ident[:])
                        at += n
                    finish(ins)
                elif what == "value":
                    g = GROUP_OF[i]
                    pe.wait_ge(*emptied(("t", i)))
                    if g >= 2 and i == GROUPS[g][0]:
                        pe.wait_ge(s_gath, g - 1)
                    o = ps[:, RING + g % 2, :]
                    vcol = KVW * r + P
                    q = pt[:, i % 2]
                    if kind == "p":
                        ins = product(o[:, HD * h:HD * h + HD],
                                      [(q[:, P * c:P * c + P], kv[:, c, vcol + lo:vcol + lo + HD]) for c in range(b + 1)])
                    elif kind == "c":
                        for k in range(NKV):
                            ins = pe.matmul(o[:, 256 * k:256 * k + 256], q[:, P * k:P * k + P], vcbd[:, k], start=True, stop=True)
                    elif kind == "s":
                        ins = product(o[:, 0:256].rearrange("p (a n) -> p a n", a=2),
                                      [(q[:, P * c:P * c + P], caches[:, r - 1, 2 * b:2 * b + 2, c, P:KVW]) for c in range(2)]
                                      + [(q[0:64, 256:384], kv[0:64, 4, vcol:vcol + P].unsqueeze(1).broadcast_to([64, 2, P]))])
                    else:
                        ins = pe.matmul(o[:, 0:256].rearrange("p (a n) -> p a n", a=2), q[0:32, 0:P],
                                        vcs[0:32, b].unsqueeze(1).broadcast_to([32, 2, P]), start=True, stop=True)
                    ins.then_inc(s_val, 1)
                elif what == "out":
                    o = begin(("o", i))
                    if b < 4 and kind == "p":
                        pe.wait_ge(s_gath, i + 1)
                        pe.wait_ge(osd_made, b + 1)
                        for k in range(4):
                            ins = pe.transpose(o[:, P * k:P * k + P], ob[:, b % 2, P * k:P * k + P], ident[:])
                    else:
                        pe.wait_ge(osd_made, 4 + b + 1)
                        ins = pe.transpose(o[:, 0:P], osd[:, b % 2], ident[:])
                    finish(ins)

            pe.wait_ge(*emptied(("o", len(GROUPS) - 1)))
            pe.wait_ge(glu_made, 8)
            for m in range(KD):
                pe.wait_ge(*w_need[f"m{m}"])
                for h in range(2):
                    cut = slice(HALF * h, HALF * h + HALF)
                    for key, at, k, src in (("ga", 0, KD, hT), ("ab", 2048, 4, gluT), ("gb", 1024, KD, hT), ("bb", 2560, 4, onsaT)):
                        o = begin((key, m, h))
                        finish(product(o[:, 0:HALF], [(wk(f"m{m}", P, at, k)[:, j], src[:, j, cut]) for j in range(k)]))
            pe.wait_ge(merged_made, 2 * KD)
            for t in range(NT):
                p = TILES[t]
                for c in range(2):
                    o = begin(("wo", t, c))
                    pe.wait_ge(*w_need[f"wo{c}"])
                    finish(product(o[0:p, :], [(merged[:, k, P * t:P * t + p], wk(f"wo{c}", 512)[:, k]) for k in range(KD)]))
            pe.wait_ge(rt_ld, 64)
            for t in range(NT):
                p = TILES[t]
                pe.wait_ge(hn_made, NT + t + 1)
                for k in range(2):
                    o = begin(("h2T", t, k))
                    for j in range(4):
                        ins = pe.transpose(o[:, j * P:j * P + p], hn[0:p, t % 2, (4 * k + j) * P:(4 * k + j + 1) * P], ident[0:p, 0:p])
                    finish(ins)
                o = begin(("rt", t))
                pe.wait_ge(*emptied(("h2T", t, 1)))
                finish(product(o[0:p, 0:20], [(hT[:, k, P * t:P * t + p], w_rt[:, k]) for k in range(KD)]))
            pe.wait_ge(p_ld, 32)
            for t in range(NT):
                p = TILES[t]
                o = begin(("pT", t))
                for j in range(2):
                    ins = pe.transpose(o[:, P * j:P * j + p], p_in[0:p, t, P * j:P * j + P], ident[0:p, 0:p])
                finish(ins)

            pe.wait_ge(*emptied(("pT", NT - 1)))
            pe.wait_ge(*emptied(("rt", NT - 1)))

            def gate_up(n, u, loads):
                pe.wait_ge(e_ld[u], loads)
                for q in range(4):
                    f, h = q // 2, q % 2
                    pe.wait_ge(act_made, n * 4 + (q + 1))
                    for w in range(2):
                        ins = product(ps[:, 2 * (q % 2) + w, 0:HALF],
                                      [(wgu[:, u, w, k, P * f:P * f + P], hT[:, k, HALF * h:HALF * h + HALF]) for k in range(KD)])
                    ins.then_inc(up_done, 1)

            def down(n, u):
                pe.wait_ge(act_made, n * 4 + 6)
                for t in range(NT):
                    p = TILES[t]
                    for c in range(2):
                        j = 2 * t + c
                        pe.wait_ge(dn_free, n * 10 + (j + 1))
                        ins = product(ps[0:p, 4 + (2 * u + j) % 4, :],
                                      [(actT[:, u, f, P * t:P * t + p], wdn[:, u, f, 512 * c:512 * c + 512]) for f in range(2)])
                        ins.then_inc(dn_done, 1)

            gate_up(0, 0, 48)
            with pe.Fori(0, NE // 2 - 1) as i:
                gate_up(i * 2 + 1, 1, i * 48 + 48)
                down(i * 2, 0)
                gate_up(i * 2 + 2, 0, i * 48 + 96)
                down(i * 2 + 1, 1)
            gate_up(NE - 1, 1, 48 * (NE // 2))
            down(NE - 2, 0)
            down(NE - 1, 1)

            pe.wait_ge(act_made, 4 * NE + 2)
            for t in range(NT):
                p = TILES[t]
                if t == 0:
                    pe.wait_ge(dn_free, 10 * NE + 4)
                for k in range(2):
                    o = begin(("x2T", t, k))
                    for j in range(4):
                        ins = pe.transpose(o[:, j * P:j * P + p], x[0:p, t, (4 * k + j) * P:(4 * k + j + 1) * P], ident[0:p, 0:p])
                    finish(ins)
                for c in range(2):
                    o = begin(("pg", t, c))
                    pe.wait_ge(*w_need[f"pg{c}"])
                    pe.wait_ge(*emptied(("x2T", t, 0)))
                    pe.wait_ge(*emptied(("x2T", t, 1)))
                    finish(product(o[0:p, :], [(hT[:, k, P * t:P * t + p], wk(f"pg{c}", 512)[:, k]) for k in range(KD)]))
                    o = begin(("pp", t, c))
                    pe.wait_ge(*w_need["ple"])
                    finish(product(o[0:p, :], [(pT[:, k, P * t:P * t + p], wk("ple", D, 0, 2)[:, k, 512 * c:512 * c + 512]) for k in range(2)]))

        def turn(eng, i, copy, take, empty):
            kind, b = ITEMS[i][0], ITEMS[i][1]
            o = take(("t", i))
            if i >= 2:
                eng.wait_ge(s_val, i - 1)
            q = pt[:, i % 2]
            if kind == "s":
                copy(q[:, 0:256], o[:, 0:256])
                empty(copy(q[0:64, 256:384], o[0:64, 256:384]))
            elif kind == "sc":
                empty(copy(q[0:32, 0:P], o[0:32, 0:P]))
            else:
                n = P * len(item_keys(ITEMS[i]))
                empty(copy(q[:, 0:n], o[:, 0:n]))

        def turned_norm(dve, t, key, which, take, empty):
            p = TILES[t]
            for k in range(2):
                o = take(key + (k,))
                empty(dve.tensor_tensor(hT[:, 4 * k:4 * k + 4, P * t:P * t + p], o.rearrange("p (k n) -> p k n", k=4)[:, :, 0:p],
                                        g_cols[:, which, 4 * k:4 * k + 4].unsqueeze(2).broadcast_to([P, 4, p]), ALU.mult))

        def router_logits(dve, t, take, empty):
            p = TILES[t]
            o = take(("rt", t))
            empty(dve.tensor_tensor(lg[0:p, t], o[0:p, 0:20], b_rt[0:p], ALU.add))

        @block.scalar
        def _(act):
            def col(ap, n):
                return ap.rearrange("(k p) -> p k", p=P)

            act.dma_start(ldt[0:64, :], I["ssm_log_dt"].rearrange("o (s g) -> o g s", g=2)[:, 0].broadcast_to([64, NS]),
                          allow_slow_non_contiguous=True).then_inc(par_ld, 16)
            act.dma_start(ldt[64:P, :], I["ssm_log_dt"].rearrange("o (s g) -> o g s", g=2)[:, 1].broadcast_to([64, NS]),
                          allow_slow_non_contiguous=True).then_inc(par_ld, 16)
            for r, name in enumerate(("ssm_lam_re", "ssm_lam_im")):
                act.dma_start(lam_r[:, r, :], I[name][0].rearrange("(s g) n -> s (g n)", g=2)).then_inc(par_ld, 16)
            for r, name in enumerate(("ssm_b_re", "ssm_b_im")):
                act.dma_start(b_r[:, r], I[name][0].rearrange("(s g) n c -> (g n) s c", g=2)).then_inc(par_ld, 16)
            for r, name in enumerate(("ssm_c_re", "ssm_c_im")):
                for u in range(2):
                    act.dma_start(c_r[:, r, :, u], I[name][0].rearrange("(b g) c n -> (g c) b n", b=4)).then_inc(par_ld, 16)
            act.dma_start(h0_r[:], I["state_ssm"][0].rearrange("q (s g) n r -> (q s) (g n r)", g=2)).then_inc(par_ld, 16)
            act.dma_start(d_b[:], I["ssm_d"].broadcast_to([NCH, SSM_W])).then_inc(par_ld, 16)
            act.dma_start(b_glu[:], col(I["b_glu"][0], 4), allow_slow_non_contiguous=True).then_inc(par_ld, 16)
            act.dma_start(g_cols[:, 0], col(I["norm1_g"][0], KD), allow_slow_non_contiguous=True).then_inc(gains_ld, 16)
            act.dma_start(g_cols[:, 1], col(I["norm2_g"][0], KD), allow_slow_non_contiguous=True).then_inc(gains_ld, 16)
            act.dma_start(ptab[:], I["page_table"].rearrange("(o s) u -> o (s u)", o=1)).then_inc(pt_ld, 16)

            def take(key):
                act.wait_ge(pe_done, PLAN.done(key))
                return bank(key)

            def empty(ins):
                ins.then_inc(drained["act"], 1)

            def copy(key, dst, src):
                empty(act.activation(dst, src, ACT.Copy))

            junk = flat(gluT)
            for t in range(NT):
                act.wait_ge(x_ld[t], 16)
                p = TILES[t]
                act.activation(junk[0:p, 0:D], x_in[0:p, t], ACT.Square, accum_out=stat[0:p, 0, t:t + 1]).then_inc(sq_done, 1)
                act.wait_ge(sq_done, t + 1)
            for t in range(NT):
                o = take(("u", t))
                p = TILES[t]
                copy(None, u_rows[0:p, t], o[0:p, :])
            for t in range(NT):
                p = TILES[t]
                for c in range(2):
                    o = take(("kv", t, c))
                    copy(None, kv[0:p, t, 396 * c:396 * c + 396], o[0:p, 0:396])
            act.wait_ge(par_ld, PARS)
            act.activation(sm[:, 2], ldt[:], ACT.Exp).then_inc(dt_done, 1)
            act.wait_ge(drained["act"], PLAN.by[("kv", NT - 1, 1)][1])
            for t in range(NT):
                p = TILES[t]
                act.activation(tgate[0:p, t], kv[0:p, t, 3 * KVW:], ACT.Tanh, scale=0.5).then_inc(gates_made, 1)
            act.wait_ge(angles, 1)
            act.activation(sm[:, 8], sm[:, 3], ACT.Exp)
            act.activation(sm[:, 9], sm[:, 6], ACT.Sin)
            act.activation(sm[:, 10], sm[:, 7], ACT.Sin).then_inc(trig, 1)
            for i in range(8):
                o = take(("vt", i))
                copy(None, vt[:, 4 * i:4 * i + 4].rearrange("p a b -> p (a b)"), o)
            for i in range(8):
                o = take(("k", i))
                if i >= 2:
                    act.wait_ge(k_out[i % 2], 16 * (i // 2))
                copy(None, ks[:, i % 2].rearrange("p g n -> p (g n)"), o[0:GRP, :])
            act.wait_ge(*emptied(("h0",)))
            for i in range(6):
                o = take(("d", i))
                s0, s1 = 3 * i, min(3 * i + 3, NS)
                n = s1 - s0
                v = o[:, 0:n * 2 * NCH].rearrange("p (s r c) -> p r s c", s=n, r=2)
                for r in range(2):
                    act.activation(hst[:, r, s0:s1, 1:NPC], v[:, r, :, 0:NPC - 1], ACT.Copy)
                    ins = act.activation(fin[:, r, :, s0:s1].rearrange("p c s -> p s c"), v[:, r, :, NPC - 1:NCH], ACT.Copy)
                empty(ins)
            for m in range(GQA):
                for h in range(2):
                    o = take(("q", m, h))
                    empty(act.activation(qT[:, m, HALF * h:HALF * h + HALF], o[:, 0:HALF], ACT.Copy, scale=SCALE))
            for i in range(8):
                act.wait_ge(*emptied(("y", i)))
                v = uc.rearrange("p t (b j g c) -> p t b g j c", b=4, j=4, g=2)[:, :, i // 2, i % 2]
                act.activation(v, v, GELU).then_inc(y_gelu, 1)
            o = take(("fin",))
            act.activation(fo.rearrange("p n r -> p r n"), o[:, 0:2 * P].rearrange("p (r n) -> p r n", r=2), ACT.Copy)
            copy(None, fo_p[:].rearrange("p n r -> p r n"), o[0:NS, 2 * P:4 * P].rearrange("p (r n) -> p r n", r=2))
            act.wait_ge(bglu_half, 1)
            for m in range(4):
                for h in range(2):
                    o = take(("glu", m, h))
                    empty(act.activation(gluT[:, m, HALF * h:HALF * h + HALF], o[:, 0:HALF], ACT.Tanh,
                                         bias=stat[:, 3, m:m + 1], scale=0.5))
            act.wait_ge(glu_made, 8)
            act.wait_ge(fin_out, 32)
            o = take(("pe",))
            copy(None, kvct[:, :, 0:CL], o[:, 0:2 * CL].rearrange("p (k i) -> p k i", k=2))
            for i in range(10):
                o = take(("ct", i))
                at = CT0 + 2 * P * i
                copy(None, kvct[:, :, at:at + 2 * P].rearrange("p k (u n) -> p u k n", u=2), o.rearrange("p (u k n) -> p u k n", u=2, k=2))
            for k in range(2):
                act.wait_ge(*emptied(("pre", k)))
                act.activation(cx[:, k, 1], cx[:, k, 0], GELU).then_inc(cmp_g, 1)
            act.activation(cxr[:], cx[:, 1, 0, CJ_P:CJ_P + 32].unsqueeze(1).broadcast_to([P, 4, 32]), GELU).then_inc(cmp_g, 1)
            for r in range(2):
                o = take(("ktp", r))
                copy(None, kt[:, r, 0:NP_], o)
            o = take(("ktn",))
            copy(None, kt[:, :, NP_:ROWS], o[:, 0:P].rearrange("p (r n) -> p r n", r=2))
            for r in range(2):
                for i in range(4):
                    o = take(("kts", r, i))
                    copy(None, kts[:, r, 2 * i:2 * i + 2].rearrange("p s n -> p (s n)"), o)
            for what, i in attention_steps():
                if what == "score":
                    kind = ITEMS[i][0]
                    o = take(("s", i))
                    n = sum(item_keys(ITEMS[i]))
                    if i >= 3:
                        act.wait_ge(pe_done, PLAN.done(("t", i - 3)))
                    act.wait_ge(s_max, i + 1)
                    if kind == "c":
                        empty(act.activation(pb[:, i % 3, 0:n], sct[:, 0:n], ACT.Exp))
                    elif kind == "sc":
                        empty(act.activation(pb[:, i % 3, 0:n], sct[:, 0:n], ACT.Exp, bias=nm[:, i:i + 1], accum_out=rs[:, i:i + 1]))
                    else:
                        empty(act.activation(pb[:, i % 3, 0:n], o[:, 0:n], ACT.Exp, bias=nm[:, i:i + 1], accum_out=rs[:, i:i + 1]))
                elif what == "turn" and i % 2 == 0:
                    turn(act, i, lambda d, s: act.activation(d, s, ACT.Copy), take, empty)
            for m in range(KD):
                for h in range(2):
                    for w, key in enumerate(("ga", "gb")):
                        o = take((key, m, h))
                        n = 2 * (2 * m + h) + w
                        if n < 4:
                            act.wait_ge(*emptied(("o", len(GROUPS) - 1)))
                        else:
                            before = 2 * m + h - 2
                            act.wait_ge(*emptied(("bb" if w else "ab", before // 2, before % 2)))
                        empty(act.activation(tg[:, n % 4], o[:, 0:HALF], ACT.Tanh, scale=0.5))
            for t in range(NT):
                p = TILES[t]
                act.wait_ge(*emptied(("wo", t, 1)))
                if t == 0:
                    act.wait_ge(pe_done, PLAN.done(("bb", KD - 1, 1)))
                act.activation(junk[0:p, 0:D], x[0:p, t], ACT.Square, accum_out=stat[0:p, 0, t:t + 1]).then_inc(sq_done, 1)
                act.wait_ge(sq_done, NT + t + 1)
            act.wait_ge(lg_made, 1)
            act.activation(r16[:, :, 0:5], r16[:, :, 0:5], ACT.Exp).then_inc(lg_exp, 1)
            for t in range(NT):
                p = TILES[t]
                o = take(("pT", t))
                copy(None, pT[:, :, P * t:P * t + p], o[:, 0:2 * P].rearrange("p (k n) -> p k n", k=2)[:, :, 0:p])

            def gates(n):
                for q in range(4):
                    act.wait_ge(up_done, n * 4 + (q + 1))
                    act.activation(th[:, q % 2], ps[:, 2 * (q % 2), 0:HALF], ACT.Tanh, scale=0.5).then_inc(th_made, 1)
            with act.Fori(0, NE) as n:
                gates(n)
            for t in range(NT):
                p = TILES[t]
                o = take(("x2T", t, 0))
                copy(None, hT[:, 0:4, P * t:P * t + p], o.rearrange("p (k n) -> p k n", k=4)[:, :, 0:p])
                for c in range(2):
                    o = take(("pg", t, c))
                    if 2 * t + c >= 2:
                        act.wait_ge(x3_made, 2 * t + c - 1)
                    empty(act.activation(tpg[0:p, c], o[0:p, :], ACT.Tanh, scale=0.5))
            for t in range(NT):
                p = TILES[t]
                act.wait_ge(x3_made, 2 * t + 2)
                act.activation(junk[0:p, 0:D], x[0:p, t], ACT.Square, accum_out=stat[0:p, 0, t:t + 1]).then_inc(sq_done, 1)
                act.wait_ge(sq_done, 2 * NT + t + 1)

        @block.vector
        def _(dve):
            count = [0]

            def link(ins):
                count[0] += 1
                ins.then_inc(dve_step, 1)
                dve.wait_ge(dve_step, count[0])

            def tt(out, a, b, op):
                return dve.tensor_tensor(out, a, b, op)

            def take(key):
                dve.wait_ge(pe_done, PLAN.done(key))
                return bank(key)

            def empty(ins):
                ins.then_inc(drained["dve"], 1)

            dve.wait_ge(gains_ld, 32)
            for t in range(NT):
                p = TILES[t]
                dve.wait_ge(rstd_done, t + 1)
                dve.tensor_scalar(x_in[0:p, t], x_in[0:p, t], stat[0:p, 2, t:t + 1], None, ALU.mult).then_inc(hn_made, 1)
            for t in range(NT):
                turned_norm(dve, t, ("hT", t), 0, take, empty)
            dve.wait_ge(pe_done, PLAN.done(("hT", NT - 1, 1)))
            link(dve.memset(stat[:, 3, 0:4], 0.0))
            dve.wait_ge(par_ld, PARS)
            dve.tensor_scalar(stat[:, 3, 0:4], b_glu[:], 0.5, None, ALU.mult).then_inc(bglu_half, 1)
            o = take(("lam",))
            empty(dve.tensor_copy(sm[:, 0:2], o[:, 0:2 * NS].rearrange("p (r s) -> p r s", r=2)))
            lr, li, dt, er, an, kk, ra, rb, mg, sn, cs, den, t0, t1, cr, ci, a1 = (sm[:, j] for j in range(17))
            dve.wait_ge(*emptied(("lam",)))
            dve.wait_ge(dt_done, 1)
            two_pi = 2.0 * math.pi
            hi = 6.28125
            magic = 1.5 * 2.0 ** 23
            tt(er, lr, dt, ALU.mult)
            link(tt(an, li, dt, ALU.mult))
            link(dve.tensor_scalar(kk, an, 1.0 / two_pi, magic, ALU.mult, ALU.add))
            link(dve.tensor_scalar(kk, kk, -magic, None, ALU.add))
            link(dve.scalar_tensor_tensor(ra, kk, -hi, an, ALU.mult, ALU.add))
            link(dve.scalar_tensor_tensor(ra, kk, -(two_pi - hi), ra, ALU.mult, ALU.add))
            link(dve.tensor_scalar(t0, ra, math.pi / 2, -two_pi, ALU.is_gt, ALU.mult))
            link(dve.scalar_tensor_tensor(rb, ra, math.pi / 2, t0, ALU.add, ALU.add))
            link(dve.tensor_scalar(ra, ra, 3.1415925, -3.1415925, ALU.min, ALU.max))
            dve.tensor_scalar(rb, rb, 3.1415925, -3.1415925, ALU.min, ALU.max).then_inc(angles, 1)
            for r in range(2):
                o = take(("c", r))
                v = o.rearrange("p (s g c) -> p s g c", g=2, c=GRP)
                dve.tensor_copy(cst[0:64, r], v[0:64, :, 0])
                empty(dve.tensor_copy(cst[64:P, r], v[64:P, :, 1]))
            o = take(("h0",))
            dve.memset(hst[:, :, :, 0:1], 0.0)
            empty(dve.tensor_copy(hst[:, :, :, NPC:NCH].rearrange("p r s q -> p r q s"),
                                  o[:, 0:2 * P].rearrange("p (r q s) -> p r q s", r=2, q=NSEQ)))
            dve.wait_ge(trig, 1)
            dve.memset(pw[:, 0, 0], 1.0)
            dve.memset(pw[:, 0, 1], 0.0)
            tt(pw[:, 1, 0], mg, cs, ALU.mult)
            link(tt(pw[:, 1, 1], mg, sn, ALU.mult))
            for m in (1, 2, 4):
                a_r, a_i = pw[:, 1:m + 1, 0], pw[:, 1:m + 1, 1]
                b_re = pw[:, m:m + 1, 0].broadcast_to([P, m, NS])
                b_im = pw[:, m:m + 1, 1].broadcast_to([P, m, NS])
                u0 = tmp_v[:, 0:m * NS].rearrange("p (m s) -> p m s", m=m)
                u1 = tmp_v[:, 64:64 + m * NS].rearrange("p (m s) -> p m s", m=m)
                tt(u0, a_i, b_im, ALU.mult)
                tt(u1, a_i, b_re, ALU.mult)
                tt(pw[:, m + 1:2 * m + 1, 0], a_r, b_re, ALU.mult)
                link(tt(pw[:, m + 1:2 * m + 1, 1], a_r, b_im, ALU.mult))
                tt(pw[:, m + 1:2 * m + 1, 0], pw[:, m + 1:2 * m + 1, 0], u0, ALU.subtract)
                link(tt(pw[:, m + 1:2 * m + 1, 1], pw[:, m + 1:2 * m + 1, 1], u1, ALU.add))
            dve.tensor_copy(pwr[:, 0], pw[:, CH - 1]).then_inc(powers, 1)
            for j in range(1, CH):
                dve.tensor_copy(pwr[:, j], pw[:, CH - 1 - j])
            link(dve.tensor_scalar(a1, pw[:, 1, 0], -1.0, None, ALU.add))
            tt(t0, lr, lr, ALU.mult)
            link(tt(t1, li, li, ALU.mult))
            link(tt(den, t0, t1, ALU.add))
            link(dve.reciprocal(den, den))
            tt(t0, a1, lr, ALU.mult)
            link(tt(t1, pw[:, 1, 1], li, ALU.mult))
            link(tt(t0, t0, t1, ALU.add))
            link(tt(cr, t0, den, ALU.mult))
            tt(t0, pw[:, 1, 1], lr, ALU.mult)
            link(tt(t1, a1, li, ALU.mult))
            link(tt(t0, t0, t1, ALU.subtract))
            link(tt(ci, t0, den, ALU.mult))
            sc = [P, NS, GRP]
            crb, cib = cr.unsqueeze(2).broadcast_to(sc), ci.unsqueeze(2).broadcast_to(sc)
            u0 = tmp_v[:, 0:NS * GRP].rearrange("p (s c) -> p s c", s=NS)
            tt(bbar[:, 0], b_r[:, 0], crb, ALU.mult)
            link(tt(u0, b_r[:, 1], cib, ALU.mult))
            tt(bbar[:, 0], bbar[:, 0], u0, ALU.subtract)
            link(tt(bbar[:, 1], b_r[:, 1], crb, ALU.mult))
            link(tt(u0, b_r[:, 0], cib, ALU.mult))
            link(tt(bbar[:, 1], bbar[:, 1], u0, ALU.add))
            n8 = [P, NS, CH, GRP]
            u8 = tmp_v[:, 0:NS * CH * GRP].rearrange("p (s t c) -> p s t c", s=NS, t=CH)
            qr, qi = (pwr[:, :, r].rearrange("p t s -> p s t").unsqueeze(3).broadcast_to(n8) for r in range(2))
            br8, bi8 = (bbar[:, r].unsqueeze(2).broadcast_to(n8) for r in range(2))
            v8 = [vn[:, :, r].rearrange("p s (t c) -> p s t c", t=CH) for r in range(2)]
            tt(v8[0], qr, br8, ALU.mult)
            link(tt(u8, qi, bi8, ALU.mult))
            link(tt(v8[0], v8[0], u8, ALU.subtract))
            tt(v8[1], qr, bi8, ALU.mult)
            link(tt(u8, qi, br8, ALU.mult))
            tt(v8[1], v8[1], u8, ALU.add).then_inc(v_made, 1)
            dve.wait_ge(gates_made, NT)
            dve.tensor_scalar(tgate[:, 0:4], tgate[:, 0:4], 1.0, None, ALU.add).then_inc(gates_made, 1)
            dve.tensor_scalar(tgate[0:64, 4], tgate[0:64, 4], 1.0, None, ALU.add).then_inc(gates_made, 1)
            dve.wait_ge(uc_ld, 16)
            dve.tensor_copy(ucg.rearrange("p g (t c) -> p g t c", t=CH), uc.rearrange("p t (g c) -> p g t c", g=NG)
                            ).then_inc(ucg_made, 1)
            for i in range(5):
                o = take(("x", i))
                n = min(7, NG - 7 * i)
                empty(dve.tensor_copy(xg[:, 7 * i:7 * i + n].rearrange("p g n -> p (g n)"), o[:, 0:n * NCH]))
            dve.wait_ge(ud_made, 1)
            for i in range(8):
                o = take(("y", i))
                v = uc.rearrange("p t (b j g c) -> p t b g j c", b=4, j=4, g=2)[:, :, i // 2, i % 2]
                empty(tt(v, o[0:NCH, :].rearrange("p (g t c) -> p t g c", g=4, t=CH), v, ALU.add))
            for t in range(CH):
                o = take(("zg", t))
                empty(dve.tensor_copy(zgT.rearrange("p k (c t) -> p k c t", t=CH)[:, :, :, t],
                                      o[:, 0:4 * NCH].rearrange("p (k c) -> p k c", k=4)))
            dve.wait_ge(*emptied(("zg", CH - 1)))
            for m in range(4):
                for h in range(2):
                    cut = slice(HALF * h, HALF * h + HALF)
                    dve.wait_ge(*emptied(("glu", m, h)))
                    dve.scalar_tensor_tensor(gluT[:, m, cut], gluT[:, m, cut], 1.0, zgT[:, m, cut], ALU.add, ALU.mult
                                             ).then_inc(glu_made, 1)
            dve.wait_ge(glu_made, 8)
            dve.wait_ge(fin_out, 32)
            dve.wait_ge(masks, 1)
            link(dve.tensor_scalar(rowi[:, 1:2], rowi[:, 0:1], 7, None, ALU.bitwise_and))
            link(dve.tensor_scalar(rowi[:, 2:3], rowi[:, 0:1], 6, None, ALU.logical_shift_right))
            dve.tensor_copy(rowf[:, 0:1], rowi[:, 1:2])
            link(dve.tensor_copy(rowf[:, 1:2], rowi[:, 2:3]))
            dve.tensor_scalar(rowf[:, 2:3], rowf[:, 1:2], 8.0, None, ALU.mult)
            link(dve.tensor_scalar(rowf[:, 3:4], rowf[:, 1:2], 16.0, None, ALU.mult))
            link(dve.scalar_tensor_tensor(rowf[:, 0:1], rowf[:, 1:2], 8.0, rowf[:, 0:1], ALU.mult, ALU.add))
            dve.tensor_scalar(nmk[:, 1], nmk[:, 0], rowf[:, 2:3], NEG, ALU.is_lt, ALU.mult)
            link(dve.tensor_scalar(nmk[:, 2], nmk[:, 0], rowf[:, 0:1], NEG, ALU.is_gt, ALU.mult))
            tt(new_mask[:], nmk[:, 1], nmk[:, 2], ALU.add).then_inc(row_masks, 1)
            dve.tensor_scalar(csneg[:, 1], csneg[:, 0], rowf[:, 3:4], NEG, ALU.is_lt, ALU.mult)
            link(dve.tensor_scalar(csneg[:, 0], csneg[:, 0], rowf[:, 3:4], None, ALU.subtract))
            link(dve.tensor_scalar(csneg[:, 2], csneg[:, 0], float(SJ - 2), NEG, ALU.is_gt, ALU.mult))
            link(tt(csneg[:, 1], csneg[:, 1], csneg[:, 2], ALU.add))
            for k in range(2):
                o = take(("pre", k))
                link(dve.tensor_copy(cc[:, k:k + 1], o[:, 0:1]))
                empty(dve.tensor_scalar(cx[:, k, 0], o[:, 0:NBLK], cc[:, k:k + 1], None, ALU.add))
            o = take(("kc",))
            empty(dve.tensor_copy(kc[:], o[:, 0:NBLK]))
            o = take(("vcp",))
            dve.wait_ge(masks, 2)
            for g in range(4):
                ins = dve.tensor_copy(vcbd[32 * g:32 * g + 32, :, g], o[32 * g:32 * g + 32, 0:P].rearrange("p (k n) -> p k n", k=NKV))
            empty(ins)
            o = take(("vcs",))
            link(dve.memset(vcs[:], 0.0))
            dve.tensor_copy(vcs[:, 0:3], o[0:32, 0:3 * P].rearrange("p (t n) -> p t n", t=3))
            empty(dve.tensor_copy(vcs[0:31, 3], o[0:31, 3 * P:4 * P]))
            dve.wait_ge(gs_ld, 16 * 16)
            dve.wait_ge(gates_made, NT + 2)
            for what, i in attention_steps():
                if what == "score":
                    kind, b, r, h = ITEMS[i]
                    o = take(("s", i))
                    n = sum(item_keys(ITEMS[i]))
                    if kind in "ps":
                        dve.tensor_reduce(nm[:, i:i + 1], o[:, 0:n], axis=X, op=ALU.max, negate=True).then_inc(s_max, 1)
                    elif kind == "c":
                        v = o[:, 0:256].rearrange("p (h j) -> p h j", h=NH)
                        sv = sct[:].rearrange("p (h j) -> p h j", h=NH)
                        pv = pb[:, i % 3, 0:256].rearrange("p (h j) -> p h j", h=NH)
                        link(tt(sv, v, cmneg[:, b:b + 1].broadcast_to([P, NH, 32]), ALU.add))
                        link(dve.tensor_reduce(mx8[:], sv, axis=X, op=ALU.max))
                        tt(sv, sv, mx8[:].unsqueeze(2).broadcast_to([P, NH, 32]), ALU.subtract).then_inc(s_max, 1)
                        dve.wait_ge(*emptied(("s", i)))
                        link(dve.tensor_reduce(rs8[:], pv, axis=X, op=ALU.add))
                        tt(pv, pv, cm01[:, b:b + 1].broadcast_to([P, NH, 32]), ALU.mult).then_inc(s_prob, 1)
                    else:
                        m = min(32, NBLK - (CJ_S + 2 * SJ * b))
                        if b:
                            dve.wait_ge(*emptied(("s", i - 3)))
                        if m < 32:
                            link(dve.memset(sct[:, 0:32], NEG))
                        link(tt(sct[:, 0:m], o[:, 0:m], csneg[:, 1, 0:m], ALU.add))
                        dve.tensor_reduce(nm[:, i:i + 1], sct[:, 0:32], axis=X, op=ALU.max, negate=True).then_inc(s_max, 1)
                elif what == "turn" and i % 2:
                    turn(dve, i, lambda d, s: dve.tensor_copy(d, s), take, empty)
                elif what == "gather":
                    g = i
                    last = GROUPS[g][-1]
                    kind, b, r, h = ITEMS[last]
                    o = ps[:, RING + g % 2, :]
                    dve.wait_ge(s_val, last + 1)
                    w = w8[:, g % 2]
                    if kind in "cp":
                        src = rs8[:] if kind == "c" else rs[:, GROUPS[g][0]:last + 1]
                        link(dve.reciprocal(w, src))
                        link(tt(w, w, tgate[:, b, r:3 * NH:3], ALU.mult))
                        wb = w.unsqueeze(2).broadcast_to([P, NH, HD])
                        ov = o.rearrange("p (h n) -> p h n", h=NH)
                        dst = ob[:, b % 2] if r == 0 else tmp_o[:]
                        if r == 0 and b >= 2:
                            dve.wait_ge(*emptied(("o", GROUP_OF[ITEMS.index(("p", b - 2, 2, NH - 1))])))
                        ins = tt(dst.rearrange("p (h n) -> p h n", h=NH), ov, wb, ALU.mult)
                        ins.then_inc(s_gath, 1)
                        dve.wait_ge(s_gath, g + 1)
                        if r:
                            ins = tt(ob[:, b % 2], ob[:, b % 2], tmp_o[:], ALU.add)
                            if r == 2:
                                ins.then_inc(osd_made, 1)
                            else:
                                link(ins)
                    else:
                        link(dve.reciprocal(w[:, 0:1], rs[:, last:last + 1]))
                        link(dve.tensor_scalar(w[:, 4:8], sel4[:], w[:, 0:1], tgate_s[:, b, r:r + 1], ALU.mult, ALU.mult))
                        wb = w[:, 4:8].unsqueeze(2).broadcast_to([P, 4, HD])
                        ov = o[:, 0:256].rearrange("p (h n) -> p h n", h=4)
                        dst = ob[:, b % 2, 0:256] if r == 0 else tmp_o[:, 0:256]
                        ins = tt(dst.rearrange("p (h n) -> p h n", h=4), ov, wb, ALU.mult)
                        ins.then_inc(s_gath, 1)
                        dve.wait_ge(s_gath, g + 1)
                        if r:
                            link(tt(ob[:, b % 2, 0:256], ob[:, b % 2, 0:256], tmp_o[:, 0:256], ALU.add))
                        if r == 2:
                            ow = ob[:, b % 2, 0:256].rearrange("p (h n) -> p n h", h=4)
                            if b >= 2:
                                dve.wait_ge(*emptied(("o", GROUP_OF[ITEMS.index(("s", b - 2, 2, 0))])))
                            dve.tensor_reduce(osd[:, b % 2, 0], ow, axis=X, op=ALU.add)
                            dve.tensor_reduce(osd[:, b % 2, 1], ow, axis=X, op=ALU.add).then_inc(osd_made, 1)
                elif what == "out":
                    kind, b, r, h = ITEMS[GROUPS[i][0]]
                    o = take(("o", i))
                    if kind == "p":
                        empty(dve.tensor_copy(onsaT[:, :, P * b:P * b + P], o.rearrange("p (k n) -> p k n", k=4)))
                    else:
                        at = NP_ + 2 * NDEC * b
                        for e in range(2):
                            dv = onsaT[HD * e:HD * e + HD, :, at:at + 2 * NDEC].rearrange("p k (a q) -> p a k q", a=2)
                            sv = o[HD * e:HD * e + HD, 0:P].rearrange("p (a k e q) -> p a k e q", a=2, k=4, e=2)[:, :, :, e]
                            ins = dve.tensor_copy(dv, sv)
                        empty(ins)
            for m in range(KD):
                for h in range(2):
                    n = 2 * (2 * m + h)
                    cut = slice(HALF * h, HALF * h + HALF)
                    for w, key in enumerate(("ab", "bb")):
                        o = take((key, m, h))
                        dve.wait_ge(*emptied(("ga" if w == 0 else "gb", m, h)))
                        ins = dve.scalar_tensor_tensor(mt[:, w], tg[:, (n + w) % 4], 1.0, o[:, 0:HALF], ALU.add, ALU.mult)
                        empty(ins)
                        dve.wait_ge(*emptied((key, m, h)))
                    tt(merged[:, m, cut], mt[:, 0], mt[:, 1], ALU.add).then_inc(merged_made, 1)
                    dve.wait_ge(merged_made, 2 * m + h + 1)
            dve.wait_ge(x_res, 16 * NT)
            for t in range(NT):
                p = TILES[t]
                for c in range(2):
                    o = take(("wo", t, c))
                    cut = slice(512 * c, 512 * c + 512)
                    ins = dve.scalar_tensor_tensor(x[0:p, t, cut], o[0:p, :], 0.25, x[0:p, t, cut], ALU.mult, ALU.add)
                    empty(ins)
            dve.wait_ge(*emptied(("wo", NT - 1, 1)))
            dve.wait_ge(rt_ld, 64)
            link(dve.memset(lg[:], 0.0))
            for t in range(NT):
                p = TILES[t]
                dve.wait_ge(rstd_done, NT + t + 1)
                if t >= 2:
                    dve.wait_ge(pe_done, PLAN.done(("h2T", t - 2, 1)))
                dve.tensor_scalar(hn[0:p, t % 2], x[0:p, t], stat[0:p, 2, t:t + 1], None, ALU.mult).then_inc(hn_made, 1)
                if t:
                    turned_norm(dve, t - 1, ("h2T", t - 1), 1, take, empty)
                    router_logits(dve, t - 1, take, empty)
            turned_norm(dve, NT - 1, ("h2T", NT - 1), 1, take, empty)
            router_logits(dve, NT - 1, take, empty)
            dve.wait_ge(*emptied(("rt", NT - 1)))

            q = [P, NT, 4]
            G, E1, E2, S1, S2, W4, T4, T5 = (rtmp[:, j] for j in range(8))

            def first_of_largest(sel, v, mx):
                link(dve.tensor_reduce(mx, v, axis=X, op=ALU.max))
                link(tt(sel, v, mx.unsqueeze(2).broadcast_to(q), ALU.is_equal))
                for j in range(4):
                    ins = dve.tensor_scalar(T5[:, :, j:j + 1], sel[:, :, j:j + 1], float(4 - j), None, ALU.mult)
                link(ins)
                link(dve.tensor_reduce(rtmp[:, 9, :, 0], T5, axis=X, op=ALU.max))
                link(tt(sel, T5, rtmp[:, 9, :, 0].unsqueeze(2).broadcast_to(q), ALU.is_equal))

            gl = lg[:, :, 0:4]
            mxg, m1, m2 = rtmp[:, 8, :, 0], rtmp[:, 8, :, 1], rtmp[:, 8, :, 2]
            first_of_largest(G, gl, mxg)
            el = lg[:, :, 4:20].rearrange("p t (g e) -> p t g e", g=4)
            for g in range(4):
                gb = G[:, :, g:g + 1].broadcast_to(q)
                if g == 0:
                    link(tt(E1, el[:, :, 0], gb, ALU.mult))
                else:
                    link(tt(T4, el[:, :, g], gb, ALU.mult))
                    link(tt(E1, E1, T4, ALU.add))
            first_of_largest(S1, E1, m1)
            link(dve.scalar_tensor_tensor(E2, S1, NEG, E1, ALU.mult, ALU.add))
            first_of_largest(S2, E2, m2)
            tt(r16[:, :, 0:4], gl, mxg.unsqueeze(2).broadcast_to(q), ALU.subtract)
            tt(r16[:, :, 4:5], m2.unsqueeze(2), m1.unsqueeze(2), ALU.subtract).then_inc(lg_made, 1)
            dve.wait_ge(lg_exp, 1)
            link(dve.tensor_reduce(rtmp[:, 10, :, 0], r16[:, :, 0:4], axis=X, op=ALU.add))
            link(dve.tensor_scalar(rtmp[:, 10, :, 1], r16[:, :, 4], 1.0, None, ALU.add))
            link(tt(rtmp[:, 10, :, 0], rtmp[:, 10, :, 0], rtmp[:, 10, :, 1], ALU.mult))
            link(dve.reciprocal(rtmp[:, 10, :, 0], rtmp[:, 10, :, 0]))
            link(dve.tensor_scalar(rtmp[:, 10, :, 0], rtmp[:, 10, :, 0], 0.5, None, ALU.mult))
            link(tt(S2, S2, r16[:, :, 4:5].broadcast_to(q), ALU.mult))
            link(tt(S1, S1, S2, ALU.add))
            link(tt(S1, S1, rtmp[:, 10, :, 0].unsqueeze(2).broadcast_to(q), ALU.mult))
            for g in range(4):
                ins = tt(comb[:, :, 4 * g:4 * g + 4], S1, G[:, :, g:g + 1].broadcast_to(q), ALU.mult)
            link(ins)

            dve.sem_inc(act_made, 2)
            dve.sem_inc(dn_free, 4)

            def activate(n, u):
                for s in range(4):
                    f, h = s // 2, s % 2
                    dve.wait_ge(th_made, n * 4 + (s + 1))
                    dve.scalar_tensor_tensor(si[:, s % 2], th[:, s % 2], 1.0, ps[:, 2 * (s % 2), 0:HALF], ALU.add, ALU.mult
                                             ).then_inc(si_made, 1)
                    dve.wait_ge(si_made, n * 4 + (s + 1))
                    tt(actT[:, u, f, HALF * h:HALF * h + HALF], si[:, s % 2], ps[:, 2 * (s % 2) + 1, 0:HALF], ALU.mult
                       ).then_inc(act_made, 1)

            def add_down(n, u):
                for t in range(NT):
                    p = TILES[t]
                    for c in range(2):
                        j = 2 * t + c
                        cut = slice(512 * c, 512 * c + 512)
                        dve.wait_ge(dn_done, n * 10 + (j + 1))
                        one = bass.ds(n, 1) if not isinstance(n, int) else slice(n, n + 1)
                        dve.scalar_tensor_tensor(x[0:p, t, cut], ps[0:p, 4 + (2 * u + j) % 4, :], comb[0:p, t, one],
                                                 x[0:p, t, cut], ALU.mult, ALU.add).then_inc(dn_free, 1)

            activate(0, 0)
            with dve.Fori(0, NE // 2 - 1) as i:
                activate(i * 2 + 1, 1)
                add_down(i * 2, 0)
                activate(i * 2 + 2, 0)
                add_down(i * 2 + 1, 1)
            activate(NE - 1, 1)
            add_down(NE - 2, 0)
            add_down(NE - 1, 1)
            dve.wait_ge(dn_free, 10 * NE + 4)
            for t in range(NT):
                p = TILES[t]
                o = take(("x2T", t, 1))
                empty(dve.tensor_copy(hT[:, 4:8, P * t:P * t + p], o.rearrange("p (k n) -> p k n", k=4)[:, :, 0:p]))
                for c in range(2):
                    cut = slice(512 * c, 512 * c + 512)
                    o = take(("pp", t, c))
                    dve.wait_ge(*emptied(("pg", t, c)))
                    ins = dve.scalar_tensor_tensor(tpg[0:p, c], tpg[0:p, c], 1.0, o[0:p, :], ALU.add, ALU.mult)
                    empty(ins)
                    dve.wait_ge(*emptied(("pp", t, c)))
                    dve.scalar_tensor_tensor(x[0:p, t, cut], tpg[0:p, c], 0.5, x[0:p, t, cut], ALU.mult, ALU.add
                                             ).then_inc(x3_made, 1)
            dve.wait_ge(gf_ld, 16)
            for t in range(NT):
                p = TILES[t]
                dve.wait_ge(rstd_done, 2 * NT + t + 1)
                dve.wait_ge(x3_made, 2 * t + 2)
                dve.scalar_tensor_tensor(x[0:p, t], x[0:p, t], stat[0:p, 2, t:t + 1], gf[0:p], ALU.mult, ALU.mult
                                         ).then_inc(y_made, 1)


_INS = ["x_prompt", "x_sample", "p_prompt", "p_sample", "cache_cmp_kv", "cache_slc_kv", "cache_win_kv", "state_ssm",
        "page_table", "norm1_g", "w_in", "ssm_lam_re", "ssm_lam_im", "ssm_log_dt", "ssm_b_re", "ssm_b_im", "ssm_c_re",
        "ssm_c_im", "ssm_d", "w_glu", "b_glu", "cmp_pe", "cmp_w1", "cmp_w2", "w_ssm_out", "w_nsa_out", "w_o", "norm2_g",
        "w_route_group", "b_route_group", "w_route_expert", "b_route_expert", "w_exp_gate", "w_exp_up", "w_exp_down",
        "w_ple", "w_ple_gate", "final_norm_g"]
_OUTS = [(1, NP_, D), (NSEQ, NDEC, D), (1, 1, NP_, 2, NKV, HD), (1, 1, NP_, 2, NKV, HD), (1, 1, NP_, 2, NKV, HD),
         (1, 1, NG, NST, 2), (1, NSEQ, NDEC, 2, NKV, HD), (1, NSEQ, NDEC, 2, NKV, HD),
         (1, NSEQ, PAST + NDEC, 2, NKV, HD), (1, NSEQ, NG, NST, 2)]


def kernel(**inputs):
    import concourse.bacc as bacc
    from concourse.bass_utils import run_bass_kernel_spmd

    nc = bacc.Bacc("TRN2", target_bir_lowering=False, num_devices=1)
    arrays, ins, outs = {}, {}, []
    for name in _INS:
        a = np.ascontiguousarray(inputs[name])
        arrays[f"in_{name}"] = a
        ins[name] = nc.dram_tensor(f"in_{name}", a.shape, mybir.dt.from_np(a.dtype), kind="ExternalInput").ap()
    for i, shape in enumerate(_OUTS):
        outs.append(nc.dram_tensor(f"out_{i}", shape, F32, kind="ExternalOutput").ap())
    build(nc, ins, outs)
    r = run_bass_kernel_spmd(nc, [arrays], core_ids=[0])
    return tuple(r.results[0][f"out_{i}"] for i in range(len(_OUTS)))
```

```python
from contextlib import ExitStack
import math

import numpy as np

import concourse.bass as bass
from concourse import mybir

F32 = mybir.dt.float32
BF16 = mybir.dt.bfloat16
I32 = mybir.dt.int32
ALU = mybir.AluOpType
ACT = mybir.ActivationFunctionType
X = mybir.AxisListType.X

P = 128
D = 1024
KD = D // P
NP_, NSEQ, NDEC = 512, 8, 8
ROWS = NP_ + NSEQ * NDEC
HALF = ROWS // 2
TILES = [128, 128, 128, 128, 64]
NT = len(TILES)
PAST, PAGE = 256, 128
SSM_W, GRP, NG, NST = 512, 16, 32, 64
CH = 8
NCH = ROWS // CH
NPC = NP_ // CH
NS = NG // 2
HD, NH, NKV, GQA = 64, 8, 2, 4
KVW = 256
COL_Q, COL_KV, COL_GA, COL_GB = 512, 1024, 1816, 2840
NKVG = 3 * KVW + 3 * NH
SCALE = HD ** -0.5
NEG = -1e30
CL, CS = 32, 16
CT0 = CL
CTOK = CT0 + NP_ + NSEQ * PAST
NBLK = CTOK // CS - 1
CJ_P = CT0 // CS
CJ_S = CJ_P + NP_ // CS
SJ = PAST // CS
NE, FF = 16, 256
PLE = 256
CAP = 128
MAXR = -(-ROWS // CAP)
EPS = 1e-6
RING = 6
GELU = ACT.Gelu_apprx_tanh


class Plan:

    def __init__(self):
        self.at, self.by, self.count, self.order = {}, {}, {}, []

    def add(self, key, engine):
        self.at[key] = len(self.order)
        self.order.append(key)
        self.count[engine] = self.count.get(engine, 0) + 1
        self.by[key] = (engine, self.count[engine])

    def done(self, key):
        return self.at[key] + 1


def attention_items():
    items = []
    for b in range(4):
        items += [("c", b, 0, 0)]
        items += [("p", b, r, h) for r in (1, 2) for h in range(NH)]
    for t in range(NSEQ // 2):
        items += [("sc", t, 0, 0), ("s", t, 1, 0), ("s", t, 2, 0)]
    return items


ITEMS = attention_items()
GROUPS = []
for _i, _it in enumerate(ITEMS):
    if GROUPS and (ITEMS[GROUPS[-1][-1]][:3] == _it[:3]):
        GROUPS[-1].append(_i)
    else:
        GROUPS.append([_i])
GROUP_OF = {i: g for g, m in enumerate(GROUPS) for i in m}
T_LAG, V_LAG, O_LAG = 2, 3, 2


def item_keys(it):
    kind, b = it[0], it[1]
    if kind == "p":
        return [128] * (b + 1)
    if kind == "c":
        return [128, 128]
    return [32] if kind == "sc" else [128, 128, 64]


def attention_steps():
    steps, late = [], []
    n = len(ITEMS)
    for i in range(n + V_LAG + O_LAG):
        if i < n:
            steps.append(("score", i))
        if 0 <= i - T_LAG < n:
            steps.append(("turn", i - T_LAG))
        if 0 <= i - V_LAG < n:
            j = i - V_LAG
            steps.append(("value", j))
            if j == GROUPS[GROUP_OF[j]][-1]:
                steps.append(("gather", GROUP_OF[j]))
                if ITEMS[j][2] == 2:
                    late.append((i + O_LAG, GROUP_OF[j]))
        if late and late[0][0] == i:
            steps.append(("out", late.pop(0)[1]))
    return steps


KD_A = 3


def gate_jobs(p, m):
    for h in range(2):
        for w in ("ga", "gb"):
            p.add((w, m, h), "act")


def gates_out(buf, n):
    return len(range(buf, n, 4))


def make_plan():
    p = Plan()
    for t in range(NT):
        for k in range(2):
            p.add(("hT", t, k), "dve")
    for t in range(NT):
        p.add(("u", t), "act")
    for t in range(NT):
        for c in range(2):
            p.add(("kv", t, c), "act")
    p.add(("lam",), "dve")
    p.add(("c", 0), "dve")
    p.add(("c", 1), "dve")
    p.add(("h0",), "dve")
    for m in range(KD_A):
        gate_jobs(p, m)
    for i in range(5):
        p.add(("x", i), "dve")
    for i in range(8):
        p.add(("vt", i), "act")
    for i in range(8):
        p.add(("k", i), "act")
    for i in range(6):
        p.add(("d", i), "act")
    for m in range(4):
        for h in range(2):
            p.add(("q", m, h), "act")
    for m in range(KD_A, KD):
        gate_jobs(p, m)
    for i in range(8):
        p.add(("y", i), "dve")
    p.add(("fin",), "act")
    for t in range(CH):
        p.add(("zg", t), "dve")
    for m in range(4):
        for h in range(2):
            p.add(("glu", m, h), "act")
    p.add(("pe",), "act")
    for i in range(10):
        p.add(("ct", i), "act")
    for k in range(2):
        p.add(("pre", k), "dve")
    p.add(("kc",), "dve")
    p.add(("vcp",), "dve")
    p.add(("vcs",), "dve")
    for r in range(2):
        p.add(("ktp", r), "act")
    p.add(("ktn",), "act")
    for r in range(2):
        for i in range(4):
            p.add(("kts", r, i), "act")
    for what, i in attention_steps():
        if what == "score":
            p.add(("s", i), "act")
        elif what == "turn":
            p.add(("t", i), "dve" if i % 2 else "act")
        elif what == "out":
            p.add(("o", i), "dve")
    for m in range(KD):
        for h in range(2):
            for w in ("ab", "bb"):
                p.add((w, m, h), "dve")
    for c in range(2):
        for t in range(NT):
            p.add(("wo", t, c), "dve")
    for t in range(NT):
        for k in range(2):
            p.add(("h2T", t, k), "dve")
        p.add(("rt", t), "dve")
    for t in range(NT):
        p.add(("pT", t), "act")
    p.add(("rank",), "dve")
    for t in range(NT):
        for k in range(2):
            p.add(("x2T", t, k), "dve" if k else "act")
        for c in range(2):
            p.add(("pg", t, c), "act")
            p.add(("pp", t, c), "dve")
    return p


PLAN = make_plan()

WEIGHTS = [("u", ("u", NT - 1)), ("kv0", ("kv", NT - 1, 0)), ("kv1", ("kv", NT - 1, 1)), ("g0", ("gb", 1, 1)),
           ("g1", ("gb", 3, 1)), ("q", ("q", 3, 1)), ("g2", ("gb", 5, 1)), ("g3", ("gb", 7, 1)), ("glu", ("glu", 3, 1)),
           ("so", ("ab", KD - 1, 1)), ("no", ("bb", KD - 1, 1)), ("wo0", ("wo", NT - 1, 0)), ("wo1", ("wo", NT - 1, 1)),
           ("ple", ("pp", NT - 1, 1)), ("pg0", ("pg", NT - 1, 0)), ("pg1", ("pg", NT - 1, 1))]
NW = 3
W_AT = {name: i for i, (name, _) in enumerate(WEIGHTS)}


def build(nc, I, O):
    (y_prompt, y_sample, o_cmp_p, o_slc_p, o_win_p, o_ssm_p, o_cmp_s, o_slc_s, o_win_s, o_ssm_s) = O
    u_dram = nc.dram_tensor("u_rows", (ROWS, SSM_W), F32).ap()
    g_dram = nc.dram_tensor("gate_rows", (NSEQ * NDEC, 3 * NH), F32).ap()
    tg_dram = nc.dram_tensor("gates_by_features", (KD, P, 2, ROWS), F32).ap()
    k_dram = nc.dram_tensor("kernel_taps", (GRP, NG, P), F32).ap()
    h2_dram = nc.dram_tensor("h2_rows", (ROWS, D), F32).ap()
    list_dram = nc.dram_tensor("row_of_slot", (NE * MAXR * CAP, 1), I32).ap()
    ye_dram = nc.dram_tensor("expert_rows", (NE * CAP, D), F32).ap()
    w_in = I["w_in"][0]
    n_pool = I["cache_cmp_kv"].shape[1]
    PARS = 16 * 13

    with ExitStack() as ctx:
        def sem(name):
            return ctx.enter_context(nc.semaphore(name))

        def sb(name, shape, dt=F32, stack=ctx):
            return stack.enter_context(nc.sbuf_tensor(name, shape, dt))

        def flat(t):
            return (t if isinstance(t, bass.AP) else t[:]).rearrange("p a b -> p (a b)")

        ps = ctx.enter_context(nc.psum_tensor("ps", [P, 8, 512], F32))
        ident = sb("ident", [P, P])
        ident_b = sb("ident_b", [P, P], BF16)
        causal = sb("causal", [P, P], BF16)
        new_mask = sb("new_mask", [P, 4, 64], BF16)
        g_cols = sb("g_cols", [P, 2, KD])
        tri_b = sb("tri_b", [P, P], BF16)
        ones_b = sb("ones_b", [P, P], BF16)
        msk_b = sb("msk_b", [P, NT, NE], BF16)
        tokid = sb("tokid", [P, NT], I32)
        ebase = sb("ebase", [P, NE])
        zero_i = sb("zero_i", [P, NE * MAXR], I32)
        halfneg = sb("halfneg", [P, 1])
        stat = sb("stat", [P, 4, 8])
        b_glu = sb("b_glu", [P, 4])
        ptab = sb("ptab", [1, 2 * NSEQ], I32)
        ring = [sb(f"w_slot{i}", [P, 4096]) for i in range(NW)]
        hT = sb("hT", [P, KD, ROWS])
        gates = flat(hT).rearrange("p (m w n) -> p m w n", m=4, w=2)
        kv = sb("kv", [P, NT, NKVG])
        tgate = sb("tgate", [P, NT, 3 * NH])
        tgate_s = sb("tgate_s", [P, 4, 3])
        qg_t = sb("qg", [P, 2 * 4 * ROWS])
        qT = qg_t[:, 0:4 * ROWS].rearrange("p (g n) -> p g n", g=GQA)
        gluT = qg_t[:, 4 * ROWS:].rearrange("p (k n) -> p k n", k=4)
        ucg = qg_t[0:NCH, 0:CH * SSM_W].rearrange("p (g n) -> p g n", g=NG)

        with ExitStack() as s5:
            x_in = sb("x_in", [P, NT, D], stack=s5)
        with ExitStack() as s5:
            pw = sb("pw", [P, CH + 1, 2, NS], stack=s5)
            pwr = sb("pwr", [P, CH, 2, NS], stack=s5)
            sm = sb("sm", [P, 24, NS], stack=s5)
            bbar = sb("bbar", [P, 2, NS, GRP], stack=s5)
            vt = sb("vt", [P, NS * 2, P], stack=s5)
            zgT = vt[:].rearrange("p a b -> p (a b)")[:, 0:4 * ROWS].rearrange("p (k n) -> p k n", k=4)
            gm = sb("gm", [P, 2, NS, CH + 1, GRP], stack=s5)
            xg_t = sb("xg", [P, NT * SSM_W], stack=s5)
            u_rows = xg_t[:].rearrange("p (t n) -> p t n", t=NT)
            stage_a = xg_t[:, 0:8 * HALF].rearrange("p (b w n) -> p b w n", b=4, w=2)
            stage_b = flat(gluT).rearrange("p (b w n) -> p b w n", b=4, w=2)
            xg = xg_t[:, 0:NG * NCH].rearrange("p (g n) -> p g n", g=NG)
            hst = sb("hst", [P, 2, NS, NCH], stack=s5)
            fin = sb("fin", [P, 2, 1 + NSEQ, NS], stack=s5)
            walk = sb("walk", [P, 4, 2, NS], stack=s5)
            vn_t = sb("vn", [P, NS * 2 * P], stack=s5)
            vn = vn_t[:].rearrange("p (s r n) -> p s r n", s=NS, r=2)
            wt = vn_t[:].rearrange("p (g n) -> p g n", g=NG)
            uc_t = sb("uc", [P, NS * (2 * CH + 1) * GRP], stack=s5)
            uc = uc_t[0:NCH, 0:CH * SSM_W].rearrange("p (t n) -> p t n", t=CH)
            tmp_v = uc_t[:, 0:NS * CH * GRP]
            tmp_g = uc_t[:, NS * CH * GRP:]
            lam_r = sb("lam_r", [NS, 2, P], stack=s5)
            raw = sb("raw", [P, 1024], stack=s5)
            c_r = hst[:].rearrange("p r s c -> p (r s c)")[:, 0:1024].rearrange("p (r b u n) -> p r b u n", r=2, b=4, u=2)
            b_r = raw[:, 512:1024].rearrange("p (r s c) -> p r s c", r=2, s=NS)
            ks = raw[0:GRP, :].rearrange("p (u g n) -> p u g n", u=2, g=4)
            cst = sb("cst", [P, 2, NS, GRP], stack=s5)
            tmp9 = cst[:].rearrange("p r s c -> p (r s c)")[:, 0:2 * 9 * NS].rearrange("p (r q s) -> p r q s", r=2, q=9)
            h0_r = sb("h0_r", [P, 2 * P], stack=s5)
            fo = h0_r[:].rearrange("p (n r) -> p n r", r=2)
            fo_p = sb("fo_p", [NS, P, 2], stack=s5)
            d_b = sb("d_b", [NCH, SSM_W], stack=s5)
            ldt = sb("ldt", [P, NS], stack=s5)

        with ExitStack() as late:
            onsaT = sb("onsaT", [P, 4, ROWS], stack=late)
            with ExitStack() as at:
                w1_t = sb("w1", [P, 2 * CL * P], stack=at)
                w1 = w1_t[:].rearrange("p (k i e) -> p k i e", k=2, i=CL)
                caches = w1_t[:].rearrange("p (r s h n) -> p r s h n", r=2, s=NSEQ, h=2)
                kvct_t = sb("kvct", [P, 2 * CTOK], stack=at)
                kvct = kvct_t[:].rearrange("p (k n) -> p k n", k=2)
                kts = kvct_t[:, 0:2 * NSEQ * PAST].rearrange("p (r s n) -> p r s n", r=2, s=NSEQ)
                w2 = sb("w2", [P, 2, P], stack=at)
                pe_r = sb("pe_r", [2 * CL, 2, HD], stack=at)
                cxr = sb("cxr", [P, 4, 32], stack=at)
                rawc = sb("rawc", [P, 4, 2, KVW], stack=at)
                cx = sb("cx", [P, 2, 2, NBLK], stack=at)
                cc = sb("cc", [P, 2], stack=at)
                kc = sb("kc", [P, NBLK], stack=at)
                vcbd = sb("vcbd", [P, NKV, GQA, HD], stack=at)
                vcs = sb("vcs", [32, 4, P], stack=at)
                kt = sb("kt", [P, 2, ROWS], stack=at)
                qpad = sb("qpad", [P, NSEQ, P], stack=at)
                pb = rawc[:].rearrange("p b t n -> p (b t n)")[:, 0:3 * 512].rearrange("p (b n) -> p b n", b=3)
                pt = sb("pt", [P, 2, 512], stack=at)
                ob = sb("ob", [P, 2, 512], stack=at)
                tmp_o = sb("tmp_o", [P, 512], stack=at)
                sct = sb("sct", [P, 256], stack=at)
                osd = sb("osd", [P, 2, 2, HD], stack=at)
                nm = sb("nm", [P, len(ITEMS)], stack=at)
                rs = sb("rs", [P, len(ITEMS)], stack=at)
                mx8 = sb("mx8", [P, NH], stack=at)
                rs8 = sb("rs8", [P, NH], stack=at)
                w8 = sb("w8", [P, 2, NH], stack=at)
                cm01 = sb("cm01", [P, 4, 32], stack=at)
                cmneg = sb("cmneg", [P, 4, 32], stack=at)
                csneg = sb("csneg", [P, 3, 32], stack=at)
                sel4 = sb("sel4", [P, 4], stack=at)
                rowi = sb("rowi", [P, 3], I32, stack=at)
                rowf = sb("rowf", [P, 4], stack=at)
                nmk = sb("nmk", [P, 3, 4, 64], stack=at)
            with ExitStack() as fin_s:
                merged = sb("merged", [P, KD, ROWS], stack=fin_s)
                x = sb("x", [P, NT, D], stack=fin_s)
                mt = sb("mt", [P, 2, HALF], stack=fin_s)
                hn = sb("hn", [P, 2, D], stack=fin_s)
                w_rt = sb("w_rt", [P, KD, 20], stack=fin_s)
                b_rt = sb("b_rt", [P, 20], stack=fin_s)
                lg = sb("lg", [P, NT, 20], stack=fin_s)
                rtmp = sb("rtmp", [P, 12, NT, 4], stack=fin_s)
                r16 = sb("r16", [P, NT, 16], stack=fin_s)
                wgu = sb("wgu", [P, 2, 2, KD, FF], stack=fin_s)
                wdn = flat(merged)[:, 0:4 * D].rearrange("p (u k n) -> p u k n", u=2, k=2)
                th = sb("th", [P, 2, FF], stack=fin_s)
                si = sb("si", [P, 2, FF], stack=fin_s)
                actT = sb("actT", [P, 2, 2, CAP], stack=fin_s)
                both = th[:].rearrange("p u n -> p (u n)")[:, 0:4 * NT * NE].rearrange("p (a c t e) -> p a c t e", a=2, c=2, t=NT)
                sel = sb("sel", [P, 2, NT, NE], stack=fin_s)
                rk = sb("rk", [P, NT, NE], stack=fin_s)
                pos_f = sb("pos_f", [P, 4, 2, NT], stack=fin_s)
                rank = sb("rank", [P, 2, NT], stack=fin_s)
                base = sb("base", [P, 2, NT], stack=fin_s)
                wt_j = sb("wt_j", [P, 2, NT], stack=fin_s)
                pos_i = sb("pos_i", [P, 2, 2, NT], I32, stack=fin_s)
                wts = sb("wts", [P, 2, NT], stack=fin_s)
                tick = sb("tick", [P, 2], stack=fin_s)
                idx = sb("idx", [P, 2], I32, stack=fin_s)
                rnd_f = sb("rnd_f", [1, 8], stack=fin_s)
                rounds_i = sb("rounds_i", [1, 1], I32, stack=fin_s)
                ysb = flat(onsaT)[:, 0:2 * D].rearrange("p (u n) -> p u n", u=2)
                hg = flat(hT)[:, 0:2 * D].rearrange("p (u n) -> p u n", u=2)
                hgT = flat(hT)[:, 2 * D:4 * D].rearrange("p (u k n) -> p u k n", u=2, k=KD)
                yg = wgu[:].rearrange("p u w k n -> p (u w k n)")[:, 0:4 * D].rearrange("p (u c n) -> p u c n", u=2, c=2)
                p_in = flat(kv)[:, 0:NT * PLE].rearrange("p (t n) -> p t n", t=NT)
                pT = flat(kv)[:, NT * PLE:NT * PLE + 2 * ROWS].rearrange("p (k n) -> p k n", k=2)
                gf = flat(kv)[:, NT * PLE + 2 * ROWS:NT * PLE + 2 * ROWS + D]
                tpg = flat(qT)[:, 0:1024].rearrange("p (u n) -> p u n", u=2)

        pe_done = sem("pe_done")
        drained = {"dve": sem("dve_drained"), "act": sem("act_drained")}
        dve_step, act_step, pool_step = sem("dve_step"), sem("act_step"), sem("pool_step")
        x_ld = [sem(f"x_loaded{t}") for t in range(NT)]
        w_ld = [sem(f"w_loaded{i}") for i in range(NW)]
        gains_ld, par_ld, rt_ld, gf_ld, p_ld = sem("gains_loaded"), sem("s5_params_loaded"), sem("router_loaded"), sem("final_gain_loaded"), sem("ple_rows_loaded")
        consts = sem("constants_made")
        sq_done, rstd_done = sem("sum_squares"), sem("rstd_made")
        u_out, uc_ld, k_out, w_toep = sem("u_written"), sem("u_by_chunks"), [sem(f"taps_written{u}") for u in range(2)], sem("toeplitz_loaded")
        dt_done, angles, trig = sem("dt_made"), sem("angles_made"), sem("sin_cos_made")
        powers, v_made, g_made = sem("powers_made"), sem("v_made"), sem("g_made")
        half_done = sem("first_kv_head_done")
        ucg_made = sem("u_by_groups")
        w_zero, ud_made, walked, y_gelu = sem("toeplitz_zeroed"), sem("skip_made"), sem("states_walked"), sem("y_activated")
        glu_made, fin_out, outs = sem("glu_made"), sem("states_written"), sem("outputs_written")
        gates_made, gd_out, gs_ld = sem("gates_made"), sem("gates_written"), sem("sample_gates_loaded")
        pt_ld = sem("page_table_loaded")
        w1_zero, w1_ld, pe_ld, raw_ld = sem("w1_zeroed"), sem("w1_loaded"), sem("embeddings_loaded"), [sem(f"raw_pages{i}") for i in range(4)]
        cache_ld = sem("caches_loaded")
        cmp_g = sem("cmp_gelu")
        masks, row_masks, qpad_made = sem("masks_made"), sem("row_masks_made"), sem("qpad_made")
        bglu_half, si_made = sem("glu_bias_halved"), sem("silu_made")
        s_max, s_prob, s_val, s_gath = sem("score_max"), sem("probabilities"), sem("values_done"), sem("values_taken")
        osd_made = sem("sample_outputs")
        merged_made = sem("merged_made")
        x_res, hn_made = sem("x_reloaded"), sem("hn_made")
        lg_made, lg_exp = sem("logit_diffs"), sem("logit_exps")
        gu_ld, wd_ld = ([sem(f"{w}_weights_loaded{u}") for u in range(2)] for w in ("gate_up", "down"))
        h2_out, list_zero, listed = [sem(f"h2_written{u}") for u in range(2)], sem("slots_zeroed"), sem("slots_filled")
        msk_made, pos_made, rounds_made = sem("choices_made"), sem("slots_made"), sem("rounds_made")
        idx_ld, hg_ld, hg_free = ([sem(f"{w}{u}") for u in range(2)] for w in ("slot_rows_loaded", "rows_gathered", "rows_turned"))
        t_done = sem("gathered_in_psum")
        hgt_made, g_done, ta_done, actt_made = sem("gathered_turned"), sem("gate_up_done"), sem("act_turned"), sem("actT_made")
        d_done, d_taken, ye_out = sem("down_done"), sem("down_taken"), [sem(f"expert_rows_written{u}") for u in range(2)]
        yg_ld, x2_made = [sem(f"slot_outputs_loaded{u}") for u in range(2)], sem("x2_made")
        pool_tick = sem("pool_tick")
        place_step, x2_half = sem("round_places_step"), sem("first_choice_added")
        tg_out, tg_ld = ([sem(f"{w}{i}") for i in range(4)] for w in ("gates_out", "gates_back"))
        th_made, act_made = sem("gate_tanh"), sem("act_made")
        x3_made, y_made = sem("x3_made"), sem("y_made")

        def bank(key):
            return ps[:, PLAN.at[key] % RING, :]

        def freed(key):
            last = PLAN.order[PLAN.at[key] - RING]
            return drained[PLAN.by[last][0]], PLAN.by[last][1]

        def emptied(key):
            return drained[PLAN.by[key][0]], PLAN.by[key][1]

        w_parts = {"g%d" % i: 2 for i in range(KD // 2)} | {"q": KD * NKV}
        w_need, total = {}, [0] * NW
        for i, (name, _) in enumerate(WEIGHTS):
            total[i % NW] += 16 * w_parts.get(name, 1)
            w_need[name] = (w_ld[i % NW], total[i % NW])

        def slot(name):
            return ring[W_AT[name] % NW]

        def wk(name, n, at=0, k=KD):
            return slot(name)[:, at:at + k * n].rearrange("p (k n) -> p k n", k=k)

        block = ctx.enter_context(nc.Block())

        @block.sync
        def _(sp):
            xp = I["x_prompt"][0].rearrange("(t p) d -> p t d", p=P)
            xs = I["x_sample"].rearrange("s q d -> (s q) d")

            def rows(src, t, dst):
                a = src[0][:, t, :] if t < 4 else src[1]
                return sp.dma_start(dst[0:TILES[t], t, :], a)

            def load_weights(name):
                i = W_AT[name]
                if i >= NW:
                    sp.wait_ge(pe_done, PLAN.done(WEIGHTS[i - NW][1]))
                s = w_ld[i % NW]

                def one(src, at, n, k=KD):
                    sp.dma_start(slot(name)[:, at:at + k * n].rearrange("p (k n) -> p k n", k=k),
                                 src.rearrange("(k p) n -> p k n", p=P)).then_inc(s, 16)
                if name == "u":
                    one(w_in[:, 0:512], 0, 512)
                elif name == "kv0":
                    one(w_in[:, COL_KV:COL_KV + 396], 0, 396)
                elif name == "kv1":
                    one(w_in[:, COL_KV + 396:COL_GA], 0, 396)
                elif name == "q":
                    for k in range(KD):
                        for h in range(NKV):
                            sp.dma_start(slot(name)[:, 512 * k:512 * k + 512].rearrange("p (m h n) -> p h m n", m=GQA, h=NKV)[:, h],
                                         w_in[P * k:P * k + P, COL_Q + 256 * h:COL_Q + 256 * h + 256].rearrange("p (m n) -> p m n", m=GQA)
                                         ).then_inc(s, 16)
                elif name == "glu":
                    one(I["w_glu"][0], 0, 512, 4)
                elif name[:2] == "wo":
                    c = int(name[2:])
                    one(I["w_o"][0][:, 512 * c:512 * c + 512], 0, 512)
                elif name == "ple":
                    one(I["w_ple"][0], 0, D, 2)
                elif name[:2] == "pg":
                    c = int(name[2:])
                    one(I["w_ple_gate"][0][:, 512 * c:512 * c + 512], 0, 512)
                elif name == "so":
                    one(I["w_ssm_out"][0], 0, D, 4)
                elif name == "no":
                    one(I["w_nsa_out"][0], 0, D, 4)
                else:
                    at = 2 * P * int(name[1:])
                    one(w_in[:, COL_GA + at:COL_GA + at + 2 * P], 0, 2 * P)
                    one(w_in[:, COL_GB + at:COL_GB + at + 2 * P], 2048, 2 * P)

            for t in range(NT):
                rows((xp, xs), t, x_in).then_inc(x_ld[t], 16)
            for name in ("u", "kv0", "kv1"):
                load_weights(name)
            for t in range(NT):
                sp.wait_ge(*emptied(("u", t)))
                sp.dma_start(u_dram[P * t:P * t + TILES[t], :], u_rows[0:TILES[t], t, :]).then_inc(u_out, 16)
            load_weights("g0")
            load_weights("g1")
            load_weights("q")
            sp.wait_ge(*emptied(("kv", NT - 1, 1)))
            for n, (op, os) in enumerate(((o_cmp_p, o_cmp_s), (o_slc_p, o_slc_s), (o_win_p, None))):
                sp.dma_start(op[0, 0].rearrange("(t p) a h d -> p t (a h d)", p=P),
                             kv[:, 0:4, KVW * n:KVW * n + KVW]).then_inc(outs, 16)
                if os is not None:
                    sp.dma_start(os[0].rearrange("s q a h d -> (s q) (a h d)"),
                                 kv[0:64, 4, KVW * n:KVW * n + KVW]).then_inc(outs, 16)
            for s in range(NSEQ):
                sp.dma_start(o_win_s[0, s, PAST:PAST + NDEC].rearrange("q a h d -> q (a h d)"),
                             kv[NDEC * s:NDEC * s + NDEC, 4, 2 * KVW:3 * KVW]).then_inc(outs, 16)
            sp.dma_start(o_win_s[0, :, 0:PAST].rearrange("s p a h d -> s (p a h d)"),
                         I["cache_win_kv"][0].rearrange("s p a h d -> s (p a h d)")).then_inc(outs, 16)
            n_outs = 16 * (3 + 2 + NSEQ + 1)
            sp.wait_ge(u_out, 16 * NT)
            sp.wait_ge(v_made, 1)
            sp.wait_ge(g_made, 1)
            sp.dma_start(uc, u_dram.rearrange("(c t) n -> c t n", t=CH)).then_inc(uc_ld, 16)
            sp.wait_ge(gates_made, NT + 2)
            sp.dma_start(g_dram, tgate[0:64, NT - 1, :]).then_inc(gd_out, 16)
            sp.wait_ge(gd_out, 16)
            gv = g_dram.rearrange("(t a q) (k g r) -> a k g q t r", a=2, q=NDEC, k=NKV, g=GQA)
            for a in range(2):
                for k in range(NKV):
                    for g in range(GQA):
                        row = 64 * a + 32 * k + NDEC * g
                        sp.dma_start(tgate_s[row:row + NDEC], gv[a, k, g]).then_inc(gs_ld, 16)
            load_weights("g2")
            for i in range(8):
                sp.wait_ge(*emptied(("k", i)))
                sp.dma_start(k_dram[:, 8 * (i // 2) + i % 2:8 * (i // 2) + i % 2 + 7:2, :], ks[:, i % 2, :, :]).then_inc(k_out[i % 2], 16)
            for u in range(2):
                sp.wait_ge(k_out[u], 16 * 4)
            sp.wait_ge(w_zero, 1)
            for t in range(CH):
                sp.dma_start(wt[GRP * t:GRP * t + GRP, :, GRP * t:P], k_dram[:, :, 0:P - GRP * t]).then_inc(w_toep, 16)
            load_weights("g3")
            load_weights("glu")
            sp.wait_ge(*emptied(("fin",)))
            sp.dma_start(o_ssm_s[0].rearrange("q (s g) n r -> (q s) (g n r)", g=2),
                         fo.rearrange("p n r -> p (n r)")).then_inc(fin_out, 16)
            sp.dma_start(o_ssm_p[0, 0].rearrange("(s g) n r -> s (g n r)", g=2),
                         fo_p[:].rearrange("p n r -> p (n r)")).then_inc(fin_out, 16)

            sp.wait_ge(fin_out, 32)
            sp.wait_ge(glu_made, 8)
            for u in range(2):
                sp.dma_start(pe_r[:, u], I["cmp_pe"][0].rearrange("k i d -> (k i) d")).then_inc(pe_ld, 16)
            sp.wait_ge(pt_ld, 16)
            pages = [[None] * 2 for _ in range(NSEQ)]

            def page(s, u):
                return sp.value_load(ptab[0:1, 2 * s + u:2 * s + u + 1], min_val=0, max_val=n_pool - 1)

            def load_raw(s):
                for u in range(2):
                    sp.dma_start(rawc[:, s % 4, u, :],
                                 I["cache_cmp_kv"][0, bass.ds(page(s, u), 1)].rearrange("o p a h d -> (o p) (a h d)")
                                 ).then_inc(raw_ld[s % 4], 16)
            for s in range(4):
                load_raw(s)
            sp.wait_ge(w1_zero, 1)
            for h in range(NKV):
                for k in range(2):
                    sp.dma_start(w1[HD * h:HD * h + HD, k, :, HD * h:HD * h + HD],
                                 I["cmp_w1"][0][k].rearrange("i d e -> d i e")).then_inc(w1_ld, 16)
                sp.dma_start(w2[HD * h:HD * h + HD, :, HD * h:HD * h + HD],
                             I["cmp_w2"][0].rearrange("k d e -> d k e")).then_inc(w1_ld, 16)
            for s in range(4, NSEQ):
                sp.wait_ge(pe_done, PLAN.done(("ct", 2 + s - 4)))
                load_raw(s)
            sp.wait_ge(pe_done, PLAN.done(("pre", 1)))
            sp.dma_start(caches[:, 1], I["cache_win_kv"][0].rearrange("s (h p) a b d -> p s h (a b d)", p=P)
                         ).then_inc(cache_ld, 16)
            for s in range(NSEQ):
                for u in range(2):
                    sp.dma_start(caches[:, 0, s, u, :],
                                 I["cache_slc_kv"][0, bass.ds(page(s, u), 1)].rearrange("o p a h d -> (o p) (a h d)")
                                 ).then_inc(cache_ld, 16)
            load_weights("so")
            load_weights("no")
            load_weights("wo0")

            def load_gates(m):
                sp.dma_start(gates[:, m % 4], tg_dram[m]).then_inc(tg_ld[m % 4], 16)
            sp.wait_ge(pe_done, PLAN.done(("gb", KD - 1, 1)))
            for b in range(4):
                sp.wait_ge(tg_out[b], 16 * gates_out(b, 2 * KD))
            for m in range(4):
                load_gates(m)
            sp.wait_ge(pe_done, PLAN.done(("o", len(GROUPS) - 1)))
            sp.wait_ge(*emptied(("o", len(GROUPS) - 1)))
            for t in range(NT):
                rows((xp, xs), t, x).then_inc(x_res, 16)
            sp.dma_start(w_rt[:, :, 0:4], I["w_route_group"][0].rearrange("(k p) n -> p k n", p=P)).then_inc(rt_ld, 16)
            sp.dma_start(w_rt[:, :, 4:20], I["w_route_expert"][0].rearrange("(k p) n -> p k n", p=P)).then_inc(rt_ld, 16)
            sp.dma_start(b_rt[:, 0:4], I["b_route_group"].broadcast_to([P, 4])).then_inc(rt_ld, 16)
            sp.dma_start(b_rt[:, 4:20], I["b_route_expert"].broadcast_to([P, 16])).then_inc(rt_ld, 16)
            for m in range(4, KD):
                sp.wait_ge(merged_made, 2 * (m - 4) + 2)
                load_gates(m)
            load_weights("wo1")

            def load_gate_up(e, u):
                one = bass.ds(e, 1) if not isinstance(e, int) else slice(e, e + 1)
                sp.dma_start(wgu[:, u, :, :, :][:, 0], I["w_exp_gate"][0, one].rearrange("o (k p) n -> p (o k) n", p=P)).then_inc(gu_ld[u], 16)
                sp.dma_start(wgu[:, u, :, :, :][:, 1], I["w_exp_up"][0, one].rearrange("o (k p) n -> p (o k) n", p=P)).then_inc(gu_ld[u], 16)

            def load_down(e, u):
                one = bass.ds(e, 1) if not isinstance(e, int) else slice(e, e + 1)
                sp.dma_start(wdn[:, u], I["w_exp_down"][0, one].rearrange("o (k p) n -> p (o k) n", p=P)).then_inc(wd_ld[u], 16)
            for u in range(2):
                load_gate_up(u, u)
            sp.wait_ge(outs, n_outs)
            sp.dma_start(gf, I["final_norm_g"].rearrange("(o n) -> o n", o=1).broadcast_to([P, D])).then_inc(gf_ld, 16)
            sp.dma_start(p_in[:, 0:4], I["p_prompt"][0, 0].rearrange("(t p) n -> p t n", p=P)).then_inc(p_ld, 16)
            sp.dma_start(p_in[0:64, 4], I["p_sample"][0].rearrange("s q n -> (s q) n")).then_inc(p_ld, 16)
            load_weights("ple")
            sp.wait_ge(pe_done, PLAN.done(("wo", NT - 1, 1)))
            for u in range(2):
                load_down(u, u)
            load_weights("pg0")
            load_weights("pg1")
            sp.wait_ge(rounds_made, 1)
            rounds = sp.value_load(rounds_i[0:1, 0:1], min_val=1, max_val=MAXR)
            with sp.Fori(0, rounds) as j:
                with sp.Fori(0, NE // 2 - 1) as i:
                    for u in range(2):
                        sp.wait_ge(g_done, j * 16 + i * 2 + (u + 1))
                        load_gate_up(i * 2 + (u + 2), u)
                        sp.wait_ge(d_done, j * 32 + i * 4 + (2 * u + 2))
                        load_down(i * 2 + (u + 2), u)
                with sp.If(j + 1 < rounds):
                    sp.wait_ge(x2_made, j * NT + 2 * NT)
                    for u in range(2):
                        sp.wait_ge(d_done, j * 32 + (28 + 2 * u + 2))
                        load_gate_up(u, u)
                        load_down(u, u)
            ysm = y_sample.rearrange("s q d -> (s q) d")
            for t in range(NT):
                sp.wait_ge(y_made, t + 1)
                dst = y_prompt[0][P * t:P * t + P, :] if t < 4 else ysm
                sp.dma_start(dst, x[0:TILES[t], t, :]).then_inc(outs, 16)
            sp.wait_ge(outs, n_outs + 16 * NT)

        @block.gpsimd
        def _(pool):
            count = [0]

            def link(ins):
                count[0] += 1
                ins.then_inc(pool_step, 1)
                pool.wait_ge(pool_step, count[0])

            link(pool.memset(ident[:], 0.0))
            link(pool.affine_select(out=ident[:], in_=ident[:], compare_op=ALU.not_equal, fill=1.0, base=0,
                                    pattern=[[-1, P]], channel_multiplier=1))
            pool.tensor_copy(ident_b[:], ident[:]).then_inc(consts, 1)
            link(pool.memset(causal[:], 0.0))
            pool.affine_select(out=causal[:], in_=causal[:], compare_op=ALU.is_ge, fill=NEG, base=0,
                               pattern=[[-1, P]], channel_multiplier=1).then_inc(consts, 1)
            link(pool.memset(halfneg[:], -0.5))
            link(pool.memset(zero_i[:], 0))
            pool.dma_start(list_dram.rearrange("(p n) o -> p (n o)", p=P), zero_i[:]).then_inc(list_zero, 16)
            pool.memset(ones_b[:], 1.0)
            link(pool.memset(tri_b[:], 0.0))
            link(pool.affine_select(out=tri_b[:], in_=tri_b[:], compare_op=ALU.is_ge, fill=1.0, base=0,
                                    pattern=[[-1, P]], channel_multiplier=1))
            pool.iota(ebase[:], [[CAP, NE]], base=0, channel_multiplier=0, allow_small_or_imprecise_dtypes=True)
            pool.iota(tokid[:], [[P, NT]], base=0, channel_multiplier=1).then_inc(consts, 1)

            def rstd(t, at):
                p = TILES[t]
                link(pool.tensor_scalar(stat[0:p, 1, t:t + 1], stat[0:p, 0, t:t + 1], 1.0 / D, EPS, ALU.mult, ALU.add))
                pool.tensor_tensor(stat[0:p, 2, t:t + 1], stat[0:p, 1, t:t + 1], halfneg[0:p], ALU.pow).then_inc(rstd_done, 1)

            for t in range(NT):
                pool.wait_ge(sq_done, t + 1)
                rstd(t, 0)

            pool.wait_ge(powers, 1)
            pool.wait_ge(*emptied(("c", 1)))
            n9 = [P, NS, CH + 1, GRP]
            pr = pw[:, :, 0, :].rearrange("p t s -> p s t").unsqueeze(3).broadcast_to(n9)
            pi = pw[:, :, 1, :].rearrange("p t s -> p s t").unsqueeze(3).broadcast_to(n9)
            cr = cst[:, 0].unsqueeze(2).broadcast_to(n9)
            ci = cst[:, 1].unsqueeze(2).broadcast_to(n9)
            tg9 = tmp_g.rearrange("p (s t c) -> p s t c", s=NS, t=CH + 1)
            link(pool.tensor_tensor(gm[:, 0], pr, cr, ALU.mult))
            link(pool.tensor_tensor(tg9, pi, ci, ALU.mult))
            link(pool.tensor_tensor(gm[:, 0], gm[:, 0], tg9, ALU.subtract))
            link(pool.tensor_tensor(gm[:, 1], pi, cr, ALU.mult))
            link(pool.tensor_tensor(tg9, pr, ci, ALU.mult))
            link(pool.tensor_tensor(gm[:, 1], gm[:, 1], tg9, ALU.add))
            pool.tensor_scalar(gm[:, 1], gm[:, 1], -1.0, None, ALU.mult).then_inc(g_made, 1)
            pool.wait_ge(pe_done, PLAN.done(("vt", 7)))
            pool.memset(vn_t[:], 0.0).then_inc(w_zero, 1)
            pool.wait_ge(pe_done, PLAN.done(("x", 4)))
            pool.wait_ge(par_ld, PARS)
            pool.tensor_tensor(uc, uc, d_b[:].unsqueeze(1).broadcast_to([NCH, CH, SSM_W]), ALU.mult).then_inc(ud_made, 1)
            pool.wait_ge(*emptied(("d", 5)))
            pool.wait_ge(*emptied(("h0",)))
            link(pool.tensor_scalar(walk[:, 0, 0], pw[:, CH, 0], 1.0, None, ALU.mult))
            link(pool.tensor_scalar(walk[:, 0, 1], pw[:, CH, 0], 1.0, None, ALU.mult))
            link(pool.tensor_scalar(walk[:, 1, 0], pw[:, CH, 1], -1.0, None, ALU.mult))
            link(pool.tensor_scalar(walk[:, 1, 1], pw[:, CH, 1], 1.0, None, ALU.mult))
            base = count[0]
            with pool.Fori(0, NPC - 1) as c:
                now, nxt = bass.ds(c, 1), bass.ds(c + 1, 1)

                def h(r, at):
                    return (hst[:, r, :, at] if r is not None else hst[:, :, :, at])
                pool.tensor_tensor(walk[:, 2].unsqueeze(3), walk[:, 0].unsqueeze(3), hst[:, :, :, now], ALU.mult)
                pool.tensor_tensor(walk[:, 3, 0].unsqueeze(2), walk[:, 1, 0].unsqueeze(2), hst[:, 1, :, now], ALU.mult)
                pool.tensor_tensor(walk[:, 3, 1].unsqueeze(2), walk[:, 1, 1].unsqueeze(2), hst[:, 0, :, now], ALU.mult
                                   ).then_inc(pool_step, 1)
                pool.wait_ge(pool_step, c * 3 + (base + 1))
                pool.tensor_tensor(walk[:, 2], walk[:, 2], walk[:, 3], ALU.add).then_inc(pool_step, 1)
                pool.wait_ge(pool_step, c * 3 + (base + 2))
                pool.tensor_tensor(hst[:, :, :, nxt], hst[:, :, :, nxt], walk[:, 2].unsqueeze(3), ALU.add
                                   ).then_inc(pool_step, 1)
                pool.wait_ge(pool_step, c * 3 + (base + 3))
            count[0] = base + 3 * (NPC - 1)
            nine = [P, 1 + NSEQ, NS]
            hv = [hst[:, r, :, NPC - 1:NCH].rearrange("p s c -> p c s") for r in range(2)]
            a8 = [pw[:, CH, r].unsqueeze(1).broadcast_to(nine) for r in range(2)]
            t9 = [tmp9[:, j] for j in range(2)]
            for r, (p0, p1, op) in enumerate(((0, 1, ALU.subtract), (1, 0, ALU.add))):
                pool.tensor_tensor(t9[0], hv[p0], a8[0], ALU.mult)
                link(pool.tensor_tensor(t9[1], hv[p1], a8[1], ALU.mult))
                link(pool.tensor_tensor(t9[0], t9[0], t9[1], op))
                link(pool.tensor_tensor(fin[:, r], fin[:, r], t9[0], ALU.add))
            pool.memset(walk[:, 0, 0, 0:1], 0.0).then_inc(walked, 1)

            pool.wait_ge(fin_out, 32)
            pool.wait_ge(glu_made, 8)
            pool.memset(w2[:], 0.0)
            pool.memset(w1_t[:], 0.0).then_inc(w1_zero, 1)
            link(pool.memset(cm01[:], 1.0))
            link(pool.affine_select(out=cm01[:], in_=cm01[:], compare_op=ALU.is_ge, fill=0.0, base=-(CL - 1),
                                    pattern=[[P, 4], [-CS, 32]], channel_multiplier=1))
            pool.tensor_scalar(cmneg[:], cm01[:], -NEG, NEG, ALU.mult, ALU.add)
            link(pool.memset(sel4[:], 1.0))
            link(pool.affine_select(out=sel4[:], in_=sel4[:], compare_op=ALU.is_ge, fill=0.0, base=0,
                                    pattern=[[-32, 4]], channel_multiplier=1))
            link(pool.affine_select(out=sel4[:], in_=sel4[:], compare_op=ALU.is_ge, fill=0.0, base=31,
                                    pattern=[[32, 4]], channel_multiplier=-1))
            link(pool.iota(rowi[:, 0:1], [[0, 1]], base=0, channel_multiplier=1))
            link(pool.iota(csneg[:, 0, :], [[1, 32]], base=0, channel_multiplier=0, allow_small_or_imprecise_dtypes=True))
            pool.iota(nmk[:, 0], [[-16, 4], [1, 64]], base=0, channel_multiplier=0,
                      allow_small_or_imprecise_dtypes=True).then_inc(masks, 1)
            pool.memset(vcbd[:], 0.0).then_inc(masks, 1)
            link(pool.memset(qpad[:], 0.0))
            pool.wait_ge(*emptied(("q", 3, 1)))
            for k in range(NKV):
                for par in range(2):
                    dstq = qpad[HD * k:HD * k + HD].rearrange("p (s two) n -> p s two n", two=2)[:, :, par,
                                64 * par + 32 * k:64 * par + 32 * k + 32].rearrange("p s (g q) -> p s g q", g=GQA)
                    srcq = qT[HD * k:HD * k + HD, :, NP_:ROWS].rearrange("p g (s two q) -> p s two g q", two=2, q=NDEC)[:, :, par]
                    pool.tensor_copy(dstq, srcq).then_inc(qpad_made, 1)
            for t in range(NT):
                pool.wait_ge(sq_done, NT + t + 1)
                rstd(t, 1)
                pool.wait_ge(hn_made, NT + t + 1)
                pool.dma_start(h2_dram[P * t:P * t + TILES[t], :], hn[0:TILES[t], t % 2]).then_inc(h2_out[t % 2], 16)
            pool.wait_ge(pos_made, 1)
            pool.wait_ge(list_zero, 16)
            for t in range(NT):
                for c in range(2):
                    pool.indirect_dma_start(
                        out=list_dram, out_offset=bass.IndirectOffsetOnAxis(pos_i[0:TILES[t], 0, c, t:t + 1], 0),
                        in_=tokid[0:TILES[t], t:t + 1], in_offset=None).then_inc(listed, 16)
            pool.memset(tick[:, 0:1], 0.0).then_inc(pool_tick, 1)

            def carry_waits(n):
                pool.wait_ge(pool_tick, n)
                pool.tensor_tensor(tick[:, 1:2], tick[:, 0:1], tick[:, 0:1], ALU.add).then_inc(pool_tick, 1)

            pool.wait_ge(rounds_made, 1)
            rounds = pool.value_load(rounds_i[0:1, 0:1], min_val=1, max_val=MAXR)
            pool.wait_ge(listed, 16 * 2 * NT)
            pool.wait_ge(h2_out[0], 16 * 3)
            pool.wait_ge(h2_out[1], 16 * 2)
            pool.wait_ge(pe_done, PLAN.done(("rt", NT - 1)))
            with pool.Fori(0, rounds) as j:
                with pool.Fori(0, NE // 2) as i:
                    for u in range(2):
                        pool.wait_ge(hg_free[u], j * 8 + i + 1)
                        pool.dma_start(idx[:, u:u + 1], list_dram[bass.ds(i * (2 * MAXR * CAP) + j * CAP + u * MAXR * CAP, CAP), :]
                                       ).then_inc(idx_ld[u], 16)
                        pool.wait_ge(idx_ld[u], j * 128 + i * 16 + 16)
                        carry_waits(j * (NE + NT) + i * 2 + (u + 1))
                        pool.indirect_dma_start(out=hg[:, u], out_offset=None, in_=h2_dram,
                                                in_offset=bass.IndirectOffsetOnAxis(idx[:, u:u + 1], 0)).then_inc(hg_ld[u], 16)
                pool.wait_ge(pos_made, j + 2)
                for u in range(2):
                    pool.wait_ge(ye_out[u], j * 128 + (128 + 16))
                for t in range(NT):
                    pool.wait_ge(x2_made, j * NT + (NT + max(t - 1, 0)))
                    carry_waits(j * (NE + NT) + (NE + t + 1))
                    for c in range(2):
                        pool.indirect_dma_start(out=yg[0:TILES[t], t % 2, c], out_offset=None, in_=ye_dram,
                                                in_offset=bass.IndirectOffsetOnAxis(pos_i[0:TILES[t], 1, c, t:t + 1], 0)
                                                ).then_inc(yg_ld[t % 2], 16)
            for t in range(NT):
                pool.wait_ge(sq_done, 2 * NT + t + 1)
                rstd(t, 2)

        @block.tensor
        def _(pe):
            def begin(key):
                if PLAN.at[key] >= RING:
                    pe.wait_ge(*freed(key))
                return bank(key)

            def finish(ins):
                ins.then_inc(pe_done, 1)

            def product(out, pairs):
                for n, (a, b) in enumerate(pairs):
                    ins = pe.matmul(out, a, b, start=(n == 0), stop=(n == len(pairs) - 1))
                return ins

            pe.wait_ge(consts, 1)
            for t in range(NT):
                p = TILES[t]
                pe.wait_ge(hn_made, t + 1)
                for k in range(2):
                    o = begin(("hT", t, k))
                    for j in range(4):
                        ins = pe.transpose(o[:, j * P:j * P + p], x_in[0:p, t, (4 * k + j) * P:(4 * k + j + 1) * P], ident[0:p, 0:p])
                    finish(ins)
            for t in range(NT):
                p = TILES[t]
                o = begin(("u", t))
                pe.wait_ge(*emptied(("hT", t, 1)))
                pe.wait_ge(*w_need["u"])
                finish(product(o[0:p, :], [(hT[:, k, P * t:P * t + p], wk("u", 512)[:, k]) for k in range(KD)]))
            for t in range(NT):
                p = TILES[t]
                for c in range(2):
                    o = begin(("kv", t, c))
                    pe.wait_ge(*w_need[f"kv{c}"])
                    finish(product(o[0:p, 0:396], [(hT[:, k, P * t:P * t + p], wk(f"kv{c}", 396)[:, k]) for k in range(KD)]))
            pe.wait_ge(par_ld, PARS)
            o = begin(("lam",))
            pe.transpose(o[:, 0:NS], lam_r[:, 0, :], ident[0:NS, 0:NS])
            finish(pe.transpose(o[:, NS:2 * NS], lam_r[:, 1, :], ident[0:NS, 0:NS]))
            for r in range(2):
                o = begin(("c", r))
                for b in range(4):
                    ins = pe.transpose(o[:, P * b:P * b + P], c_r[:, r, b].rearrange("p u n -> p (u n)"), ident[:])
                finish(ins)
            o = begin(("h0",))
            h0v = h0_r[:].rearrange("p (n r) -> p r n", r=2)
            for r in range(2):
                ins = pe.transpose(o[:, P * r:P * r + P], h0v[:, r], ident[:])
            finish(ins)
            def gate_products(m):
                w = wk(f"g{m // 2}", 2 * P, 0, 2 * KD)
                pe.wait_ge(*w_need[f"g{m // 2}"])
                for h in range(2):
                    for at, key in enumerate(("ga", "gb")):
                        o = begin((key, m, h))
                        finish(product(o[:, 0:HALF], [(w[:, KD * at + k, P * (m % 2):P * (m % 2) + P],
                                                       hT[:, k, HALF * h:HALF * h + HALF]) for k in range(KD)]))
            for m in range(KD_A):
                gate_products(m)
            pe.wait_ge(ucg_made, 1)
            for i in range(5):
                o = begin(("x", i))
                for j, g in enumerate(range(7 * i, min(7 * i + 7, NG))):
                    ins = pe.transpose(o[:, NCH * j:NCH * j + NCH], ucg[:, g], ident[0:NCH, 0:NCH])
                finish(ins)
            for i in range(8):
                o = begin(("vt", i))
                for j in range(4):
                    q = 4 * i + j
                    ins = pe.transpose(o[:, P * j:P * j + P], vn[:, q // 2, q % 2], ident[:])
                finish(ins)
            for i in range(8):
                o = begin(("k", i))
                for j in range(4):
                    s, lo = 4 * (i // 2) + j, 64 * (i % 2)
                    ins = product(o[0:GRP, P * j:P * j + P],
                                  [(bbar[lo:lo + 64, r, s], gm[lo:lo + 64, r, s, 0:CH]) for r in range(2)])
                finish(ins)
            pe.wait_ge(*emptied(("x", 4)))
            pe.wait_ge(*emptied(("vt", 7)))
            for i in range(6):
                o = begin(("d", i))
                for s in range(3 * i, min(3 * i + 3, NS)):
                    for r in range(2):
                        at = ((s - 3 * i) * 2 + r) * NCH
                        for g2 in range(2):
                            ins = pe.matmul(o[64 * g2:64 * g2 + 64, at:at + NCH], vt[:, 2 * s + r, 64 * g2:64 * g2 + 64],
                                            xg[:, 2 * s + g2], start=True, stop=True)
                finish(ins)
            pe.wait_ge(*w_need["q"])
            for m in range(GQA):
                wq = wk("q", 512)[:, :, P * m:P * m + P]
                for h in range(2):
                    o = begin(("q", m, h))
                    finish(product(o[:, 0:HALF], [(wq[:, k], hT[:, k, HALF * h:HALF * h + HALF]) for k in range(KD)]))
            for m in range(KD_A, KD):
                gate_products(m)
            pe.wait_ge(walked, 1)
            pe.wait_ge(w_toep, 16 * CH)
            for i in range(8):
                o = begin(("y", i))
                for j in range(4):
                    s, lo = 4 * (i // 2) + j, 64 * (i % 2)
                    g = 2 * s + i % 2
                    ins = product(o[0:NCH, P * j:P * j + P],
                                  [(xg[:, g], wt[:, g])]
                                  + [(hst[lo:lo + 64, r, s], gm[lo:lo + 64, r, s, 1:CH + 1]) for r in range(2)])
                finish(ins)
            o = begin(("fin",))
            for r in range(2):
                pe.transpose(o[:, P * r:P * r + P], fin[:, r, 1:1 + NSEQ], ident[:])
            for r in range(2):
                ins = pe.transpose(o[0:NS, 256 + P * r:256 + P * r + P], fin[:, r, 0], ident[:])
            finish(ins)
            pe.wait_ge(y_gelu, 8)
            for t in range(CH):
                o = begin(("zg", t))
                for b in range(4):
                    ins = pe.transpose(o[:, NCH * b:NCH * b + NCH], uc[:, t, P * b:P * b + P], ident[0:NCH, 0:NCH])
                finish(ins)
            pe.wait_ge(*emptied(("zg", CH - 1)))
            pe.wait_ge(*w_need["glu"])
            for m in range(4):
                for h in range(2):
                    o = begin(("glu", m, h))
                    finish(product(o[:, 0:HALF], [(wk("glu", 512, k=4)[:, k, P * m:P * m + P],
                                                   zgT[:, k, HALF * h:HALF * h + HALF]) for k in range(4)]))
            o = begin(("pe",))
            pe.wait_ge(pe_ld, 32)
            finish(pe.transpose(o[:, 0:2 * CL], pe_r[:].rearrange("p u n -> p (u n)"), ident[0:64, 0:64]))
            for i in range(10):
                o = begin(("ct", i))
                if i >= 2:
                    pe.wait_ge(raw_ld[(i - 2) % 4], 32 * ((i - 2) // 4 + 1))
                for u in range(2):
                    for k in range(2):
                        src = kv[:, 2 * i + u, P * k:P * k + P] if i < 2 else rawc[:, (i - 2) % 4, u, P * k:P * k + P]
                        ins = pe.transpose(o[:, (2 * u + k) * P:(2 * u + k + 1) * P], src, ident[:])
                finish(ins)
            pe.wait_ge(*emptied(("ct", 9)))
            pe.wait_ge(w1_ld, 16 * 6)
            for k in range(2):
                o = begin(("pre", k))
                finish(product(o[:, 0:NBLK], [(w1[:, k, i], kvct[:, k, i:i + CS * (NBLK - 1) + 1:CS]) for i in range(CL)]))
            o = begin(("kc",))
            pe.wait_ge(cmp_g, 1)
            finish(pe.matmul(o[:, 0:NBLK], w2[:, 0], cx[:, 0, 1], start=True, stop=True))
            o = begin(("vcp",))
            pe.wait_ge(cmp_g, 3)
            finish(pe.matmul(o[:, 0:P], cxr[:].rearrange("p g j -> p (g j)"), w2[:, 1],
                             start=True, stop=True))
            o = begin(("vcs",))
            for t in range(4):
                j = CJ_S + 2 * SJ * t
                if t < 3:
                    ins = pe.matmul(o[0:32, P * t:P * t + P], cx[:, 1, 1, j:j + 32], w2[:, 1], start=True, stop=True)
                else:
                    ins = pe.matmul(o[0:31, P * t:P * t + P], cx[:, 1, 1, j:j + 31], w2[:, 1], start=True, stop=True)
            finish(ins)
            for r in range(2):
                o = begin(("ktp", r))
                for t in range(4):
                    ins = pe.transpose(o[:, P * t:P * t + P], kv[:, t, KVW * (r + 1):KVW * (r + 1) + P], ident[:])
                finish(ins)
            o = begin(("ktn",))
            for r in range(2):
                ins = pe.transpose(o[:, 64 * r:64 * r + 64], kv[0:64, 4, KVW * (r + 1):KVW * (r + 1) + P], ident[0:64, 0:64])
            finish(ins)
            pe.wait_ge(cache_ld, 16 * 17)
            for r in range(2):
                for i in range(4):
                    o = begin(("kts", r, i))
                    for j in range(4):
                        ins = pe.transpose(o[:, P * j:P * j + P], caches[:, r, 2 * i + j // 2, j % 2, 0:P], ident[:])
                    finish(ins)

            pe.wait_ge(*emptied(("kts", 1, 3)))
            pe.wait_ge(consts, 2)
            pe.wait_ge(row_masks, 1)
            pe.wait_ge(qpad_made, 4)
            pe.wait_ge(*emptied(("vcs",)))
            for what, i in attention_steps():
                kind, b, r, h = ITEMS[i] if what in ("score", "turn", "value") else ITEMS[GROUPS[i][0]]
                kh, m = h // GQA, h % GQA
                lo = HD * kh
                if what == "score":
                    o = begin(("s", i))
                    if kind == "p":
                        n = P * (b + 1)
                        pe.matmul(o[:, 0:n], qT[lo:lo + HD, m, P * b:P * b + P], kt[lo:lo + HD, r - 1, 0:n], start=True, stop=False)
                        finish(pe.matmul(o[:, n - P:n], ident_b[:], causal[:], start=False, stop=True))
                    elif kind == "c":
                        for hh in range(NH):
                            if hh == GQA:
                                ins.then_inc(half_done, 1)
                                pe.wait_ge(half_done, b + 1)
                            l = HD * (hh // GQA)
                            ins = pe.matmul(o[:, 32 * hh:32 * hh + 32], qT[l:l + HD, hh % GQA, P * b:P * b + P],
                                            kc[l:l + HD, CJ_P:CJ_P + 32], start=True, stop=True)
                        finish(ins)
                    elif kind == "s":
                        product(o[:, 0:PAST], [(qpad[:, 2 * b + u], kts[:, r - 1, 2 * b + u]) for u in range(2)])
                        for u in range(2):
                            pe.matmul(o[:, PAST:PAST + 64], qpad[:, 2 * b + u], kt[:, r - 1, NP_:ROWS], start=(u == 0), stop=False)
                        finish(pe.matmul(o[:, PAST:PAST + 64], ident_b[:], new_mask[:, b], start=False, stop=True))
                    else:
                        j = CJ_S + 2 * SJ * b
                        n = min(32, NBLK - j)
                        finish(product(o[:, 0:n], [(qpad[:, 2 * b + u], kc[:, j:j + n]) for u in range(2)]))
                elif what == "turn":
                    o = begin(("t", i))
                    pe.wait_ge(*emptied(("s", i)))
                    if kind == "c":
                        pe.wait_ge(s_prob, b + 1)
                    at = 0
                    for c, n in enumerate(item_keys(ITEMS[i])):
                        ins = pe.transpose(o[0:n, P * c:P * c + P], pb[:, i % 3, at:at + n], ident[:])
                        at += n
                    finish(ins)
                elif what == "value":
                    g = GROUP_OF[i]
                    pe.wait_ge(*emptied(("t", i)))
                    if g >= 2 and i == GROUPS[g][0]:
                        pe.wait_ge(s_gath, g - 1)
                    o = ps[:, RING + g % 2, :]
                    vcol = KVW * r + P
                    q = pt[:, i % 2]
                    if kind == "p":
                        ins = product(o[:, HD * h:HD * h + HD],
                                      [(q[:, P * c:P * c + P], kv[:, c, vcol + lo:vcol + lo + HD]) for c in range(b + 1)])
                    elif kind == "c":
                        for k in range(NKV):
                            ins = pe.matmul(o[:, 256 * k:256 * k + 256], q[:, P * k:P * k + P], vcbd[:, k], start=True, stop=True)
                    elif kind == "s":
                        ins = product(o[:, 0:256].rearrange("p (a n) -> p a n", a=2),
                                      [(q[:, P * c:P * c + P], caches[:, r - 1, 2 * b:2 * b + 2, c, P:KVW]) for c in range(2)]
                                      + [(q[0:64, 256:384], kv[0:64, 4, vcol:vcol + P].unsqueeze(1).broadcast_to([64, 2, P]))])
                    else:
                        ins = pe.matmul(o[:, 0:256].rearrange("p (a n) -> p a n", a=2), q[0:32, 0:P],
                                        vcs[0:32, b].unsqueeze(1).broadcast_to([32, 2, P]), start=True, stop=True)
                    ins.then_inc(s_val, 1)
                elif what == "out":
                    o = begin(("o", i))
                    if b < 4 and kind == "p":
                        pe.wait_ge(s_gath, i + 1)
                        pe.wait_ge(osd_made, b + 1)
                        for k in range(4):
                            ins = pe.transpose(o[:, P * k:P * k + P], ob[:, b % 2, P * k:P * k + P], ident[:])
                    else:
                        pe.wait_ge(osd_made, 4 + b + 1)
                        ins = pe.transpose(o[:, 0:P], osd[:, b % 2], ident[:])
                    finish(ins)

            pe.wait_ge(*emptied(("o", len(GROUPS) - 1)))
            pe.wait_ge(glu_made, 8)
            for m in range(KD):
                for h in range(2):
                    cut = slice(HALF * h, HALF * h + HALF)
                    for key, w, src in (("ab", "so", gluT), ("bb", "no", onsaT)):
                        o = begin((key, m, h))
                        pe.wait_ge(*w_need[w])
                        finish(product(o[:, 0:HALF], [(wk(w, D, 0, 4)[:, j, P * m:P * m + P], src[:, j, cut]) for j in range(4)]))
            pe.wait_ge(merged_made, 2 * KD)
            for c in range(2):
                for t in range(NT):
                    p = TILES[t]
                    o = begin(("wo", t, c))
                    pe.wait_ge(*w_need[f"wo{c}"])
                    finish(product(o[0:p, :], [(merged[:, k, P * t:P * t + p], wk(f"wo{c}", 512)[:, k]) for k in range(KD)]))
            pe.wait_ge(rt_ld, 64)
            for t in range(NT):
                p = TILES[t]
                pe.wait_ge(hn_made, NT + t + 1)
                for k in range(2):
                    o = begin(("h2T", t, k))
                    for j in range(4):
                        ins = pe.transpose(o[:, j * P:j * P + p], hn[0:p, t % 2, (4 * k + j) * P:(4 * k + j + 1) * P], ident[0:p, 0:p])
                    finish(ins)
                o = begin(("rt", t))
                pe.wait_ge(*emptied(("h2T", t, 1)))
                ins = product(o[0:p, 0:20], [(hT[:, k, P * t:P * t + p], w_rt[:, k]) for k in range(KD)])
                finish(ins)
            pe.wait_ge(p_ld, 32)
            for t in range(NT):
                p = TILES[t]
                o = begin(("pT", t))
                for j in range(2):
                    ins = pe.transpose(o[:, P * j:P * j + p], p_in[0:p, t, P * j:P * j + P], ident[0:p, 0:p])
                finish(ins)

            pe.wait_ge(consts, 3)
            pe.wait_ge(msk_made, 1)
            o = begin(("rank",))
            for t in range(NT):
                p = TILES[t]
                product(o[0:p, NE * t:NE * t + NE],
                        [(ones_b[:, 0:p], msk_b[:, q]) for q in range(t)] + [(tri_b[0:p, 0:p], msk_b[0:p, t])])
            finish(product(o[:, NE * NT:NE * NT + NE],
                           [(ones_b[0:TILES[q], :], msk_b[0:TILES[q], q]) for q in range(NT)]))
            pe.wait_ge(*emptied(("pT", NT - 1)))
            pe.wait_ge(*emptied(("rank",)))

            def turn_rows(j, n, u, half):
                pe.wait_ge(hg_ld[u], j * 128 + half * 16 + 16)
                pe.wait_ge(hgt_made, j * 32 + n * 2 + 2)
                for b in range(2):
                    for k in range(4):
                        ins = pe.transpose(ps[:, b, P * k:P * k + P], hg[:, u, (4 * b + k) * P:(4 * b + k + 1) * P], ident[:])
                    ins.then_inc(t_done, 1)
                pe.wait_ge(t_done, j * 32 + n * 2 + 2)
                pe.sem_inc(hg_free[u], 1)

            def gate_up(j, n, u, half):
                pe.wait_ge(gu_ld[u], j * 256 + half * 32 + 32)
                pe.wait_ge(hgt_made, j * 32 + n * 2 + 4)
                for w in range(2):
                    ins = product(ps[:, 2 + u, FF * w:FF * w + FF], [(hgT[:, u, k], wgu[:, u, w, k]) for k in range(KD)])
                ins.then_inc(g_done, 1)

            def turn_act(j, n, u):
                pe.wait_ge(act_made, j * 16 + n + 1)
                for f in range(2):
                    ins = pe.transpose(ps[:, 6 + u, P * f:P * f + P], si[:, u, P * f:P * f + P], ident[:])
                ins.then_inc(ta_done, 1)

            def down(j, n, u, half):
                pe.wait_ge(wd_ld[u], j * 128 + half * 16 + 16)
                pe.wait_ge(actt_made, j * 16 + n + 1)
                pe.wait_ge(d_taken, j * 32 + n * 2 + 2)
                for c in range(2):
                    ins = product(ps[:, 4 + c, :], [(actT[:, u, f], wdn[:, u, f, 512 * c:512 * c + 512]) for f in range(2)])
                    ins.then_inc(d_done, 1)

            pe.wait_ge(rounds_made, 1)
            rounds = pe.value_load(rounds_i[0:1, 0:1], min_val=1, max_val=MAXR)
            with pe.Fori(0, rounds) as j:
                turn_rows(j, 0, 0, 0)
                gate_up(j, 0, 0, 0)
                turn_rows(j, 1, 1, 0)
                turn_act(j, 0, 0)
                with pe.Fori(0, NE // 2 - 1) as i:
                    gate_up(j, i * 2 + 1, 1, i)
                    turn_rows(j, i * 2 + 2, 0, i + 1)
                    down(j, i * 2, 0, i)
                    turn_act(j, i * 2 + 1, 1)
                    gate_up(j, i * 2 + 2, 0, i + 1)
                    turn_rows(j, i * 2 + 3, 1, i + 1)
                    down(j, i * 2 + 1, 1, i)
                    turn_act(j, i * 2 + 2, 0)
                gate_up(j, NE - 1, 1, NE // 2 - 1)
                down(j, NE - 2, 0, NE // 2 - 1)
                turn_act(j, NE - 1, 1)
                down(j, NE - 1, 1, NE // 2 - 1)
            pe.wait_ge(d_taken, rounds * 32 + 2)

            for t in range(NT):
                p = TILES[t]
                if t < NT - 1:
                    pe.wait_ge(x2_made, rounds * NT + (t + 1))
                for k in range(2):
                    o = begin(("x2T", t, k))
                    for j in range(4):
                        ins = pe.transpose(o[:, j * P:j * P + p], x[0:p, t, (4 * k + j) * P:(4 * k + j + 1) * P], ident[0:p, 0:p])
                    finish(ins)
                for c in range(2):
                    o = begin(("pg", t, c))
                    pe.wait_ge(*w_need[f"pg{c}"])
                    pe.wait_ge(*emptied(("x2T", t, 0)))
                    pe.wait_ge(*emptied(("x2T", t, 1)))
                    finish(product(o[0:p, :], [(hT[:, k, P * t:P * t + p], wk(f"pg{c}", 512)[:, k]) for k in range(KD)]))
                    o = begin(("pp", t, c))
                    if (t, c) == (NT - 2, 1):
                        pe.wait_ge(x2_made, rounds * NT + NT)
                    pe.wait_ge(*w_need["ple"])
                    finish(product(o[0:p, :], [(pT[:, k, P * t:P * t + p], wk("ple", D, 0, 2)[:, k, 512 * c:512 * c + 512]) for k in range(2)]))

        def turn(eng, i, copy, take, empty):
            kind, b = ITEMS[i][0], ITEMS[i][1]
            o = take(("t", i))
            if i >= 2:
                eng.wait_ge(s_val, i - 1)
            q = pt[:, i % 2]
            if kind == "s":
                copy(q[:, 0:256], o[:, 0:256])
                empty(copy(q[0:64, 256:384], o[0:64, 256:384]))
            elif kind == "sc":
                empty(copy(q[0:32, 0:P], o[0:32, 0:P]))
            else:
                n = P * len(item_keys(ITEMS[i]))
                empty(copy(q[:, 0:n], o[:, 0:n]))

        def turned_norm(dve, t, key, which, take, empty):
            p = TILES[t]
            for k in range(2):
                o = take(key + (k,))
                empty(dve.tensor_tensor(hT[:, 4 * k:4 * k + 4, P * t:P * t + p], o.rearrange("p (k n) -> p k n", k=4)[:, :, 0:p],
                                        g_cols[:, which, 4 * k:4 * k + 4].unsqueeze(2).broadcast_to([P, 4, p]), ALU.mult))

        def router_logits(dve, t, take, empty):
            p = TILES[t]
            o = take(("rt", t))
            empty(dve.tensor_tensor(lg[0:p, t], o[0:p, 0:20], b_rt[0:p], ALU.add))

        @block.scalar
        def _(act):
            def col(ap, n):
                return ap.rearrange("(k p) -> p k", p=P)

            act.dma_start(ldt[0:64, :], I["ssm_log_dt"].rearrange("o (s g) -> o g s", g=2)[:, 0].broadcast_to([64, NS]),
                          allow_slow_non_contiguous=True).then_inc(par_ld, 16)
            act.dma_start(ldt[64:P, :], I["ssm_log_dt"].rearrange("o (s g) -> o g s", g=2)[:, 1].broadcast_to([64, NS]),
                          allow_slow_non_contiguous=True).then_inc(par_ld, 16)
            for r, name in enumerate(("ssm_lam_re", "ssm_lam_im")):
                act.dma_start(lam_r[:, r, :], I[name][0].rearrange("(s g) n -> s (g n)", g=2)).then_inc(par_ld, 16)
            for r, name in enumerate(("ssm_b_re", "ssm_b_im")):
                act.dma_start(b_r[:, r], I[name][0].rearrange("(s g) n c -> (g n) s c", g=2)).then_inc(par_ld, 16)
            for r, name in enumerate(("ssm_c_re", "ssm_c_im")):
                for u in range(2):
                    act.dma_start(c_r[:, r, :, u], I[name][0].rearrange("(b g) c n -> (g c) b n", b=4)).then_inc(par_ld, 16)
            act.dma_start(h0_r[:], I["state_ssm"][0].rearrange("q (s g) n r -> (q s) (g n r)", g=2)).then_inc(par_ld, 16)
            act.dma_start(d_b[:], I["ssm_d"].broadcast_to([NCH, SSM_W])).then_inc(par_ld, 16)
            act.dma_start(b_glu[:], col(I["b_glu"][0], 4), allow_slow_non_contiguous=True).then_inc(par_ld, 16)
            act.dma_start(g_cols[:, 0], col(I["norm1_g"][0], KD), allow_slow_non_contiguous=True).then_inc(gains_ld, 16)
            act.dma_start(g_cols[:, 1], col(I["norm2_g"][0], KD), allow_slow_non_contiguous=True).then_inc(gains_ld, 16)
            act.dma_start(ptab[:], I["page_table"].rearrange("(o s) u -> o (s u)", o=1)).then_inc(pt_ld, 16)

            def take(key):
                act.wait_ge(pe_done, PLAN.done(key))
                return bank(key)

            def empty(ins):
                ins.then_inc(drained["act"], 1)

            def copy(key, dst, src):
                empty(act.activation(dst, src, ACT.Copy))

            junk = flat(gluT)
            for t in range(NT):
                act.wait_ge(x_ld[t], 16)
                p = TILES[t]
                act.activation(junk[0:p, 0:D], x_in[0:p, t], ACT.Square, accum_out=stat[0:p, 0, t:t + 1]).then_inc(sq_done, 1)
                act.wait_ge(sq_done, t + 1)
            for t in range(NT):
                o = take(("u", t))
                p = TILES[t]
                copy(None, u_rows[0:p, t], o[0:p, :])
            for t in range(NT):
                p = TILES[t]
                for c in range(2):
                    o = take(("kv", t, c))
                    copy(None, kv[0:p, t, 396 * c:396 * c + 396], o[0:p, 0:396])
            act.wait_ge(par_ld, PARS)
            act.activation(sm[:, 2], ldt[:], ACT.Exp).then_inc(dt_done, 1)
            act.wait_ge(drained["act"], PLAN.by[("kv", NT - 1, 1)][1])
            for t in range(NT):
                p = TILES[t]
                act.activation(tgate[0:p, t], kv[0:p, t, 3 * KVW:], ACT.Tanh, scale=0.5).then_inc(gates_made, 1)
            act.wait_ge(angles, 1)
            act.activation(sm[:, 8], sm[:, 3], ACT.Exp)
            act.activation(sm[:, 9], sm[:, 6], ACT.Sin)
            act.activation(sm[:, 10], sm[:, 7], ACT.Sin).then_inc(trig, 1)

            def take_gates(m, stage):
                for h in range(2):
                    n = 2 * m + h
                    if gates_out(n % 4, n):
                        act.wait_ge(tg_out[n % 4], 16 * gates_out(n % 4, n))
                    for w, key in enumerate(("ga", "gb")):
                        o = take((key, m, h))
                        empty(act.activation(stage[:, n % 4, w], o[:, 0:HALF], ACT.Tanh, scale=0.5))
                    act.wait_ge(*emptied(("gb", m, h)))
                    act.dma_start(tg_dram[m][:, :, HALF * h:HALF * h + HALF], stage[:, n % 4]).then_inc(tg_out[n % 4], 16)
            act.wait_ge(u_out, 16 * NT)
            for m in range(KD_A):
                take_gates(m, stage_a)
            for i in range(8):
                o = take(("vt", i))
                copy(None, vt[:, 4 * i:4 * i + 4].rearrange("p a b -> p (a b)"), o)
            for i in range(8):
                o = take(("k", i))
                if i >= 2:
                    act.wait_ge(k_out[i % 2], 16 * (i // 2))
                copy(None, ks[:, i % 2].rearrange("p g n -> p (g n)"), o[0:GRP, :])
            act.wait_ge(*emptied(("h0",)))
            for i in range(6):
                o = take(("d", i))
                s0, s1 = 3 * i, min(3 * i + 3, NS)
                n = s1 - s0
                v = o[:, 0:n * 2 * NCH].rearrange("p (s r c) -> p r s c", s=n, r=2)
                for r in range(2):
                    act.activation(hst[:, r, s0:s1, 1:NPC], v[:, r, :, 0:NPC - 1], ACT.Copy)
                    ins = act.activation(fin[:, r, :, s0:s1].rearrange("p c s -> p s c"), v[:, r, :, NPC - 1:NCH], ACT.Copy)
                empty(ins)
            for m in range(GQA):
                for h in range(2):
                    o = take(("q", m, h))
                    empty(act.activation(qT[:, m, HALF * h:HALF * h + HALF], o[:, 0:HALF], ACT.Copy, scale=SCALE))
            act.wait_ge(pe_done, PLAN.done(("x", 4)))
            for m in range(KD_A, KD):
                take_gates(m, stage_b)
            for i in range(8):
                act.wait_ge(*emptied(("y", i)))
                v = uc.rearrange("p t (b j g c) -> p t b g j c", b=4, j=4, g=2)[:, :, i // 2, i % 2]
                act.activation(v, v, GELU).then_inc(y_gelu, 1)
            o = take(("fin",))
            act.activation(fo.rearrange("p n r -> p r n"), o[:, 0:2 * P].rearrange("p (r n) -> p r n", r=2), ACT.Copy)
            copy(None, fo_p[:].rearrange("p n r -> p r n"), o[0:NS, 2 * P:4 * P].rearrange("p (r n) -> p r n", r=2))
            act.wait_ge(bglu_half, 1)
            for b in range(4):
                act.wait_ge(tg_out[b], 16 * gates_out(b, 2 * KD))
            for m in range(4):
                for h in range(2):
                    o = take(("glu", m, h))
                    empty(act.activation(gluT[:, m, HALF * h:HALF * h + HALF], o[:, 0:HALF], ACT.Tanh,
                                         bias=stat[:, 3, m:m + 1], scale=0.5))
            act.wait_ge(glu_made, 8)
            act.wait_ge(fin_out, 32)
            o = take(("pe",))
            copy(None, kvct[:, :, 0:CL], o[:, 0:2 * CL].rearrange("p (k i) -> p k i", k=2))
            for i in range(10):
                o = take(("ct", i))
                at = CT0 + 2 * P * i
                copy(None, kvct[:, :, at:at + 2 * P].rearrange("p k (u n) -> p u k n", u=2), o.rearrange("p (u k n) -> p u k n", u=2, k=2))
            for k in range(2):
                act.wait_ge(*emptied(("pre", k)))
                act.activation(cx[:, k, 1], cx[:, k, 0], GELU).then_inc(cmp_g, 1)
            act.activation(cxr[:], cx[:, 1, 0, CJ_P:CJ_P + 32].unsqueeze(1).broadcast_to([P, 4, 32]), GELU).then_inc(cmp_g, 1)
            for r in range(2):
                o = take(("ktp", r))
                copy(None, kt[:, r, 0:NP_], o)
            o = take(("ktn",))
            copy(None, kt[:, :, NP_:ROWS], o[:, 0:P].rearrange("p (r n) -> p r n", r=2))
            for r in range(2):
                for i in range(4):
                    o = take(("kts", r, i))
                    copy(None, kts[:, r, 2 * i:2 * i + 2].rearrange("p s n -> p (s n)"), o)
            for what, i in attention_steps():
                if what == "score":
                    kind = ITEMS[i][0]
                    o = take(("s", i))
                    n = sum(item_keys(ITEMS[i]))
                    if i >= 3:
                        act.wait_ge(pe_done, PLAN.done(("t", i - 3)))
                    act.wait_ge(s_max, i + 1)
                    if kind == "c":
                        empty(act.activation(pb[:, i % 3, 0:n], sct[:, 0:n], ACT.Exp))
                    elif kind == "sc":
                        empty(act.activation(pb[:, i % 3, 0:n], sct[:, 0:n], ACT.Exp, bias=nm[:, i:i + 1], accum_out=rs[:, i:i + 1]))
                    else:
                        empty(act.activation(pb[:, i % 3, 0:n], o[:, 0:n], ACT.Exp, bias=nm[:, i:i + 1], accum_out=rs[:, i:i + 1]))
                elif what == "turn" and i % 2 == 0:
                    turn(act, i, lambda d, s: act.activation(d, s, ACT.Copy), take, empty)
            for t in range(NT):
                p = TILES[t]
                act.wait_ge(*emptied(("wo", t, 1)))
                if t == 0:
                    act.wait_ge(pe_done, PLAN.done(("bb", KD - 1, 1)))
                act.activation(junk[0:p, 0:D], x[0:p, t], ACT.Square, accum_out=stat[0:p, 0, t:t + 1]).then_inc(sq_done, 1)
                act.wait_ge(sq_done, NT + t + 1)
            act.wait_ge(lg_made, 1)
            act.activation(r16[:, :, 0:5], r16[:, :, 0:5], ACT.Exp).then_inc(lg_exp, 1)
            for t in range(NT):
                p = TILES[t]
                o = take(("pT", t))
                copy(None, pT[:, :, P * t:P * t + p], o[:, 0:2 * P].rearrange("p (k n) -> p k n", k=2)[:, :, 0:p])

            act.wait_ge(rounds_made, 1)
            rounds = act.value_load(rounds_i[0:1, 0:1], min_val=1, max_val=MAXR)
            act.wait_ge(pe_done, PLAN.done(("bb", KD - 1, 1)))
            for u in range(2):
                act.sem_inc(ye_out[u], 16)
            act.sem_inc(d_taken, 2)

            def tanh(j, n, u):
                act.wait_ge(g_done, j * 16 + n + 1)
                act.activation(th[:, u], ps[:, 2 + u, 0:FF], ACT.Tanh, scale=0.5).then_inc(th_made, 1)

            def take_act(j, n, u):
                act.wait_ge(ta_done, j * 16 + n + 1)
                act.activation(actT[:, u].rearrange("p f n -> p (f n)"), ps[:, 6 + u, 0:2 * P], ACT.Copy).then_inc(actt_made, 1)

            def take_down(j, n, u, half):
                act.wait_ge(ye_out[u], j * 128 + half * 16 + 16)
                for c in range(2):
                    act.wait_ge(d_done, j * 32 + n * 2 + (c + 1))
                    act.activation(ysb[:, u, 512 * c:512 * c + 512], ps[:, 4 + c, :], ACT.Copy).then_inc(d_taken, 1)
                act.wait_ge(d_taken, j * 32 + n * 2 + 4)
                act.dma_start(ye_dram[bass.ds(n * CAP, CAP), :], ysb[:, u]).then_inc(ye_out[u], 16)

            with act.Fori(0, rounds) as j:
                act.wait_ge(x2_made, j * NT + NT)
                tanh(j, 0, 0)
                take_act(j, 0, 0)
                with act.Fori(0, NE // 2 - 1) as i:
                    tanh(j, i * 2 + 1, 1)
                    take_down(j, i * 2, 0, i)
                    take_act(j, i * 2 + 1, 1)
                    tanh(j, i * 2 + 2, 0)
                    take_down(j, i * 2 + 1, 1, i)
                    take_act(j, i * 2 + 2, 0)
                tanh(j, NE - 1, 1)
                take_down(j, NE - 2, 0, NE // 2 - 1)
                take_act(j, NE - 1, 1)
                take_down(j, NE - 1, 1, NE // 2 - 1)
            for t in range(NT):
                p = TILES[t]
                o = take(("x2T", t, 0))
                copy(None, hT[:, 0:4, P * t:P * t + p], o.rearrange("p (k n) -> p k n", k=4)[:, :, 0:p])
                for c in range(2):
                    o = take(("pg", t, c))
                    if 2 * t + c >= 2:
                        act.wait_ge(x3_made, 2 * t + c - 1)
                    empty(act.activation(tpg[0:p, c], o[0:p, :], ACT.Tanh, scale=0.5))
            for t in range(NT):
                p = TILES[t]
                act.wait_ge(x3_made, 2 * t + 2)
                act.activation(junk[0:p, 0:D], x[0:p, t], ACT.Square, accum_out=stat[0:p, 0, t:t + 1]).then_inc(sq_done, 1)
                act.wait_ge(sq_done, 2 * NT + t + 1)

        @block.vector
        def _(dve):
            count = [0]

            def link(ins):
                count[0] += 1
                ins.then_inc(dve_step, 1)
                dve.wait_ge(dve_step, count[0])

            def tt(out, a, b, op):
                return dve.tensor_tensor(out, a, b, op)

            def take(key):
                dve.wait_ge(pe_done, PLAN.done(key))
                return bank(key)

            def empty(ins):
                ins.then_inc(drained["dve"], 1)

            dve.wait_ge(gains_ld, 32)
            for t in range(NT):
                p = TILES[t]
                dve.wait_ge(rstd_done, t + 1)
                dve.tensor_scalar(x_in[0:p, t], x_in[0:p, t], stat[0:p, 2, t:t + 1], None, ALU.mult).then_inc(hn_made, 1)
            for t in range(NT):
                turned_norm(dve, t, ("hT", t), 0, take, empty)
            dve.wait_ge(pe_done, PLAN.done(("hT", NT - 1, 1)))
            link(dve.memset(stat[:, 3, 0:4], 0.0))
            dve.wait_ge(par_ld, PARS)
            dve.tensor_scalar(stat[:, 3, 0:4], b_glu[:], 0.5, None, ALU.mult).then_inc(bglu_half, 1)
            o = take(("lam",))
            empty(dve.tensor_copy(sm[:, 0:2], o[:, 0:2 * NS].rearrange("p (r s) -> p r s", r=2)))
            lr, li, dt, er, an, kk, ra, rb, mg, sn, cs, den, t0, t1, cr, ci, a1 = (sm[:, j] for j in range(17))
            dve.wait_ge(*emptied(("lam",)))
            dve.wait_ge(dt_done, 1)
            two_pi = 2.0 * math.pi
            hi = 6.28125
            magic = 1.5 * 2.0 ** 23
            tt(er, lr, dt, ALU.mult)
            link(tt(an, li, dt, ALU.mult))
            link(dve.tensor_scalar(kk, an, 1.0 / two_pi, magic, ALU.mult, ALU.add))
            link(dve.tensor_scalar(kk, kk, -magic, None, ALU.add))
            link(dve.scalar_tensor_tensor(ra, kk, -hi, an, ALU.mult, ALU.add))
            link(dve.scalar_tensor_tensor(ra, kk, -(two_pi - hi), ra, ALU.mult, ALU.add))
            link(dve.tensor_scalar(t0, ra, math.pi / 2, -two_pi, ALU.is_gt, ALU.mult))
            link(dve.scalar_tensor_tensor(rb, ra, math.pi / 2, t0, ALU.add, ALU.add))
            link(dve.tensor_scalar(ra, ra, 3.1415925, -3.1415925, ALU.min, ALU.max))
            dve.tensor_scalar(rb, rb, 3.1415925, -3.1415925, ALU.min, ALU.max).then_inc(angles, 1)
            for r in range(2):
                o = take(("c", r))
                v = o.rearrange("p (s g c) -> p s g c", g=2, c=GRP)
                dve.tensor_copy(cst[0:64, r], v[0:64, :, 0])
                empty(dve.tensor_copy(cst[64:P, r], v[64:P, :, 1]))
            o = take(("h0",))
            dve.memset(hst[:, :, :, 0:1], 0.0)
            empty(dve.tensor_copy(hst[:, :, :, NPC:NCH].rearrange("p r s q -> p r q s"),
                                  o[:, 0:2 * P].rearrange("p (r q s) -> p r q s", r=2, q=NSEQ)))
            dve.wait_ge(trig, 1)
            dve.memset(pw[:, 0, 0], 1.0)
            dve.memset(pw[:, 0, 1], 0.0)
            tt(pw[:, 1, 0], mg, cs, ALU.mult)
            link(tt(pw[:, 1, 1], mg, sn, ALU.mult))
            for m in (1, 2, 4):
                a_r, a_i = pw[:, 1:m + 1, 0], pw[:, 1:m + 1, 1]
                b_re = pw[:, m:m + 1, 0].broadcast_to([P, m, NS])
                b_im = pw[:, m:m + 1, 1].broadcast_to([P, m, NS])
                u0 = tmp_v[:, 0:m * NS].rearrange("p (m s) -> p m s", m=m)
                u1 = tmp_v[:, 64:64 + m * NS].rearrange("p (m s) -> p m s", m=m)
                tt(u0, a_i, b_im, ALU.mult)
                tt(u1, a_i, b_re, ALU.mult)
                tt(pw[:, m + 1:2 * m + 1, 0], a_r, b_re, ALU.mult)
                link(tt(pw[:, m + 1:2 * m + 1, 1], a_r, b_im, ALU.mult))
                tt(pw[:, m + 1:2 * m + 1, 0], pw[:, m + 1:2 * m + 1, 0], u0, ALU.subtract)
                link(tt(pw[:, m + 1:2 * m + 1, 1], pw[:, m + 1:2 * m + 1, 1], u1, ALU.add))
            dve.tensor_copy(pwr[:, 0], pw[:, CH - 1]).then_inc(powers, 1)
            for j in range(1, CH):
                dve.tensor_copy(pwr[:, j], pw[:, CH - 1 - j])
            link(dve.tensor_scalar(a1, pw[:, 1, 0], -1.0, None, ALU.add))
            tt(t0, lr, lr, ALU.mult)
            link(tt(t1, li, li, ALU.mult))
            link(tt(den, t0, t1, ALU.add))
            link(dve.reciprocal(den, den))
            tt(t0, a1, lr, ALU.mult)
            link(tt(t1, pw[:, 1, 1], li, ALU.mult))
            link(tt(t0, t0, t1, ALU.add))
            link(tt(cr, t0, den, ALU.mult))
            tt(t0, pw[:, 1, 1], lr, ALU.mult)
            link(tt(t1, a1, li, ALU.mult))
            link(tt(t0, t0, t1, ALU.subtract))
            link(tt(ci, t0, den, ALU.mult))
            sc = [P, NS, GRP]
            crb, cib = cr.unsqueeze(2).broadcast_to(sc), ci.unsqueeze(2).broadcast_to(sc)
            u0 = tmp_v[:, 0:NS * GRP].rearrange("p (s c) -> p s c", s=NS)
            tt(bbar[:, 0], b_r[:, 0], crb, ALU.mult)
            link(tt(u0, b_r[:, 1], cib, ALU.mult))
            tt(bbar[:, 0], bbar[:, 0], u0, ALU.subtract)
            link(tt(bbar[:, 1], b_r[:, 1], crb, ALU.mult))
            link(tt(u0, b_r[:, 0], cib, ALU.mult))
            link(tt(bbar[:, 1], bbar[:, 1], u0, ALU.add))
            n8 = [P, NS, CH, GRP]
            u8 = tmp_v[:, 0:NS * CH * GRP].rearrange("p (s t c) -> p s t c", s=NS, t=CH)
            qr, qi = (pwr[:, :, r].rearrange("p t s -> p s t").unsqueeze(3).broadcast_to(n8) for r in range(2))
            br8, bi8 = (bbar[:, r].unsqueeze(2).broadcast_to(n8) for r in range(2))
            v8 = [vn[:, :, r].rearrange("p s (t c) -> p s t c", t=CH) for r in range(2)]
            tt(v8[0], qr, br8, ALU.mult)
            link(tt(u8, qi, bi8, ALU.mult))
            link(tt(v8[0], v8[0], u8, ALU.subtract))
            tt(v8[1], qr, bi8, ALU.mult)
            link(tt(u8, qi, br8, ALU.mult))
            tt(v8[1], v8[1], u8, ALU.add).then_inc(v_made, 1)
            dve.wait_ge(gates_made, NT)
            dve.tensor_scalar(tgate[:, 0:4], tgate[:, 0:4], 1.0, None, ALU.add).then_inc(gates_made, 1)
            dve.tensor_scalar(tgate[0:64, 4], tgate[0:64, 4], 1.0, None, ALU.add).then_inc(gates_made, 1)
            dve.wait_ge(uc_ld, 16)
            dve.tensor_copy(ucg.rearrange("p g (t c) -> p g t c", t=CH), uc.rearrange("p t (g c) -> p g t c", g=NG)
                            ).then_inc(ucg_made, 1)
            for b in range(4):
                dve.wait_ge(tg_out[b], 16 * gates_out(b, 2 * KD_A))
            for i in range(5):
                o = take(("x", i))
                n = min(7, NG - 7 * i)
                empty(dve.tensor_copy(xg[:, 7 * i:7 * i + n].rearrange("p g n -> p (g n)"), o[:, 0:n * NCH]))
            dve.wait_ge(ud_made, 1)
            for i in range(8):
                o = take(("y", i))
                v = uc.rearrange("p t (b j g c) -> p t b g j c", b=4, j=4, g=2)[:, :, i // 2, i % 2]
                empty(tt(v, o[0:NCH, :].rearrange("p (g t c) -> p t g c", g=4, t=CH), v, ALU.add))
            for t in range(CH):
                o = take(("zg", t))
                empty(dve.tensor_copy(zgT.rearrange("p k (c t) -> p k c t", t=CH)[:, :, :, t],
                                      o[:, 0:4 * NCH].rearrange("p (k c) -> p k c", k=4)))
            dve.wait_ge(*emptied(("zg", CH - 1)))
            for m in range(4):
                for h in range(2):
                    cut = slice(HALF * h, HALF * h + HALF)
                    dve.wait_ge(*emptied(("glu", m, h)))
                    dve.scalar_tensor_tensor(gluT[:, m, cut], gluT[:, m, cut], 1.0, zgT[:, m, cut], ALU.add, ALU.mult
                                             ).then_inc(glu_made, 1)
            dve.wait_ge(glu_made, 8)
            dve.wait_ge(fin_out, 32)
            dve.wait_ge(masks, 1)
            link(dve.tensor_scalar(rowi[:, 1:2], rowi[:, 0:1], 7, None, ALU.bitwise_and))
            link(dve.tensor_scalar(rowi[:, 2:3], rowi[:, 0:1], 6, None, ALU.logical_shift_right))
            dve.tensor_copy(rowf[:, 0:1], rowi[:, 1:2])
            link(dve.tensor_copy(rowf[:, 1:2], rowi[:, 2:3]))
            dve.tensor_scalar(rowf[:, 2:3], rowf[:, 1:2], 8.0, None, ALU.mult)
            link(dve.tensor_scalar(rowf[:, 3:4], rowf[:, 1:2], 16.0, None, ALU.mult))
            link(dve.scalar_tensor_tensor(rowf[:, 0:1], rowf[:, 1:2], 8.0, rowf[:, 0:1], ALU.mult, ALU.add))
            dve.tensor_scalar(nmk[:, 1], nmk[:, 0], rowf[:, 2:3], NEG, ALU.is_lt, ALU.mult)
            link(dve.tensor_scalar(nmk[:, 2], nmk[:, 0], rowf[:, 0:1], NEG, ALU.is_gt, ALU.mult))
            tt(new_mask[:], nmk[:, 1], nmk[:, 2], ALU.add).then_inc(row_masks, 1)
            dve.tensor_scalar(csneg[:, 1], csneg[:, 0], rowf[:, 3:4], NEG, ALU.is_lt, ALU.mult)
            link(dve.tensor_scalar(csneg[:, 0], csneg[:, 0], rowf[:, 3:4], None, ALU.subtract))
            link(dve.tensor_scalar(csneg[:, 2], csneg[:, 0], float(SJ - 2), NEG, ALU.is_gt, ALU.mult))
            link(tt(csneg[:, 1], csneg[:, 1], csneg[:, 2], ALU.add))
            for k in range(2):
                o = take(("pre", k))
                link(dve.tensor_copy(cc[:, k:k + 1], o[:, 0:1]))
                empty(dve.tensor_scalar(cx[:, k, 0], o[:, 0:NBLK], cc[:, k:k + 1], None, ALU.add))
            o = take(("kc",))
            empty(dve.tensor_copy(kc[:], o[:, 0:NBLK]))
            o = take(("vcp",))
            dve.wait_ge(masks, 2)
            for g in range(4):
                ins = dve.tensor_copy(vcbd[32 * g:32 * g + 32, :, g], o[32 * g:32 * g + 32, 0:P].rearrange("p (k n) -> p k n", k=NKV))
            empty(ins)
            o = take(("vcs",))
            link(dve.memset(vcs[:], 0.0))
            dve.tensor_copy(vcs[:, 0:3], o[0:32, 0:3 * P].rearrange("p (t n) -> p t n", t=3))
            empty(dve.tensor_copy(vcs[0:31, 3], o[0:31, 3 * P:4 * P]))
            dve.wait_ge(gs_ld, 16 * 16)
            dve.wait_ge(gates_made, NT + 2)
            for what, i in attention_steps():
                if what == "score":
                    kind, b, r, h = ITEMS[i]
                    o = take(("s", i))
                    n = sum(item_keys(ITEMS[i]))
                    if kind in "ps":
                        dve.tensor_reduce(nm[:, i:i + 1], o[:, 0:n], axis=X, op=ALU.max, negate=True).then_inc(s_max, 1)
                    elif kind == "c":
                        v = o[:, 0:256].rearrange("p (h j) -> p h j", h=NH)
                        sv = sct[:].rearrange("p (h j) -> p h j", h=NH)
                        pv = pb[:, i % 3, 0:256].rearrange("p (h j) -> p h j", h=NH)
                        link(tt(sv, v, cmneg[:, b:b + 1].broadcast_to([P, NH, 32]), ALU.add))
                        link(dve.tensor_reduce(mx8[:], sv, axis=X, op=ALU.max))
                        tt(sv, sv, mx8[:].unsqueeze(2).broadcast_to([P, NH, 32]), ALU.subtract).then_inc(s_max, 1)
                        dve.wait_ge(*emptied(("s", i)))
                        link(dve.tensor_reduce(rs8[:], pv, axis=X, op=ALU.add))
                        tt(pv, pv, cm01[:, b:b + 1].broadcast_to([P, NH, 32]), ALU.mult).then_inc(s_prob, 1)
                    else:
                        m = min(32, NBLK - (CJ_S + 2 * SJ * b))
                        if b:
                            dve.wait_ge(*emptied(("s", i - 3)))
                        if m < 32:
                            link(dve.memset(sct[:, 0:32], NEG))
                        link(tt(sct[:, 0:m], o[:, 0:m], csneg[:, 1, 0:m], ALU.add))
                        dve.tensor_reduce(nm[:, i:i + 1], sct[:, 0:32], axis=X, op=ALU.max, negate=True).then_inc(s_max, 1)
                elif what == "turn" and i % 2:
                    turn(dve, i, lambda d, s: dve.tensor_copy(d, s), take, empty)
                elif what == "gather":
                    g = i
                    last = GROUPS[g][-1]
                    kind, b, r, h = ITEMS[last]
                    o = ps[:, RING + g % 2, :]
                    dve.wait_ge(s_val, last + 1)
                    w = w8[:, g % 2]
                    if kind in "cp":
                        src = rs8[:] if kind == "c" else rs[:, GROUPS[g][0]:last + 1]
                        link(dve.reciprocal(w, src))
                        link(tt(w, w, tgate[:, b, r:3 * NH:3], ALU.mult))
                        wb = w.unsqueeze(2).broadcast_to([P, NH, HD])
                        ov = o.rearrange("p (h n) -> p h n", h=NH)
                        dst = ob[:, b % 2] if r == 0 else tmp_o[:]
                        if r == 0 and b >= 2:
                            dve.wait_ge(*emptied(("o", GROUP_OF[ITEMS.index(("p", b - 2, 2, NH - 1))])))
                        ins = tt(dst.rearrange("p (h n) -> p h n", h=NH), ov, wb, ALU.mult)
                        ins.then_inc(s_gath, 1)
                        dve.wait_ge(s_gath, g + 1)
                        if r:
                            ins = tt(ob[:, b % 2], ob[:, b % 2], tmp_o[:], ALU.add)
                            if r == 2:
                                ins.then_inc(osd_made, 1)
                            else:
                                link(ins)
                    else:
                        link(dve.reciprocal(w[:, 0:1], rs[:, last:last + 1]))
                        link(dve.tensor_scalar(w[:, 4:8], sel4[:], w[:, 0:1], tgate_s[:, b, r:r + 1], ALU.mult, ALU.mult))
                        wb = w[:, 4:8].unsqueeze(2).broadcast_to([P, 4, HD])
                        ov = o[:, 0:256].rearrange("p (h n) -> p h n", h=4)
                        dst = ob[:, b % 2, 0:256] if r == 0 else tmp_o[:, 0:256]
                        ins = tt(dst.rearrange("p (h n) -> p h n", h=4), ov, wb, ALU.mult)
                        ins.then_inc(s_gath, 1)
                        dve.wait_ge(s_gath, g + 1)
                        if r:
                            link(tt(ob[:, b % 2, 0:256], ob[:, b % 2, 0:256], tmp_o[:, 0:256], ALU.add))
                        if r == 2:
                            ow = ob[:, b % 2, 0:256].rearrange("p (h n) -> p n h", h=4)
                            if b >= 2:
                                dve.wait_ge(*emptied(("o", GROUP_OF[ITEMS.index(("s", b - 2, 2, 0))])))
                            dve.tensor_reduce(osd[:, b % 2, 0], ow, axis=X, op=ALU.add)
                            dve.tensor_reduce(osd[:, b % 2, 1], ow, axis=X, op=ALU.add).then_inc(osd_made, 1)
                elif what == "out":
                    kind, b, r, h = ITEMS[GROUPS[i][0]]
                    o = take(("o", i))
                    if kind == "p":
                        empty(dve.tensor_copy(onsaT[:, :, P * b:P * b + P], o.rearrange("p (k n) -> p k n", k=4)))
                    else:
                        at = NP_ + 2 * NDEC * b
                        for e in range(2):
                            dv = onsaT[HD * e:HD * e + HD, :, at:at + 2 * NDEC].rearrange("p k (a q) -> p a k q", a=2)
                            sv = o[HD * e:HD * e + HD, 0:P].rearrange("p (a k e q) -> p a k e q", a=2, k=4, e=2)[:, :, :, e]
                            ins = dve.tensor_copy(dv, sv)
                        empty(ins)
            for m in range(KD):
                for h in range(2):
                    dve.wait_ge(tg_ld[m % 4], 16 * (m // 4 + 1))
                    cut = slice(HALF * h, HALF * h + HALF)
                    for w, key in enumerate(("ab", "bb")):
                        o = take((key, m, h))
                        ins = dve.scalar_tensor_tensor(mt[:, w], gates[:, m % 4, w, cut], 1.0, o[:, 0:HALF], ALU.add, ALU.mult)
                        empty(ins)
                        dve.wait_ge(*emptied((key, m, h)))
                    tt(merged[:, m, cut], mt[:, 0], mt[:, 1], ALU.add).then_inc(merged_made, 1)
                    dve.wait_ge(merged_made, 2 * m + h + 1)
            dve.wait_ge(x_res, 16 * NT)
            for c in range(2):
                for t in range(NT):
                    p = TILES[t]
                    o = take(("wo", t, c))
                    cut = slice(512 * c, 512 * c + 512)
                    ins = dve.scalar_tensor_tensor(x[0:p, t, cut], o[0:p, :], 0.25, x[0:p, t, cut], ALU.mult, ALU.add)
                    empty(ins)
            dve.wait_ge(*emptied(("wo", NT - 1, 1)))
            dve.wait_ge(rt_ld, 64)
            link(dve.memset(lg[:], 0.0))
            for t in range(NT):
                p = TILES[t]
                dve.wait_ge(rstd_done, NT + t + 1)
                if t >= 2:
                    dve.wait_ge(pe_done, PLAN.done(("h2T", t - 2, 1)))
                    dve.wait_ge(h2_out[t % 2], 16 * (t // 2))
                dve.tensor_scalar(hn[0:p, t % 2], x[0:p, t], stat[0:p, 2, t:t + 1], None, ALU.mult).then_inc(hn_made, 1)
                if t:
                    turned_norm(dve, t - 1, ("h2T", t - 1), 1, take, empty)
                    router_logits(dve, t - 1, take, empty)
            turned_norm(dve, NT - 1, ("h2T", NT - 1), 1, take, empty)
            router_logits(dve, NT - 1, take, empty)
            dve.wait_ge(*emptied(("rt", NT - 1)))

            q = [P, NT, 4]
            G, E1, E2, S1, S2, W4, T4, T5 = (rtmp[:, j] for j in range(8))

            def first_of_largest(sel, v, mx):
                link(dve.tensor_reduce(mx, v, axis=X, op=ALU.max))
                link(tt(sel, v, mx.unsqueeze(2).broadcast_to(q), ALU.is_equal))
                for j in range(4):
                    ins = dve.tensor_scalar(T5[:, :, j:j + 1], sel[:, :, j:j + 1], float(4 - j), None, ALU.mult)
                link(ins)
                link(dve.tensor_reduce(rtmp[:, 9, :, 0], T5, axis=X, op=ALU.max))
                link(tt(sel, T5, rtmp[:, 9, :, 0].unsqueeze(2).broadcast_to(q), ALU.is_equal))

            gl = lg[:, :, 0:4]
            mxg, m1, m2 = rtmp[:, 8, :, 0], rtmp[:, 8, :, 1], rtmp[:, 8, :, 2]
            first_of_largest(G, gl, mxg)
            el = lg[:, :, 4:20].rearrange("p t (g e) -> p t g e", g=4)
            for g in range(4):
                gb = G[:, :, g:g + 1].broadcast_to(q)
                if g == 0:
                    link(tt(E1, el[:, :, 0], gb, ALU.mult))
                else:
                    link(tt(T4, el[:, :, g], gb, ALU.mult))
                    link(tt(E1, E1, T4, ALU.add))
            first_of_largest(S1, E1, m1)
            link(dve.scalar_tensor_tensor(E2, S1, NEG, E1, ALU.mult, ALU.add))
            first_of_largest(S2, E2, m2)
            tt(r16[:, :, 0:4], gl, mxg.unsqueeze(2).broadcast_to(q), ALU.subtract)
            tt(r16[:, :, 4:5], m2.unsqueeze(2), m1.unsqueeze(2), ALU.subtract).then_inc(lg_made, 1)
            n44 = [P, NT, 4, 4]
            for c, S in enumerate((S1, S2)):
                ins = tt(sel[:, c].rearrange("p t (g e) -> p t g e", g=4), G.unsqueeze(3).broadcast_to(n44),
                         S.unsqueeze(2).broadcast_to(n44), ALU.mult)
            link(ins)
            tt(msk_b[:], sel[:, 0], sel[:, 1], ALU.add).then_inc(msk_made, 1)
            dve.wait_ge(lg_exp, 1)
            link(dve.tensor_reduce(rtmp[:, 10, :, 0], r16[:, :, 0:4], axis=X, op=ALU.add))
            link(dve.tensor_scalar(rtmp[:, 10, :, 1], r16[:, :, 4], 1.0, None, ALU.add))
            link(tt(rtmp[:, 10, :, 0], rtmp[:, 10, :, 0], rtmp[:, 10, :, 1], ALU.mult))
            link(dve.reciprocal(rtmp[:, 10, :, 0], rtmp[:, 10, :, 0]))
            link(dve.tensor_scalar(wts[:, 0], rtmp[:, 10, :, 0], 0.5, None, ALU.mult))
            tt(wts[:, 1], wts[:, 0], r16[:, :, 4], ALU.mult)
            dve.wait_ge(consts, 3)
            o = take(("rank",))
            link(dve.memset(rk[:], 0.0))
            dve.tensor_copy(rk[:, 0:4], o[:, 0:4 * NE].rearrange("p (t e) -> p t e", e=NE))
            link(dve.tensor_copy(rk[0:64, 4], o[0:64, 4 * NE:5 * NE]))
            link(dve.tensor_reduce(rnd_f[:, 1:2], o[0:1, NT * NE:NT * NE + NE], axis=X, op=ALU.max))
            for k in range(1, MAXR):
                ins = dve.tensor_scalar(rnd_f[:, 1 + k:2 + k], rnd_f[:, 1:2], float(k * CAP), None, ALU.is_gt)
            link(ins)
            link(dve.tensor_reduce(rnd_f[:, 7:8], rnd_f[:, 2:1 + MAXR], axis=X, op=ALU.add))
            dve.tensor_scalar(rounds_i[:], rnd_f[:, 7:8], 1.0, None, ALU.add).then_inc(rounds_made, 1)
            for c in range(2):
                tt(both[:, 0, c], sel[:, c], rk[:], ALU.mult)
                ins = tt(both[:, 1, c], sel[:, c], ebase[:].unsqueeze(1).broadcast_to([P, NT, NE]), ALU.mult)
            link(ins)
            for c in range(2):
                dve.tensor_reduce(rank[:, c], both[:, 0, c], axis=X, op=ALU.add)
                ins = dve.tensor_reduce(base[:, c], both[:, 1, c], axis=X, op=ALU.add)
            link(ins)
            dve.scalar_tensor_tensor(pos_i[:, 0], base[:], float(MAXR), rank[:], ALU.mult, ALU.add).then_inc(pos_made, 1)
            empty(dve.memset(rnd_f[:, 0:1], 0.0))

            dve.sem_inc(hgt_made, 2)
            dve.sem_inc(x2_made, NT)
            for u in range(2):
                dve.sem_inc(hg_free[u], 1)
            dve.wait_ge(pos_made, 1)
            rounds = dve.value_load(rounds_i[0:1, 0:1], min_val=1, max_val=MAXR)

            def take_rows(j, n, u):
                for b in range(2):
                    dve.wait_ge(t_done, j * 32 + n * 2 + (b + 1))
                    ins = tt(hgT[:, u, 4 * b:4 * b + 4], ps[:, b].rearrange("p (k n) -> p k n", k=4),
                             g_cols[:, 1, 4 * b:4 * b + 4].unsqueeze(2).broadcast_to([P, 4, P]), ALU.mult)
                    ins.then_inc(hgt_made, 1)

            def activate(j, n, u):
                dve.wait_ge(th_made, j * 16 + n + 1)
                dve.scalar_tensor_tensor(th[:, u], th[:, u], 1.0, ps[:, 2 + u, 0:FF], ALU.add, ALU.mult).then_inc(si_made, 1)
                dve.wait_ge(si_made, j * 16 + n + 1)
                tt(si[:, u], th[:, u], ps[:, 2 + u, FF:2 * FF], ALU.mult).then_inc(act_made, 1)

            places = 4

            def place_link(j, ins, n):
                ins.then_inc(place_step, 1)
                dve.wait_ge(place_step, j * places + n)

            with dve.Fori(0, rounds) as j:
                dve.tensor_scalar(pos_f[:, 0], rank[:], 0.0, None, ALU.is_ge)
                place_link(j, dve.tensor_scalar(pos_f[:, 1], rank[:], float(CAP), None, ALU.is_lt), 1)
                place_link(j, tt(pos_f[:, 2], pos_f[:, 0], pos_f[:, 1], ALU.mult), 2)
                tt(wt_j[:], wts[:], pos_f[:, 2], ALU.mult)
                place_link(j, tt(pos_f[:, 3], rank[:], pos_f[:, 2], ALU.mult), 3)
                tt(pos_i[:, 1], pos_f[:, 3], base[:], ALU.add).then_inc(pos_made, 1)
                place_link(j, dve.tensor_scalar(rank[:], rank[:], float(CAP), None, ALU.subtract), 4)
                take_rows(j, 0, 0)
                activate(j, 0, 0)
                take_rows(j, 1, 1)
                with dve.Fori(0, NE // 2 - 1) as i:
                    activate(j, i * 2 + 1, 1)
                    take_rows(j, i * 2 + 2, 0)
                    activate(j, i * 2 + 2, 0)
                    take_rows(j, i * 2 + 3, 1)
                activate(j, NE - 1, 1)
                for t in range(NT):
                    p = TILES[t]
                    dve.wait_ge(yg_ld[t % 2], j * (32 * (3 - t % 2)) + 32 * (t // 2 + 1))
                    dve.scalar_tensor_tensor(x[0:p, t], yg[0:p, t % 2, 0], wt_j[0:p, 0, t:t + 1], x[0:p, t], ALU.mult, ALU.add
                                             ).then_inc(x2_half, 1)
                    dve.wait_ge(x2_half, j * NT + (t + 1))
                    dve.scalar_tensor_tensor(x[0:p, t], yg[0:p, t % 2, 1], wt_j[0:p, 1, t:t + 1], x[0:p, t], ALU.mult, ALU.add
                                             ).then_inc(x2_made, 1)
            for t in range(NT):
                p = TILES[t]
                o = take(("x2T", t, 1))
                empty(dve.tensor_copy(hT[:, 4:8, P * t:P * t + p], o.rearrange("p (k n) -> p k n", k=4)[:, :, 0:p]))
                for c in range(2):
                    cut = slice(512 * c, 512 * c + 512)
                    o = take(("pp", t, c))
                    dve.wait_ge(*emptied(("pg", t, c)))
                    ins = dve.scalar_tensor_tensor(tpg[0:p, c], tpg[0:p, c], 1.0, o[0:p, :], ALU.add, ALU.mult)
                    empty(ins)
                    dve.wait_ge(*emptied(("pp", t, c)))
                    dve.scalar_tensor_tensor(x[0:p, t, cut], tpg[0:p, c], 0.5, x[0:p, t, cut], ALU.mult, ALU.add
                                             ).then_inc(x3_made, 1)
            dve.wait_ge(gf_ld, 16)
            for t in range(NT):
                p = TILES[t]
                dve.wait_ge(rstd_done, 2 * NT + t + 1)
                dve.wait_ge(x3_made, 2 * t + 2)
                dve.scalar_tensor_tensor(x[0:p, t], x[0:p, t], stat[0:p, 2, t:t + 1], gf[0:p], ALU.mult, ALU.mult
                                         ).then_inc(y_made, 1)


_INS = ["x_prompt", "x_sample", "p_prompt", "p_sample", "cache_cmp_kv", "cache_slc_kv", "cache_win_kv", "state_ssm",
        "page_table", "norm1_g", "w_in", "ssm_lam_re", "ssm_lam_im", "ssm_log_dt", "ssm_b_re", "ssm_b_im", "ssm_c_re",
        "ssm_c_im", "ssm_d", "w_glu", "b_glu", "cmp_pe", "cmp_w1", "cmp_w2", "w_ssm_out", "w_nsa_out", "w_o", "norm2_g",
        "w_route_group", "b_route_group", "w_route_expert", "b_route_expert", "w_exp_gate", "w_exp_up", "w_exp_down",
        "w_ple", "w_ple_gate", "final_norm_g"]
_OUTS = [(1, NP_, D), (NSEQ, NDEC, D), (1, 1, NP_, 2, NKV, HD), (1, 1, NP_, 2, NKV, HD), (1, 1, NP_, 2, NKV, HD),
         (1, 1, NG, NST, 2), (1, NSEQ, NDEC, 2, NKV, HD), (1, NSEQ, NDEC, 2, NKV, HD),
         (1, NSEQ, PAST + NDEC, 2, NKV, HD), (1, NSEQ, NG, NST, 2)]


def kernel(**inputs):
    import concourse.bacc as bacc
    from concourse.bass_utils import run_bass_kernel_spmd

    nc = bacc.Bacc("TRN2", target_bir_lowering=False, num_devices=1)
    arrays, ins, outs = {}, {}, []
    for name in _INS:
        a = np.ascontiguousarray(inputs[name])
        arrays[f"in_{name}"] = a
        ins[name] = nc.dram_tensor(f"in_{name}", a.shape, mybir.dt.from_np(a.dtype), kind="ExternalInput").ap()
    for i, shape in enumerate(_OUTS):
        outs.append(nc.dram_tensor(f"out_{i}", shape, F32, kind="ExternalOutput").ap())
    build(nc, ins, outs)
    r = run_bass_kernel_spmd(nc, [arrays], core_ids=[0])
    return tuple(r.results[0][f"out_{i}"] for i in range(len(_OUTS)))
```

```python
from contextlib import ExitStack
import math

import numpy as np

import concourse.bass as bass
from concourse import mybir

F32 = mybir.dt.float32
BF16 = mybir.dt.bfloat16
I32 = mybir.dt.int32
ALU = mybir.AluOpType
ACT = mybir.ActivationFunctionType
X = mybir.AxisListType.X

P = 128
D = 1024
KD = D // P
NP_, NSEQ, NDEC = 512, 8, 8
ROWS = NP_ + NSEQ * NDEC
HALF = ROWS // 2
TILES = [128, 128, 128, 128, 64]
NT = len(TILES)
PAST = 256
SSM_W, GRP, NG, NST = 512, 16, 32, 64
CH = 8
NCH = ROWS // CH
NPC = NP_ // CH
NS = NG // 2
HD, NH, NKV, GQA = 64, 8, 2, 4
KVW = 256
COL_Q, COL_KV, COL_GA, COL_GB = 512, 1024, 1816, 2840
NKVG = 3 * KVW + 3 * NH
SCALE = HD ** -0.5
NEG = -1e30
CL, CS = 32, 16
CT0 = CL
CTOK = CT0 + NP_ + NSEQ * PAST
NBLK = CTOK // CS - 1
CJ_P = CT0 // CS
CJ_S = CJ_P + NP_ // CS
SJ = PAST // CS
NE, FF = 16, 256
PLE = 256
CAP = 128
MAXR = -(-ROWS // CAP)
EPS = 1e-6
RING = 6
GELU = ACT.Gelu_apprx_tanh


class Plan:

    def __init__(self):
        self.at, self.by, self.count, self.order = {}, {}, {}, []

    def add(self, key, engine):
        self.at[key] = len(self.order)
        self.order.append(key)
        self.count[engine] = self.count.get(engine, 0) + 1
        self.by[key] = (engine, self.count[engine])

    def done(self, key):
        return self.at[key] + 1


def attention_items():
    items = []
    for b in range(4):
        items += [("c", b, 0, 0)]
        items += [("p", b, r, h) for r in (1, 2) for h in range(NH)]
    for t in range(NSEQ // 2):
        items += [("sc", t, 0, 0), ("s", t, 1, 0), ("s", t, 2, 0)]
    return items


ITEMS = attention_items()
GROUPS = []
for _i, _it in enumerate(ITEMS):
    if GROUPS and (ITEMS[GROUPS[-1][-1]][:3] == _it[:3]):
        GROUPS[-1].append(_i)
    else:
        GROUPS.append([_i])
GROUP_OF = {i: g for g, m in enumerate(GROUPS) for i in m}
T_LAG, V_LAG, O_LAG = 3, 5, 2


def item_keys(it):
    kind, b = it[0], it[1]
    if kind == "p":
        return [128] * (b + 1)
    if kind == "c":
        return [128, 128]
    return [32] if kind == "sc" else [128, 128, 64]


def attention_steps():
    steps, late = [], []
    n = len(ITEMS)
    first = [it[0] for it in ITEMS].index("sc")
    for i in range(n + V_LAG + O_LAG):
        if 0 <= i - (first - 8) < 8:
            steps.append(("cached", i - (first - 8)))
        if i < n:
            steps.append(("score", i))
        if 0 <= i - T_LAG < n:
            steps.append(("turn", i - T_LAG))
        if 0 <= i - V_LAG < n:
            j = i - V_LAG
            steps.append(("value", j))
            if j == GROUPS[GROUP_OF[j]][-1]:
                steps.append(("gather", GROUP_OF[j]))
                if ITEMS[j][2] == 2:
                    late.append((i + O_LAG, GROUP_OF[j]))
        if late and late[0][0] == i:
            steps.append(("out", late.pop(0)[1]))
    return steps


KD_A = 3


def gate_jobs(p, m):
    for h in range(2):
        for w in ("ga", "gb"):
            p.add((w, m, h), "act")


def gates_out(buf, n):
    return len(range(buf, n, 4))


def second_norm_steps():
    steps = []
    for t in range(NT):
        steps.append(("wo", t))
        if t >= 2:
            steps.append(("rt", t - 2))
        if t >= 1:
            steps.append(("h2T", t - 1))
    steps += [("pT", t) for t in range(NT)]
    steps += [("rt", NT - 2), ("pp", 0), ("h2T", NT - 1), ("pp", 1), ("rt", NT - 1), ("pp", 2), ("rank", 0)]
    steps += [("first", 0), ("pp", NT - 2)]
    return steps


def embedding_steps():
    steps = [("product", NT - 1, 0), ("product", NT - 1, 1), ("turn", 0, 0)]
    for t in range(NT):
        steps.append(("gate", t, 0))
        if t + 1 < NT:
            steps.append(("turn", t + 1, 0))
        steps.append(("gate", t, 1))
    return steps


def make_plan():
    p = Plan()
    for t in range(NT):
        for k in range(2):
            p.add(("hT", t, k), "dve")
    for t in range(NT):
        p.add(("u", t), "act")
    for t in range(NT):
        for c in range(2):
            p.add(("kv", t, c), "act")
    p.add(("lam",), "dve")
    p.add(("c", 0), "dve")
    p.add(("c", 1), "dve")
    p.add(("h0",), "dve")
    for m in range(KD_A):
        gate_jobs(p, m)
    for i in range(5):
        p.add(("x", i), "dve")
    for i in range(8):
        p.add(("vt", i), "act")
    for i in range(8):
        p.add(("k", i), "act")
    for i in range(6):
        p.add(("d", i), "act")
    for m in range(4):
        for h in range(2):
            p.add(("q", m, h), "act")
    for m in range(KD_A, KD):
        gate_jobs(p, m)
    for i in range(8):
        p.add(("y", i), "dve")
    p.add(("fin",), "act")
    for t in range(CH):
        p.add(("zg", t), "dve")
    for m in range(4):
        for h in range(2):
            p.add(("glu", m, h), "act")
    p.add(("pe",), "act")
    for i in range(10):
        p.add(("ct", i), "act")
    for r in range(2):
        p.add(("ktp", r), "act")
    p.add(("ktn",), "act")
    for k in range(2):
        p.add(("pre", k), "dve")
    p.add(("kc",), "dve")
    p.add(("vcp",), "dve")
    p.add(("vcs",), "dve")
    for what, i in attention_steps():
        if what == "score":
            p.add(("s", i), "act")
        elif what == "turn":
            p.add(("t", i), "dve" if i % 2 else "act")
        elif what == "cached":
            p.add(("kts", i // 4, i % 4), "act")
        elif what == "out":
            p.add(("o", i), "dve")
    for m in range(KD):
        for h in range(2):
            for w in ("ab", "bb"):
                p.add((w, m, h), "dve")
    for t in range(NT):
        p.add(("wo", t, 0), "dve")
    for what, t in second_norm_steps():
        if what == "wo":
            p.add(("wo", t, 1), "dve")
        elif what == "h2T":
            for k in range(2):
                p.add(("h2T", t, k), "dve")
        elif what == "rt":
            p.add(("rt", t), "dve")
        elif what == "pT":
            p.add(("pT", t), "act")
        elif what == "pp":
            for c in range(2):
                p.add(("pp", t, c), "act")
        else:
            p.add((what,), "dve")
    for what, t, c in embedding_steps():
        if what == "turn":
            for k in range(2):
                p.add(("x2T", t, k), "act")
        elif what == "product":
            p.add(("pp", t, c), "act")
        else:
            p.add(("pg", t, c), "act")
    return p


PLAN = make_plan()

WEIGHTS = [("u", ("u", NT - 1)), ("kv0", ("kv", NT - 1, 0)), ("kv1", ("kv", NT - 1, 1)), ("g0", ("gb", 1, 1)),
           ("g1", ("gb", 3, 1)), ("q", ("q", 3, 1)), ("g2", ("gb", 5, 1)), ("g3", ("gb", 7, 1)), ("glu", ("glu", 3, 1)),
           ("w1k0", ("pre", 0)), ("w1k1", ("pre", 1)),
           ("so", ("ab", KD - 1, 1)), ("no", ("bb", KD - 1, 1)), ("wo0", ("wo", NT - 1, 0)), ("wo1", ("wo", NT - 1, 1)),
           ("ple", ("pp", NT - 1, 1)), ("pg0", ("pg", NT - 1, 0)), ("pg1", ("pg", NT - 1, 1))]
NW = 3
W_AT = {name: i for i, (name, _) in enumerate(WEIGHTS)}


def build(nc, I, O):
    (y_prompt, y_sample, o_cmp_p, o_slc_p, o_win_p, o_ssm_p, o_cmp_s, o_slc_s, o_win_s, o_ssm_s) = O
    u_dram = nc.dram_tensor("u_rows", (ROWS, SSM_W), F32).ap()
    g_dram = nc.dram_tensor("gate_rows", (NSEQ * NDEC, 3 * NH), F32).ap()
    tg_dram = nc.dram_tensor("gates_by_features", (KD, P, 2, ROWS), F32).ap()
    k_dram = nc.dram_tensor("kernel_taps", (GRP, NG, P), F32).ap()
    h2_dram = nc.dram_tensor("h2_rows", (ROWS, D), F32).ap()
    list_dram = nc.dram_tensor("row_of_slot", (NE * MAXR * CAP, 1), I32).ap()
    ye_dram = nc.dram_tensor("expert_rows", (NE * CAP, D), F32).ap()
    w_in = I["w_in"][0]
    n_pool = I["cache_cmp_kv"].shape[1]
    PARS = 16 * 13

    with ExitStack() as ctx:
        def sem(name):
            return ctx.enter_context(nc.semaphore(name))

        def sb(name, shape, dt=F32, stack=ctx):
            return stack.enter_context(nc.sbuf_tensor(name, shape, dt))

        def flat(t):
            return (t if isinstance(t, bass.AP) else t[:]).rearrange("p a b -> p (a b)")

        ps = ctx.enter_context(nc.psum_tensor("ps", [P, 8, 512], F32))
        ident = sb("ident", [P, P])
        ident_b = sb("ident_b", [P, P], BF16)
        causal = sb("causal", [P, P], BF16)
        new_mask = sb("new_mask", [P, 4, 64], BF16)
        g_cols = sb("g_cols", [P, 2, KD])
        tri_b = sb("tri_b", [P, P], BF16)
        ones_b = sb("ones_b", [P, P], BF16)
        msk_b = sb("msk_b", [P, NT, NE], BF16)
        tokid = sb("tokid", [P, NT], I32)
        ebase = sb("ebase", [P, NE])
        zero_i = sb("zero_i", [P, NE * MAXR], I32)
        halfneg = sb("halfneg", [P, 1])
        stat = sb("stat", [P, 4, 8])
        b_glu = sb("b_glu", [P, 4])
        ptab = sb("ptab", [1, 2 * NSEQ], I32)
        ring = [sb(f"w_slot{i}", [P, 4096]) for i in range(NW)]
        hT = sb("hT", [P, KD, ROWS])
        gates = flat(hT).rearrange("p (m w n) -> p m w n", m=4, w=2)
        kv = sb("kv", [P, NT, NKVG])
        tgate = sb("tgate", [P, NT, 3 * NH])
        tgate_s = sb("tgate_s", [P, 4, 3])
        qg_t = sb("qg", [P, 2 * 4 * ROWS])
        qT = qg_t[:, 0:4 * ROWS].rearrange("p (g n) -> p g n", g=GQA)
        gluT = qg_t[:, 4 * ROWS:].rearrange("p (k n) -> p k n", k=4)
        ucg = qg_t[0:NCH, 0:CH * SSM_W].rearrange("p (g n) -> p g n", g=NG)

        with ExitStack() as s5:
            x_in = sb("x_in", [P, NT, D], stack=s5)
        with ExitStack() as s5:
            pw = sb("pw", [P, CH + 1, 2, NS], stack=s5)
            pwr = sb("pwr", [P, CH, 2, NS], stack=s5)
            sm = sb("sm", [P, 24, NS], stack=s5)
            bbar = sb("bbar", [P, 2, NS, GRP], stack=s5)
            vt = sb("vt", [P, NS * 2, P], stack=s5)
            zgT = vt[:].rearrange("p a b -> p (a b)")[:, 0:4 * ROWS].rearrange("p (k n) -> p k n", k=4)
            gm = sb("gm", [P, 2, NS, CH + 1, GRP], stack=s5)
            xg_t = sb("xg", [P, NT * SSM_W], stack=s5)
            u_rows = xg_t[:].rearrange("p (t n) -> p t n", t=NT)
            stage_a = xg_t[:, 0:8 * HALF].rearrange("p (b w n) -> p b w n", b=4, w=2)
            stage_b = flat(gluT).rearrange("p (b w n) -> p b w n", b=4, w=2)
            xg = xg_t[:, 0:NG * NCH].rearrange("p (g n) -> p g n", g=NG)
            hst = sb("hst", [P, 2, NS, NCH], stack=s5)
            fin = sb("fin", [P, 2, 1 + NSEQ, NS], stack=s5)
            walk = sb("walk", [P, 4, 2, NS], stack=s5)
            vn_t = sb("vn", [P, NS * 2 * P], stack=s5)
            vn = vn_t[:].rearrange("p (s r n) -> p s r n", s=NS, r=2)
            wt = vn_t[:].rearrange("p (g n) -> p g n", g=NG)
            uc_t = sb("uc", [P, NS * (2 * CH + 1) * GRP], stack=s5)
            uc = uc_t[0:NCH, 0:CH * SSM_W].rearrange("p (t n) -> p t n", t=CH)
            tmp_v = uc_t[:, 0:NS * CH * GRP]
            tmp_g = uc_t[:, NS * CH * GRP:]
            lam_r = sb("lam_r", [NS, 2, P], stack=s5)
            raw = sb("raw", [P, 1024], stack=s5)
            c_r = hst[:].rearrange("p r s c -> p (r s c)")[:, 0:1024].rearrange("p (r b u n) -> p r b u n", r=2, b=4, u=2)
            b_r = raw[:, 512:1024].rearrange("p (r s c) -> p r s c", r=2, s=NS)
            ks = raw[0:GRP, :].rearrange("p (u g n) -> p u g n", u=2, g=4)
            cst = sb("cst", [P, 2, NS, GRP], stack=s5)
            tmp9 = cst[:].rearrange("p r s c -> p (r s c)")[:, 0:2 * 9 * NS].rearrange("p (r q s) -> p r q s", r=2, q=9)
            h0_r = sb("h0_r", [P, 2 * P], stack=s5)
            fo = h0_r[:].rearrange("p (n r) -> p n r", r=2)
            fo_p = sb("fo_p", [NS, P, 2], stack=s5)
            d_b = sb("d_b", [NCH, SSM_W], stack=s5)
            ldt = sb("ldt", [P, NS], stack=s5)

        with ExitStack() as late:
            onsaT = sb("onsaT", [P, 4, ROWS], stack=late)
            with ExitStack() as at:
                caches = sb("caches", [P, 2, NSEQ, 2, KVW], stack=at)
                kvct_t = sb("kvct", [P, 2 * CTOK], stack=at)
                kvct = kvct_t[:].rearrange("p (k n) -> p k n", k=2)
                kts = kvct_t[:, 0:2 * NSEQ * PAST].rearrange("p (r s n) -> p r s n", r=2, s=NSEQ)
                pe_r = flat(hT)[0:2 * CL, 4096:4096 + 2 * HD].rearrange("p (u d) -> p u d", u=2)
                w2 = flat(hT)[:, 4224:4224 + 2 * P].rearrange("p (k e) -> p k e", k=2)
                cxr = sb("cxr", [P, 4, 32], stack=at)
                rawc = flat(hT)[:, 0:NSEQ * 2 * KVW].rearrange("p (s u n) -> p s u n", s=NSEQ, u=2)
                cx = sb("cx", [P, 2, 2, NBLK], stack=at)
                cc = sb("cc", [P, 2], stack=at)
                kc = sb("kc", [P, NBLK], stack=at)
                vcbd = sb("vcbd", [P, NKV, GQA, HD], stack=at)
                vcs = sb("vcs", [32, 4, P], stack=at)
                kt = sb("kt", [P, 2, ROWS], stack=at)
                qpad = sb("qpad", [P, NSEQ, P], stack=at)
                pb = sb("pb", [P, T_LAG + 1, 512], stack=at)
                pt = sb("pt", [P, V_LAG - T_LAG + 1, 512], stack=at)
                ob = sb("ob", [P, 2, 512], stack=at)
                tmp_o = sb("tmp_o", [P, 512], stack=at)
                sct = sb("sct", [P, 256], stack=at)
                osd = sb("osd", [P, 2, 2, HD], stack=at)
                nm = sb("nm", [P, len(ITEMS)], stack=at)
                rs = sb("rs", [P, len(ITEMS)], stack=at)
                mx8 = sb("mx8", [P, NH], stack=at)
                rs8 = sb("rs8", [P, NH], stack=at)
                w8 = sb("w8", [P, 2, NH], stack=at)
                cm01 = sb("cm01", [P, 4, 32], stack=at)
                cmneg = sb("cmneg", [P, 4, 32], stack=at)
                csneg = sb("csneg", [P, 3, 32], stack=at)
                sel4 = sb("sel4", [P, 4], stack=at)
                rowi = sb("rowi", [P, 3], I32, stack=at)
                rowf = sb("rowf", [P, 4], stack=at)
                nmk = pb[:].rearrange("p i n -> p (i n)")[:, 0:3 * 4 * 64].rearrange("p (i j n) -> p i j n", i=3, j=4)
            with ExitStack() as fin_s:
                merged = sb("merged", [P, KD, ROWS], stack=fin_s)
                x = sb("x", [P, NT, D], stack=fin_s)
                mt = sb("mt", [P, 2, HALF], stack=fin_s)
                hn = sb("hn", [P, 2, D], stack=fin_s)
                w_rt = sb("w_rt", [P, KD, 20], stack=fin_s)
                b_rt = sb("b_rt", [P, 20], stack=fin_s)
                lg = sb("lg", [P, NT, 20], stack=fin_s)
                rtmp = sb("rtmp", [P, 9, NT, 4], stack=fin_s)
                r16 = sb("r16", [P, NT, 16], stack=fin_s)
                wgu = sb("wgu", [P, 2, 2, KD, FF], stack=fin_s)
                wdn = flat(merged)[:, 0:4 * D].rearrange("p (u k n) -> p u k n", u=2, k=2)
                th = sb("th", [P, 2, FF], stack=fin_s)
                si = sb("si", [P, 2, FF], stack=fin_s)
                actT = sb("actT", [P, 2, 2, CAP], stack=fin_s)
                picked = th[:].rearrange("p u n -> p (u n)")[:, 0:16 * NT].rearrange("p (t g e) -> p t g e", t=NT, g=4)
                both = th[:].rearrange("p u n -> p (u n)")[:, 0:4 * NT * NE].rearrange("p (a c t e) -> p a c t e", a=2, c=2, t=NT)
                slot_no = sb("slot_no", [P, P], stack=fin_s)
                place = sb("place", [P, NT, 2], stack=fin_s)
                at_slot = sb("at_slot", [P, 2, NT, P], BF16, stack=fin_s)
                row_f = sb("row_f", [P, 2, NT], stack=fin_s)
                row_b = sb("row_b", [P, 2, NT], BF16, stack=fin_s)
                first_f = sb("first_f", [P, 2, 2], stack=fin_s)
                sel = sb("sel", [P, 2, NT, NE], stack=fin_s)
                rk = sb("rk", [P, NT, NE], stack=fin_s)
                pos_f = sb("pos_f", [P, 4, 2, NT], stack=fin_s)
                rank = sb("rank", [P, 2, NT], stack=fin_s)
                base = sb("base", [P, 2, NT], stack=fin_s)
                wt_j = sb("wt_j", [P, 2, NT], stack=fin_s)
                pos_i = sb("pos_i", [P, 2, 2, NT], I32, stack=fin_s)
                wts = sb("wts", [P, 2, NT], stack=fin_s)
                tick = sb("tick", [P, 2], stack=fin_s)
                idx = sb("idx", [P, 2], I32, stack=fin_s)
                rnd_f = sb("rnd_f", [1, 8], stack=fin_s)
                rounds_i = sb("rounds_i", [1, 1], I32, stack=fin_s)
                ysb = flat(onsaT)[:, 0:2 * D].rearrange("p (u n) -> p u n", u=2)
                hg = flat(hT)[:, 0:2 * D].rearrange("p (u n) -> p u n", u=2)
                hgT = flat(hT)[:, 2 * D:4 * D].rearrange("p (u k n) -> p u k n", u=2, k=KD)
                yg = wgu[:].rearrange("p u w k n -> p (u w k n)")[:, 0:4 * D].rearrange("p (u c n) -> p u c n", u=2, c=2)
                p_in = flat(kv)[:, 0:NT * PLE].rearrange("p (t n) -> p t n", t=NT)
                pT = flat(kv)[:, NT * PLE:NT * PLE + 2 * ROWS].rearrange("p (k n) -> p k n", k=2)
                gf = flat(kv)[:, NT * PLE + 2 * ROWS:NT * PLE + 2 * ROWS + D]
                pps = [qg_t[:, 1024 + D * t:1024 + D * t + D] for t in range(3)] + [hn[:, 1], hn[:, 0]]
                tpg = flat(qT)[:, 0:1024].rearrange("p (u n) -> p u n", u=2)

        pe_done = sem("pe_done")
        drained = {"dve": sem("dve_drained"), "act": sem("act_drained")}
        dve_step, pool_step = sem("dve_step"), sem("pool_step")
        x_ld = [sem(f"x_loaded{t}") for t in range(NT)]
        w_ld = [sem(f"w_loaded{i}") for i in range(NW)]
        gains_ld, par_ld, rt_ld, gf_ld, p_ld = sem("gains_loaded"), sem("s5_params_loaded"), sem("router_loaded"), sem("final_gain_loaded"), sem("ple_rows_loaded")
        consts = sem("constants_made")
        sq_done, rstd_done = sem("sum_squares"), sem("rstd_made")
        u_out, uc_ld, k_out, w_toep = sem("u_written"), sem("u_by_chunks"), [sem(f"taps_written{u}") for u in range(2)], sem("toeplitz_loaded")
        dt_done, angles, trig = sem("dt_made"), sem("angles_made"), sem("sin_cos_made")
        powers, v_made, g_made = sem("powers_made"), sem("v_made"), sem("g_made")
        half_done = sem("first_kv_head_done")
        ucg_made = sem("u_by_groups")
        w_zero, ud_made, walked, y_gelu = sem("toeplitz_zeroed"), sem("skip_made"), sem("states_walked"), sem("y_activated")
        glu_made, fin_out, outs = sem("glu_made"), sem("states_written"), sem("outputs_written")
        gates_made, gd_out, gs_ld = sem("gates_made"), sem("gates_written"), sem("sample_gates_loaded")
        pt_ld = sem("page_table_loaded")
        w_cmp_zero, w2_ld, pe_ld, raw_ld = sem("w1_w2_zeroed"), sem("w2_loaded"), sem("embeddings_loaded"), [sem(f"raw_pages{i}") for i in range(NSEQ)]
        cache_ld = sem("caches_loaded")
        cmp_g = sem("cmp_gelu")
        masks, row_masks, qpad_made = sem("masks_made"), sem("row_masks_made"), sem("qpad_made")
        bglu_half, si_made = sem("glu_bias_halved"), sem("silu_made")
        s_max, s_prob, s_val, s_gath = sem("score_max"), sem("probabilities"), sem("values_done"), sem("values_taken")
        osd_made = sem("sample_outputs")
        merged_made = sem("merged_made")
        x_res, hn_made = sem("x_reloaded"), sem("hn_made")
        lg_made, lg_exp = sem("logit_diffs"), sem("logit_exps")
        gu_ld, wd_ld = ([sem(f"{w}_weights_loaded{u}") for u in range(2)] for w in ("gate_up", "down"))
        h2_out, list_zero, listed = [sem(f"h2_written{u}") for u in range(2)], sem("slots_zeroed"), sem("slots_filled")
        msk_made, pos_made, rounds_made = sem("choices_made"), sem("slots_made"), sem("rounds_made")
        idx_ld, hg_ld, hg_free = ([sem(f"{w}{u}") for u in range(2)] for w in ("slot_rows_loaded", "rows_gathered", "rows_turned"))
        t_done = sem("gathered_in_psum")
        hgt_made, g_done, ta_done, actt_made = sem("gathered_turned"), sem("gate_up_done"), sem("act_turned"), sem("actT_made")
        d_done, d_taken, ye_out = sem("down_done"), sem("down_taken"), [sem(f"expert_rows_written{u}") for u in range(2)]
        yg_ld, x2_made = [[sem(f"slot_outputs_loaded{u}{c}") for c in range(2)] for u in range(2)], sem("x2_made")
        slot_nos, at_slots = sem("slot_numbers_made"), sem("rows_compared")
        pool_tick = sem("pool_tick")
        place_step, x2_half = sem("round_places_step"), sem("first_choice_added")
        tg_out, tg_ld = ([sem(f"{w}{i}") for i in range(4)] for w in ("gates_out", "gates_back"))
        th_made, act_made = sem("gate_tanh"), sem("act_made")
        x3_made, y_made = sem("x3_made"), sem("y_made")

        def bank(key):
            return ps[:, PLAN.at[key] % RING, :]

        def freed(key):
            last = PLAN.order[PLAN.at[key] - RING]
            return drained[PLAN.by[last][0]], PLAN.by[last][1]

        def emptied(key):
            return drained[PLAN.by[key][0]], PLAN.by[key][1]

        w_parts = {"g%d" % i: 2 for i in range(KD // 2)} | {"q": KD * NKV, "w1k0": NKV, "w1k1": NKV}
        w_need, total = {}, [0] * NW
        for i, (name, _) in enumerate(WEIGHTS):
            total[i % NW] += 16 * w_parts.get(name, 1)
            w_need[name] = (w_ld[i % NW], total[i % NW])

        def slot(name):
            return ring[W_AT[name] % NW]

        def wk(name, n, at=0, k=KD):
            return slot(name)[:, at:at + k * n].rearrange("p (k n) -> p k n", k=k)

        def w1(k):
            return wk(f"w1k{k}", P, 0, CL)

        block = ctx.enter_context(nc.Block())

        @block.sync
        def _(sp):
            xp = I["x_prompt"][0].rearrange("(t p) d -> p t d", p=P)
            xs = I["x_sample"].rearrange("s q d -> (s q) d")

            def rows(src, t, dst):
                a = src[0][:, t, :] if t < 4 else src[1]
                return sp.dma_start(dst[0:TILES[t], t, :], a)

            def load_weights(name):
                i = W_AT[name]
                if i >= NW:
                    sp.wait_ge(pe_done, PLAN.done(WEIGHTS[i - NW][1]))
                s = w_ld[i % NW]

                def one(src, at, n, k=KD):
                    sp.dma_start(slot(name)[:, at:at + k * n].rearrange("p (k n) -> p k n", k=k),
                                 src.rearrange("(k p) n -> p k n", p=P)).then_inc(s, 16)
                if name == "u":
                    one(w_in[:, 0:512], 0, 512)
                elif name == "kv0":
                    one(w_in[:, COL_KV:COL_KV + 396], 0, 396)
                elif name == "kv1":
                    one(w_in[:, COL_KV + 396:COL_GA], 0, 396)
                elif name == "q":
                    for k in range(KD):
                        for h in range(NKV):
                            sp.dma_start(slot(name)[:, 512 * k:512 * k + 512].rearrange("p (m h n) -> p h m n", m=GQA, h=NKV)[:, h],
                                         w_in[P * k:P * k + P, COL_Q + 256 * h:COL_Q + 256 * h + 256].rearrange("p (m n) -> p m n", m=GQA)
                                         ).then_inc(s, 16)
                elif name == "glu":
                    one(I["w_glu"][0], 0, 512, 4)
                elif name[:2] == "wo":
                    c = int(name[2:])
                    one(I["w_o"][0][:, 512 * c:512 * c + 512], 0, 512)
                elif name == "ple":
                    one(I["w_ple"][0], 0, D, 2)
                elif name[:2] == "pg":
                    c = int(name[2:])
                    one(I["w_ple_gate"][0][:, 512 * c:512 * c + 512], 0, 512)
                elif name[:3] == "w1k":
                    for h in range(NKV):
                        sp.dma_start(w1(int(name[3:]))[HD * h:HD * h + HD, :, HD * h:HD * h + HD],
                                     I["cmp_w1"][0][int(name[3:])].rearrange("i d e -> d i e")).then_inc(s, 16)
                elif name == "so":
                    one(I["w_ssm_out"][0], 0, D, 4)
                elif name == "no":
                    one(I["w_nsa_out"][0], 0, D, 4)
                else:
                    at = 2 * P * int(name[1:])
                    one(w_in[:, COL_GA + at:COL_GA + at + 2 * P], 0, 2 * P)
                    one(w_in[:, COL_GB + at:COL_GB + at + 2 * P], 2048, 2 * P)

            for t in range(NT):
                rows((xp, xs), t, x_in).then_inc(x_ld[t], 16)
            for name in ("u", "kv0", "kv1"):
                load_weights(name)
            for t in range(NT):
                sp.wait_ge(*emptied(("u", t)))
                sp.dma_start(u_dram[P * t:P * t + TILES[t], :], u_rows[0:TILES[t], t, :]).then_inc(u_out, 16)
            load_weights("g0")
            load_weights("g1")
            load_weights("q")
            sp.wait_ge(*emptied(("kv", NT - 1, 1)))
            for n, (op, os) in enumerate(((o_cmp_p, o_cmp_s), (o_slc_p, o_slc_s), (o_win_p, None))):
                sp.dma_start(op[0, 0].rearrange("(t p) a h d -> p t (a h d)", p=P),
                             kv[:, 0:4, KVW * n:KVW * n + KVW]).then_inc(outs, 16)
                if os is not None:
                    sp.dma_start(os[0].rearrange("s q a h d -> (s q) (a h d)"),
                                 kv[0:64, 4, KVW * n:KVW * n + KVW]).then_inc(outs, 16)
            for s in range(NSEQ):
                sp.dma_start(o_win_s[0, s, PAST:PAST + NDEC].rearrange("q a h d -> q (a h d)"),
                             kv[NDEC * s:NDEC * s + NDEC, 4, 2 * KVW:3 * KVW]).then_inc(outs, 16)
            sp.dma_start(o_win_s[0, :, 0:PAST].rearrange("s p a h d -> s (p a h d)"),
                         I["cache_win_kv"][0].rearrange("s p a h d -> s (p a h d)")).then_inc(outs, 16)
            n_outs = 16 * (3 + 2 + NSEQ + 1)
            sp.wait_ge(u_out, 16 * NT)
            sp.wait_ge(v_made, 1)
            sp.wait_ge(g_made, 1)
            sp.dma_start(uc, u_dram.rearrange("(c t) n -> c t n", t=CH)).then_inc(uc_ld, 16)
            sp.wait_ge(gates_made, NT + 2)
            sp.dma_start(g_dram, tgate[0:64, NT - 1, :]).then_inc(gd_out, 16)
            sp.wait_ge(gd_out, 16)
            gv = g_dram.rearrange("(t a q) (k g r) -> a k g q t r", a=2, q=NDEC, k=NKV, g=GQA)
            for a in range(2):
                for k in range(NKV):
                    for g in range(GQA):
                        row = 64 * a + 32 * k + NDEC * g
                        sp.dma_start(tgate_s[row:row + NDEC], gv[a, k, g]).then_inc(gs_ld, 16)
            load_weights("g2")
            for i in range(8):
                sp.wait_ge(*emptied(("k", i)))
                sp.dma_start(k_dram[:, 8 * (i // 2) + i % 2:8 * (i // 2) + i % 2 + 7:2, :], ks[:, i % 2, :, :]).then_inc(k_out[i % 2], 16)
            for u in range(2):
                sp.wait_ge(k_out[u], 16 * 4)
            sp.wait_ge(w_zero, 1)
            for t in range(CH):
                sp.dma_start(wt[GRP * t:GRP * t + GRP, :, GRP * t:P], k_dram[:, :, 0:P - GRP * t]).then_inc(w_toep, 16)
            load_weights("g3")
            load_weights("glu")
            sp.wait_ge(pt_ld, 16)

            def page(s, u):
                return sp.value_load(ptab[0:1, 2 * s + u:2 * s + u + 1], min_val=0, max_val=n_pool - 1)

            def load_raw(s):
                for u in range(2):
                    sp.dma_start(rawc[:, s, u, :],
                                 I["cache_cmp_kv"][0, bass.ds(page(s, u), 1)].rearrange("o p a h d -> (o p) (a h d)")
                                 ).then_inc(raw_ld[s], 16)
            sp.wait_ge(pe_done, PLAN.done(("gb", KD - 1, 1)))
            for s in range(NSEQ):
                load_raw(s)
            for u in range(2):
                sp.dma_start(pe_r[:, u], I["cmp_pe"][0].rearrange("k i d -> (k i) d")).then_inc(pe_ld, 16)
            for h in range(NKV):
                sp.dma_start(w2[HD * h:HD * h + HD, :, HD * h:HD * h + HD],
                             I["cmp_w2"][0].rearrange("k d e -> d k e")).then_inc(w2_ld, 16)
            load_weights("w1k0")
            load_weights("w1k1")
            sp.wait_ge(*emptied(("fin",)))
            sp.dma_start(o_ssm_s[0].rearrange("q (s g) n r -> (q s) (g n r)", g=2),
                         fo.rearrange("p n r -> p (n r)")).then_inc(fin_out, 16)
            sp.dma_start(o_ssm_p[0, 0].rearrange("(s g) n r -> s (g n r)", g=2),
                         fo_p[:].rearrange("p n r -> p (n r)")).then_inc(fin_out, 16)

            sp.wait_ge(fin_out, 32)
            sp.wait_ge(glu_made, 8)
            sp.dma_start(caches[:, 1], I["cache_win_kv"][0].rearrange("s (h p) a b d -> p s h (a b d)", p=P)
                         ).then_inc(cache_ld, 16)
            for s in range(NSEQ):
                for u in range(2):
                    sp.dma_start(caches[:, 0, s, u, :],
                                 I["cache_slc_kv"][0, bass.ds(page(s, u), 1)].rearrange("o p a h d -> (o p) (a h d)")
                                 ).then_inc(cache_ld, 16)
            load_weights("so")
            load_weights("no")
            load_weights("wo0")

            def load_gates(m):
                sp.dma_start(gates[:, m % 4], tg_dram[m]).then_inc(tg_ld[m % 4], 16)
            sp.wait_ge(pe_done, PLAN.done(("vcs",)))
            for b in range(4):
                sp.wait_ge(tg_out[b], 16 * gates_out(b, 2 * KD))
            for m in range(4):
                load_gates(m)
            sp.wait_ge(pe_done, PLAN.done(("o", len(GROUPS) - 1)))
            sp.wait_ge(*emptied(("o", len(GROUPS) - 1)))
            for t in range(NT):
                rows((xp, xs), t, x).then_inc(x_res, 16)
            sp.dma_start(w_rt[:, :, 0:4], I["w_route_group"][0].rearrange("(k p) n -> p k n", p=P)).then_inc(rt_ld, 16)
            sp.dma_start(w_rt[:, :, 4:20], I["w_route_expert"][0].rearrange("(k p) n -> p k n", p=P)).then_inc(rt_ld, 16)
            sp.dma_start(b_rt[:, 0:4], I["b_route_group"].broadcast_to([P, 4])).then_inc(rt_ld, 16)
            sp.dma_start(b_rt[:, 4:20], I["b_route_expert"].broadcast_to([P, 16])).then_inc(rt_ld, 16)
            for m in range(4, KD):
                sp.wait_ge(merged_made, 2 * (m - 4) + 2)
                load_gates(m)
            load_weights("wo1")

            def load_gate_up(e, u):
                one = bass.ds(e, 1) if not isinstance(e, int) else slice(e, e + 1)
                sp.dma_start(wgu[:, u, :, :, :][:, 0], I["w_exp_gate"][0, one].rearrange("o (k p) n -> p (o k) n", p=P)).then_inc(gu_ld[u], 16)
                sp.dma_start(wgu[:, u, :, :, :][:, 1], I["w_exp_up"][0, one].rearrange("o (k p) n -> p (o k) n", p=P)).then_inc(gu_ld[u], 16)

            def load_down(e, u):
                one = bass.ds(e, 1) if not isinstance(e, int) else slice(e, e + 1)
                sp.dma_start(wdn[:, u], I["w_exp_down"][0, one].rearrange("o (k p) n -> p (o k) n", p=P)).then_inc(wd_ld[u], 16)
            for u in range(2):
                load_gate_up(u, u)
            sp.wait_ge(outs, n_outs)
            sp.dma_start(gf, I["final_norm_g"].rearrange("(o n) -> o n", o=1).broadcast_to([P, D])).then_inc(gf_ld, 16)
            sp.dma_start(p_in[:, 0:4], I["p_prompt"][0, 0].rearrange("(t p) n -> p t n", p=P)).then_inc(p_ld, 16)
            sp.dma_start(p_in[0:64, 4], I["p_sample"][0].rearrange("s q n -> (s q) n")).then_inc(p_ld, 16)
            load_weights("ple")
            sp.wait_ge(pe_done, PLAN.done(("wo", NT - 1, 1)))
            for u in range(2):
                load_down(u, u)
            load_weights("pg0")
            load_weights("pg1")
            sp.wait_ge(rounds_made, 1)
            rounds = sp.value_load(rounds_i[0:1, 0:1], min_val=1, max_val=MAXR)
            with sp.Fori(0, rounds) as j:
                sp.wait_ge(g_done, j * 16 + 1)
                load_gate_up(2, 0)
                with sp.Fori(0, NE // 2 - 2) as i:
                    for u in range(2):
                        sp.wait_ge(g_done, j * 16 + i * 2 + (u + 2))
                        load_gate_up(i * 2 + (u + 3), 1 - u)
                        sp.wait_ge(d_done, j * 32 + i * 4 + (2 * u + 2))
                        load_down(i * 2 + (u + 2), u)
                sp.wait_ge(g_done, j * 16 + (NE - 2))
                load_gate_up(NE - 1, 1)
                for u in range(2):
                    sp.wait_ge(d_done, j * 32 + (2 * NE - 6 + 2 * u))
                    load_down(NE - 2 + u, u)
                with sp.If(j + 1 < rounds):
                    sp.wait_ge(x2_made, j * NT + 2 * NT)
                    for u in range(2):
                        load_gate_up(u, u)
                        load_down(u, u)
            ysm = y_sample.rearrange("s q d -> (s q) d")
            for t in range(NT):
                sp.wait_ge(y_made, t + 1)
                dst = y_prompt[0][P * t:P * t + P, :] if t < 4 else ysm
                sp.dma_start(dst, x[0:TILES[t], t, :]).then_inc(outs, 16)
            sp.wait_ge(outs, n_outs + 16 * NT)

        @block.gpsimd
        def _(pool):
            count = [0]

            def link(ins):
                count[0] += 1
                ins.then_inc(pool_step, 1)
                pool.wait_ge(pool_step, count[0])

            link(pool.memset(ident[:], 0.0))
            link(pool.affine_select(out=ident[:], in_=ident[:], compare_op=ALU.not_equal, fill=1.0, base=0,
                                    pattern=[[-1, P]], channel_multiplier=1))
            pool.tensor_copy(ident_b[:], ident[:]).then_inc(consts, 1)
            link(pool.memset(causal[:], 0.0))
            pool.affine_select(out=causal[:], in_=causal[:], compare_op=ALU.is_ge, fill=NEG, base=0,
                               pattern=[[-1, P]], channel_multiplier=1).then_inc(consts, 1)
            link(pool.memset(halfneg[:], -0.5))
            link(pool.memset(zero_i[:], 0))
            pool.dma_start(list_dram.rearrange("(p n) o -> p (n o)", p=P), zero_i[:]).then_inc(list_zero, 16)
            pool.memset(ones_b[:], 1.0)
            link(pool.memset(tri_b[:], 0.0))
            link(pool.affine_select(out=tri_b[:], in_=tri_b[:], compare_op=ALU.is_ge, fill=1.0, base=0,
                                    pattern=[[-1, P]], channel_multiplier=1))
            pool.iota(ebase[:], [[CAP, NE]], base=0, channel_multiplier=0, allow_small_or_imprecise_dtypes=True)
            pool.iota(tokid[:], [[P, NT]], base=0, channel_multiplier=1).then_inc(consts, 1)

            def rstd(t, at):
                p = TILES[t]
                link(pool.tensor_scalar(stat[0:p, 1, t:t + 1], stat[0:p, 0, t:t + 1], 1.0 / D, EPS, ALU.mult, ALU.add))
                pool.tensor_tensor(stat[0:p, 2, t:t + 1], stat[0:p, 1, t:t + 1], halfneg[0:p], ALU.pow).then_inc(rstd_done, 1)

            for t in range(NT):
                pool.wait_ge(sq_done, t + 1)
                rstd(t, 0)

            pool.wait_ge(powers, 1)
            pool.wait_ge(*emptied(("c", 1)))
            n9 = [P, NS, CH + 1, GRP]
            pr = pw[:, :, 0, :].rearrange("p t s -> p s t").unsqueeze(3).broadcast_to(n9)
            pi = pw[:, :, 1, :].rearrange("p t s -> p s t").unsqueeze(3).broadcast_to(n9)
            cr = cst[:, 0].unsqueeze(2).broadcast_to(n9)
            ci = cst[:, 1].unsqueeze(2).broadcast_to(n9)
            tg9 = tmp_g.rearrange("p (s t c) -> p s t c", s=NS, t=CH + 1)
            link(pool.tensor_tensor(gm[:, 0], pr, cr, ALU.mult))
            link(pool.tensor_tensor(tg9, pi, ci, ALU.mult))
            link(pool.tensor_tensor(gm[:, 0], gm[:, 0], tg9, ALU.subtract))
            link(pool.tensor_tensor(gm[:, 1], pi, cr, ALU.mult))
            link(pool.tensor_tensor(tg9, pr, ci, ALU.mult))
            link(pool.tensor_tensor(gm[:, 1], gm[:, 1], tg9, ALU.add))
            pool.tensor_scalar(gm[:, 1], gm[:, 1], -1.0, None, ALU.mult).then_inc(g_made, 1)
            pool.wait_ge(pe_done, PLAN.done(("vt", 7)))
            pool.memset(vn_t[:], 0.0).then_inc(w_zero, 1)
            pool.wait_ge(pe_done, PLAN.done(("x", 4)))
            pool.wait_ge(par_ld, PARS)
            pool.tensor_tensor(uc, uc, d_b[:].unsqueeze(1).broadcast_to([NCH, CH, SSM_W]), ALU.mult).then_inc(ud_made, 1)
            pool.wait_ge(pe_done, PLAN.done(("gb", KD - 1, 1)))
            for n in range(NKV):
                lo, hi = HD * n, HD * (1 - n)
                for v in (w1(0), w1(1), w2):
                    pool.memset(v[lo:lo + HD, :, hi:hi + HD], 0.0).then_inc(w_cmp_zero, 1)
                pool.wait_ge(w_cmp_zero, 3 * (n + 1))
            pool.wait_ge(fin_out, 32)
            pool.wait_ge(glu_made, 8)
            link(pool.memset(cm01[:], 1.0))
            link(pool.affine_select(out=cm01[:], in_=cm01[:], compare_op=ALU.is_ge, fill=0.0, base=-(CL - 1),
                                    pattern=[[P, 4], [-CS, 32]], channel_multiplier=1))
            pool.tensor_scalar(cmneg[:], cm01[:], -NEG, NEG, ALU.mult, ALU.add)
            link(pool.memset(sel4[:], 1.0))
            link(pool.affine_select(out=sel4[:], in_=sel4[:], compare_op=ALU.is_ge, fill=0.0, base=0,
                                    pattern=[[-32, 4]], channel_multiplier=1))
            link(pool.affine_select(out=sel4[:], in_=sel4[:], compare_op=ALU.is_ge, fill=0.0, base=31,
                                    pattern=[[32, 4]], channel_multiplier=-1))
            link(pool.iota(rowi[:, 0:1], [[0, 1]], base=0, channel_multiplier=1))
            link(pool.iota(csneg[:, 0, :], [[1, 32]], base=0, channel_multiplier=0, allow_small_or_imprecise_dtypes=True))
            pool.iota(nmk[:, 0], [[-16, 4], [1, 64]], base=0, channel_multiplier=0,
                      allow_small_or_imprecise_dtypes=True).then_inc(masks, 1)
            pool.memset(vcbd[:], 0.0).then_inc(masks, 1)
            link(pool.memset(qpad[:], 0.0))
            pool.wait_ge(*emptied(("q", 3, 1)))
            for k in range(NKV):
                for par in range(2):
                    dstq = qpad[HD * k:HD * k + HD].rearrange("p (s two) n -> p s two n", two=2)[:, :, par,
                                64 * par + 32 * k:64 * par + 32 * k + 32].rearrange("p s (g q) -> p s g q", g=GQA)
                    srcq = qT[HD * k:HD * k + HD, :, NP_:ROWS].rearrange("p g (s two q) -> p s two g q", two=2, q=NDEC)[:, :, par]
                    pool.tensor_copy(dstq, srcq).then_inc(qpad_made, 1)
            pool.wait_ge(pe_done, PLAN.done(("o", len(GROUPS) - 1)))
            pool.wait_ge(*emptied(("o", len(GROUPS) - 1)))
            pool.iota(slot_no[:], [[1, P]], base=1, channel_multiplier=0, allow_small_or_imprecise_dtypes=True)
            pool.iota(row_f[:, 0], [[P, NT]], base=0, channel_multiplier=0, allow_small_or_imprecise_dtypes=True)
            link(pool.iota(row_f[:, 1], [[0, NT]], base=0, channel_multiplier=1, allow_small_or_imprecise_dtypes=True))
            pool.tensor_copy(row_b[:], row_f[:]).then_inc(slot_nos, 1)
            for t in range(NT):
                pool.wait_ge(sq_done, NT + t + 1)
                rstd(t, 1)
                pool.wait_ge(hn_made, NT + t + 1)
                pool.dma_start(h2_dram[P * t:P * t + TILES[t], :], hn[0:TILES[t], t % 2]).then_inc(h2_out[t % 2], 16)
            pool.wait_ge(h2_out[0], 16 * 3)
            pool.wait_ge(h2_out[1], 16 * 2)
            pool.wait_ge(pe_done, PLAN.done(("rt", NT - 1)))
            pool.wait_ge(*emptied(("first",)))
            for u in range(2):
                pool.indirect_dma_start(out=hg[:, u], out_offset=None, in_=h2_dram,
                                        in_offset=bass.IndirectOffsetOnAxis(idx[:, u:u + 1], 0)).then_inc(hg_ld[u], 16)
            pool.wait_ge(pos_made, 1)
            pool.wait_ge(list_zero, 16)
            for t in range(NT):
                for c in range(2):
                    pool.indirect_dma_start(
                        out=list_dram, out_offset=bass.IndirectOffsetOnAxis(pos_i[0:TILES[t], 0, c, t:t + 1], 0),
                        in_=tokid[0:TILES[t], t:t + 1], in_offset=None).then_inc(listed, 16)
            pool.memset(tick[:, 0:1], 0.0).then_inc(pool_tick, 1)

            def carry_waits(n):
                pool.wait_ge(pool_tick, n)
                pool.tensor_tensor(tick[:, 1:2], tick[:, 0:1], tick[:, 0:1], ALU.add).then_inc(pool_tick, 1)

            def gather_rows(first_slot, u, freed, loaded, tick_no):
                pool.wait_ge(hg_free[u], freed)
                pool.dma_start(idx[:, u:u + 1], list_dram[bass.ds(first_slot, CAP), :]).then_inc(idx_ld[u], 16)
                pool.wait_ge(idx_ld[u], loaded)
                carry_waits(tick_no)
                pool.indirect_dma_start(out=hg[:, u], out_offset=None, in_=h2_dram,
                                        in_offset=bass.IndirectOffsetOnAxis(idx[:, u:u + 1], 0)).then_inc(hg_ld[u], 16)

            pool.wait_ge(rounds_made, 1)
            rounds = pool.value_load(rounds_i[0:1, 0:1], min_val=1, max_val=MAXR)
            pool.wait_ge(listed, 16 * 2 * NT)
            ticks = NE + NT
            with pool.Fori(0, rounds) as j:
                with pool.Fori(0, NE // 2 - 1) as i:
                    for u in range(2):
                        gather_rows(i * (2 * MAXR * CAP) + j * CAP + (2 + u) * MAXR * CAP, u, j * 8 + i + 2,
                                    j * 128 + i * 16 + 16, j * ticks + i * 2 + (u + 1))
                pool.wait_ge(pos_made, j + 2)
                for u in range(2):
                    pool.wait_ge(ye_out[u], j * 128 + (128 + 16))
                for t in range(NT):
                    pool.wait_ge(x2_made, j * NT + (NT + max(t - 1, 0)))
                    carry_waits(j * ticks + (NE - 2 + t + 1))
                    for c in range(2):
                        pool.indirect_dma_start(out=yg[0:TILES[t], t % 2, c], out_offset=None, in_=ye_dram,
                                                in_offset=bass.IndirectOffsetOnAxis(pos_i[0:TILES[t], 1, c, t:t + 1], 0)
                                                ).then_inc(yg_ld[t % 2][c], 16)
                with pool.If(j + 1 < rounds):
                    for u in range(2):
                        gather_rows(j * CAP + (CAP + u * MAXR * CAP), u, j * 8 + 9, j * 128 + 128, j * ticks + (NE - 2 + NT + u + 1))
            for t in range(NT):
                pool.wait_ge(sq_done, 2 * NT + t + 1)
                rstd(t, 2)

        @block.tensor
        def _(pe):
            def begin(key):
                if PLAN.at[key] >= RING:
                    pe.wait_ge(*freed(key))
                return bank(key)

            def finish(ins):
                ins.then_inc(pe_done, 1)

            def product(out, pairs):
                for n, (a, b) in enumerate(pairs):
                    ins = pe.matmul(out, a, b, start=(n == 0), stop=(n == len(pairs) - 1))
                return ins

            pe.wait_ge(consts, 1)
            for t in range(NT):
                p = TILES[t]
                pe.wait_ge(hn_made, t + 1)
                for k in range(2):
                    o = begin(("hT", t, k))
                    for j in range(4):
                        ins = pe.transpose(o[:, j * P:j * P + p], x_in[0:p, t, (4 * k + j) * P:(4 * k + j + 1) * P], ident[0:p, 0:p])
                    finish(ins)
            for t in range(NT):
                p = TILES[t]
                o = begin(("u", t))
                pe.wait_ge(*emptied(("hT", t, 1)))
                pe.wait_ge(*w_need["u"])
                finish(product(o[0:p, :], [(hT[:, k, P * t:P * t + p], wk("u", 512)[:, k]) for k in range(KD)]))
            for t in range(NT):
                p = TILES[t]
                for c in range(2):
                    o = begin(("kv", t, c))
                    pe.wait_ge(*w_need[f"kv{c}"])
                    finish(product(o[0:p, 0:396], [(hT[:, k, P * t:P * t + p], wk(f"kv{c}", 396)[:, k]) for k in range(KD)]))
            pe.wait_ge(par_ld, PARS)
            o = begin(("lam",))
            pe.transpose(o[:, 0:NS], lam_r[:, 0, :], ident[0:NS, 0:NS])
            finish(pe.transpose(o[:, NS:2 * NS], lam_r[:, 1, :], ident[0:NS, 0:NS]))
            for r in range(2):
                o = begin(("c", r))
                for b in range(4):
                    ins = pe.transpose(o[:, P * b:P * b + P], c_r[:, r, b].rearrange("p u n -> p (u n)"), ident[:])
                finish(ins)
            o = begin(("h0",))
            h0v = h0_r[:].rearrange("p (n r) -> p r n", r=2)
            for r in range(2):
                ins = pe.transpose(o[:, P * r:P * r + P], h0v[:, r], ident[:])
            finish(ins)
            def gate_products(m):
                w = wk(f"g{m // 2}", 2 * P, 0, 2 * KD)
                pe.wait_ge(*w_need[f"g{m // 2}"])
                for h in range(2):
                    for at, key in enumerate(("ga", "gb")):
                        o = begin((key, m, h))
                        finish(product(o[:, 0:HALF], [(w[:, KD * at + k, P * (m % 2):P * (m % 2) + P],
                                                       hT[:, k, HALF * h:HALF * h + HALF]) for k in range(KD)]))
            for m in range(KD_A):
                gate_products(m)
            pe.wait_ge(ucg_made, 1)
            for i in range(5):
                o = begin(("x", i))
                for j, g in enumerate(range(7 * i, min(7 * i + 7, NG))):
                    ins = pe.transpose(o[:, NCH * j:NCH * j + NCH], ucg[:, g], ident[0:NCH, 0:NCH])
                finish(ins)
            for i in range(8):
                o = begin(("vt", i))
                for j in range(4):
                    q = 4 * i + j
                    ins = pe.transpose(o[:, P * j:P * j + P], vn[:, q // 2, q % 2], ident[:])
                finish(ins)
            for i in range(8):
                o = begin(("k", i))
                for j in range(4):
                    s, lo = 4 * (i // 2) + j, 64 * (i % 2)
                    ins = product(o[0:GRP, P * j:P * j + P],
                                  [(bbar[lo:lo + 64, r, s], gm[lo:lo + 64, r, s, 0:CH]) for r in range(2)])
                finish(ins)
            pe.wait_ge(*emptied(("x", 4)))
            pe.wait_ge(*emptied(("vt", 7)))
            for i in range(6):
                o = begin(("d", i))
                for s in range(3 * i, min(3 * i + 3, NS)):
                    for r in range(2):
                        at = ((s - 3 * i) * 2 + r) * NCH
                        for g2 in range(2):
                            ins = pe.matmul(o[64 * g2:64 * g2 + 64, at:at + NCH], vt[:, 2 * s + r, 64 * g2:64 * g2 + 64],
                                            xg[:, 2 * s + g2], start=True, stop=True)
                finish(ins)
            pe.wait_ge(*w_need["q"])
            for m in range(GQA):
                wq = wk("q", 512)[:, :, P * m:P * m + P]
                for h in range(2):
                    o = begin(("q", m, h))
                    finish(product(o[:, 0:HALF], [(wq[:, k], hT[:, k, HALF * h:HALF * h + HALF]) for k in range(KD)]))
            for m in range(KD_A, KD):
                gate_products(m)
            pe.wait_ge(walked, 1)
            pe.wait_ge(w_toep, 16 * CH)
            for i in range(8):
                o = begin(("y", i))
                for j in range(4):
                    s, lo = 4 * (i // 2) + j, 64 * (i % 2)
                    g = 2 * s + i % 2
                    ins = product(o[0:NCH, P * j:P * j + P],
                                  [(xg[:, g], wt[:, g])]
                                  + [(hst[lo:lo + 64, r, s], gm[lo:lo + 64, r, s, 1:CH + 1]) for r in range(2)])
                finish(ins)
            o = begin(("fin",))
            for r in range(2):
                pe.transpose(o[:, P * r:P * r + P], fin[:, r, 1:1 + NSEQ], ident[:])
            for r in range(2):
                ins = pe.transpose(o[0:NS, 256 + P * r:256 + P * r + P], fin[:, r, 0], ident[:])
            finish(ins)
            pe.wait_ge(y_gelu, 8)
            for t in range(CH):
                o = begin(("zg", t))
                for b in range(4):
                    ins = pe.transpose(o[:, NCH * b:NCH * b + NCH], uc[:, t, P * b:P * b + P], ident[0:NCH, 0:NCH])
                finish(ins)
            pe.wait_ge(*emptied(("zg", CH - 1)))
            pe.wait_ge(*w_need["glu"])
            for m in range(4):
                for h in range(2):
                    o = begin(("glu", m, h))
                    finish(product(o[:, 0:HALF], [(wk("glu", 512, k=4)[:, k, P * m:P * m + P],
                                                   zgT[:, k, HALF * h:HALF * h + HALF]) for k in range(4)]))
            o = begin(("pe",))
            pe.wait_ge(pe_ld, 32)
            finish(pe.transpose(o[:, 0:2 * CL], pe_r[:].rearrange("p u n -> p (u n)"), ident[0:64, 0:64]))
            for i in range(10):
                o = begin(("ct", i))
                if i >= 2:
                    pe.wait_ge(raw_ld[i - 2], 32)
                for u in range(2):
                    for k in range(2):
                        src = kv[:, 2 * i + u, P * k:P * k + P] if i < 2 else rawc[:, i - 2, u, P * k:P * k + P]
                        ins = pe.transpose(o[:, (2 * u + k) * P:(2 * u + k + 1) * P], src, ident[:])
                finish(ins)
            for r in range(2):
                o = begin(("ktp", r))
                for t in range(4):
                    ins = pe.transpose(o[:, P * t:P * t + P], kv[:, t, KVW * (r + 1):KVW * (r + 1) + P], ident[:])
                finish(ins)
            o = begin(("ktn",))
            for r in range(2):
                ins = pe.transpose(o[:, 64 * r:64 * r + 64], kv[0:64, 4, KVW * (r + 1):KVW * (r + 1) + P], ident[0:64, 0:64])
            finish(ins)
            pe.wait_ge(*emptied(("ct", 9)))
            pe.wait_ge(w2_ld, 16 * NKV)
            pe.wait_ge(w_cmp_zero, 3 * NKV)
            for k in range(2):
                o = begin(("pre", k))
                pe.wait_ge(*w_need[f"w1k{k}"])
                finish(product(o[:, 0:NBLK], [(w1(k)[:, i], kvct[:, k, i:i + CS * (NBLK - 1) + 1:CS]) for i in range(CL)]))
            o = begin(("kc",))
            pe.wait_ge(cmp_g, 1)
            finish(pe.matmul(o[:, 0:NBLK], w2[:, 0], cx[:, 0, 1], start=True, stop=True))
            o = begin(("vcp",))
            pe.wait_ge(cmp_g, 3)
            finish(pe.matmul(o[:, 0:P], cxr[:].rearrange("p g j -> p (g j)"), w2[:, 1],
                             start=True, stop=True))
            o = begin(("vcs",))
            for t in range(4):
                j = CJ_S + 2 * SJ * t
                if t < 3:
                    ins = pe.matmul(o[0:32, P * t:P * t + P], cx[:, 1, 1, j:j + 32], w2[:, 1], start=True, stop=True)
                else:
                    ins = pe.matmul(o[0:31, P * t:P * t + P], cx[:, 1, 1, j:j + 31], w2[:, 1], start=True, stop=True)
            finish(ins)

            pe.wait_ge(*emptied(("ktn",)))
            pe.wait_ge(consts, 2)
            pe.wait_ge(row_masks, 1)
            pe.wait_ge(qpad_made, 4)
            pe.wait_ge(*emptied(("vcs",)))
            for what, i in attention_steps():
                if what == "cached":
                    r, i = i // 4, i % 4
                    o = begin(("kts", r, i))
                    pe.wait_ge(cache_ld, 16 * 17)
                    for j in range(4):
                        ins = pe.transpose(o[:, P * j:P * j + P], caches[:, r, 2 * i + j // 2, j % 2, 0:P], ident[:])
                    finish(ins)
                    continue
                kind, b, r, h = ITEMS[i] if what in ("score", "turn", "value") else ITEMS[GROUPS[i][0]]
                kh, m = h // GQA, h % GQA
                lo = HD * kh
                if what == "score":
                    o = begin(("s", i))
                    if kind == "p":
                        n = P * (b + 1)
                        pe.matmul(o[:, 0:n], qT[lo:lo + HD, m, P * b:P * b + P], kt[lo:lo + HD, r - 1, 0:n], start=True, stop=False)
                        finish(pe.matmul(o[:, n - P:n], ident_b[:], causal[:], start=False, stop=True))
                    elif kind == "c":
                        for hh in range(NH):
                            if hh == GQA:
                                ins.then_inc(half_done, 1)
                                pe.wait_ge(half_done, b + 1)
                            l = HD * (hh // GQA)
                            ins = pe.matmul(o[:, 32 * hh:32 * hh + 32], qT[l:l + HD, hh % GQA, P * b:P * b + P],
                                            kc[l:l + HD, CJ_P:CJ_P + 32], start=True, stop=True)
                        finish(ins)
                    elif kind == "s":
                        pe.wait_ge(*emptied(("kts", 1, 3)))
                        product(o[:, 0:PAST], [(qpad[:, 2 * b + u], kts[:, r - 1, 2 * b + u]) for u in range(2)])
                        for u in range(2):
                            pe.matmul(o[:, PAST:PAST + 64], qpad[:, 2 * b + u], kt[:, r - 1, NP_:ROWS], start=(u == 0), stop=False)
                        finish(pe.matmul(o[:, PAST:PAST + 64], ident_b[:], new_mask[:, b], start=False, stop=True))
                    else:
                        j = CJ_S + 2 * SJ * b
                        n = min(32, NBLK - j)
                        finish(product(o[:, 0:n], [(qpad[:, 2 * b + u], kc[:, j:j + n]) for u in range(2)]))
                elif what == "turn":
                    o = begin(("t", i))
                    pe.wait_ge(*emptied(("s", i)))
                    if kind == "c":
                        pe.wait_ge(s_prob, b + 1)
                    at = 0
                    for c, n in enumerate(item_keys(ITEMS[i])):
                        ins = pe.transpose(o[0:n, P * c:P * c + P], pb[:, i % (T_LAG + 1), at:at + n], ident[:])
                        at += n
                    finish(ins)
                elif what == "value":
                    g = GROUP_OF[i]
                    pe.wait_ge(*emptied(("t", i)))
                    if g >= 2 and i == GROUPS[g][0]:
                        pe.wait_ge(s_gath, g - 1)
                    o = ps[:, RING + g % 2, :]
                    vcol = KVW * r + P
                    q = pt[:, i % (V_LAG - T_LAG + 1)]
                    if kind == "p":
                        ins = product(o[:, HD * h:HD * h + HD],
                                      [(q[:, P * c:P * c + P], kv[:, c, vcol + lo:vcol + lo + HD]) for c in range(b + 1)])
                    elif kind == "c":
                        for k in range(NKV):
                            ins = pe.matmul(o[:, 256 * k:256 * k + 256], q[:, P * k:P * k + P], vcbd[:, k], start=True, stop=True)
                    elif kind == "s":
                        ins = product(o[:, 0:256].rearrange("p (a n) -> p a n", a=2),
                                      [(q[:, P * c:P * c + P], caches[:, r - 1, 2 * b:2 * b + 2, c, P:KVW]) for c in range(2)]
                                      + [(q[0:64, 256:384], kv[0:64, 4, vcol:vcol + P].unsqueeze(1).broadcast_to([64, 2, P]))])
                    else:
                        ins = pe.matmul(o[:, 0:256].rearrange("p (a n) -> p a n", a=2), q[0:32, 0:P],
                                        vcs[0:32, b].unsqueeze(1).broadcast_to([32, 2, P]), start=True, stop=True)
                    ins.then_inc(s_val, 1)
                elif what == "out":
                    o = begin(("o", i))
                    if b < 4 and kind == "p":
                        pe.wait_ge(s_gath, i + 1)
                        pe.wait_ge(osd_made, b + 1)
                        for k in range(4):
                            ins = pe.transpose(o[:, P * k:P * k + P], ob[:, b % 2, P * k:P * k + P], ident[:])
                    else:
                        pe.wait_ge(osd_made, 4 + b + 1)
                        ins = pe.transpose(o[:, 0:P], osd[:, b % 2], ident[:])
                    finish(ins)

            pe.wait_ge(*emptied(("o", len(GROUPS) - 1)))
            pe.wait_ge(glu_made, 8)
            for m in range(KD):
                for h in range(2):
                    cut = slice(HALF * h, HALF * h + HALF)
                    for key, w, src in (("ab", "so", gluT), ("bb", "no", onsaT)):
                        o = begin((key, m, h))
                        pe.wait_ge(*w_need[w])
                        finish(product(o[:, 0:HALF], [(wk(w, D, 0, 4)[:, j, P * m:P * m + P], src[:, j, cut]) for j in range(4)]))
            pe.wait_ge(merged_made, 2 * KD)
            def through_w_o(t, c):
                p = TILES[t]
                o = begin(("wo", t, c))
                pe.wait_ge(*w_need[f"wo{c}"])
                finish(product(o[0:p, :], [(merged[:, k, P * t:P * t + p], wk(f"wo{c}", 512)[:, k]) for k in range(KD)]))

            def embedding_product(t, c):
                o = begin(("pp", t, c))
                finish(product(o[0:TILES[t], :], [(pT[:, k, P * t:P * t + TILES[t]], wk("ple", D, 0, 2)[:, k, 512 * c:512 * c + 512])
                                                  for k in range(2)]))
            for t in range(NT):
                through_w_o(t, 0)
            for what, t in second_norm_steps():
                p = TILES[t]
                if what == "wo":
                    through_w_o(t, 1)
                elif what == "h2T":
                    pe.wait_ge(hn_made, NT + t + 1)
                    for k in range(2):
                        o = begin(("h2T", t, k))
                        for j in range(4):
                            ins = pe.transpose(o[:, j * P:j * P + p], hn[0:p, t % 2, (4 * k + j) * P:(4 * k + j + 1) * P], ident[0:p, 0:p])
                        finish(ins)
                elif what == "rt":
                    o = begin(("rt", t))
                    pe.wait_ge(rt_ld, 64)
                    pe.wait_ge(*emptied(("h2T", t, 1)))
                    finish(product(o[0:p, 0:20], [(hT[:, k, P * t:P * t + p], w_rt[:, k]) for k in range(KD)]))
                elif what == "pT":
                    pe.wait_ge(p_ld, 32)
                    o = begin(("pT", t))
                    for j in range(2):
                        ins = pe.transpose(o[:, P * j:P * j + p], p_in[0:p, t, P * j:P * j + P], ident[0:p, 0:p])
                    finish(ins)
                elif what == "pp":
                    pe.wait_ge(*emptied(("pT", t)))
                    pe.wait_ge(*w_need["ple"])
                    for c in range(2):
                        embedding_product(t, c)
                elif what == "first":
                    pe.wait_ge(at_slots, 1)
                    o = begin(("first",))
                    for e in range(2):
                        ins = product(o[:, 2 * e:2 * e + 2],
                                      [(at_slot[0:TILES[q], e, q], row_b[0:TILES[q], :, q]) for q in range(NT)])
                    finish(ins)
                else:
                    pe.wait_ge(consts, 3)
                    pe.wait_ge(msk_made, 1)
                    o = begin(("rank",))
                    for t in range(NT):
                        p = TILES[t]
                        product(o[0:p, NE * t:NE * t + NE],
                                [(ones_b[:, 0:p], msk_b[:, q]) for q in range(t)] + [(tri_b[0:p, 0:p], msk_b[0:p, t])])
                    finish(product(o[:, NE * NT:NE * NT + NE],
                                   [(ones_b[0:TILES[q], :], msk_b[0:TILES[q], q]) for q in range(NT)]))

            pe.wait_ge(*emptied(("pp", NT - 2, 1)))
            pe.wait_ge(*emptied(("first",)))

            def turn_rows(j, n, u, half):
                pe.wait_ge(hg_ld[u], j * 128 + half * 16 + 16)
                pe.wait_ge(hgt_made, j * 32 + n * 2 + 2)
                for b in range(2):
                    for k in range(4):
                        ins = pe.transpose(ps[:, b, P * k:P * k + P], hg[:, u, (4 * b + k) * P:(4 * b + k + 1) * P], ident[:])
                    ins.then_inc(t_done, 1)
                pe.wait_ge(t_done, j * 32 + n * 2 + 2)
                pe.sem_inc(hg_free[u], 1)

            def gate_up(j, n, u, half):
                pe.wait_ge(gu_ld[u], j * 256 + half * 32 + 32)
                pe.wait_ge(hgt_made, j * 32 + n * 2 + 4)
                for w in range(2):
                    ins = product(ps[:, 2 + u, FF * w:FF * w + FF], [(hgT[:, u, k], wgu[:, u, w, k]) for k in range(KD)])
                ins.then_inc(g_done, 1)

            def turn_act(j, n, u):
                pe.wait_ge(act_made, j * 16 + n + 1)
                for f in range(2):
                    ins = pe.transpose(ps[:, 6 + u, P * f:P * f + P], si[:, u, P * f:P * f + P], ident[:])
                ins.then_inc(ta_done, 1)

            def down(j, n, u, half):
                pe.wait_ge(wd_ld[u], j * 128 + half * 16 + 16)
                pe.wait_ge(actt_made, j * 16 + n + 1)
                pe.wait_ge(d_taken, j * 32 + n * 2 + 2)
                for c in range(2):
                    ins = product(ps[:, 4 + c, :], [(actT[:, u, f], wdn[:, u, f, 512 * c:512 * c + 512]) for f in range(2)])
                    ins.then_inc(d_done, 1)

            pe.wait_ge(rounds_made, 1)
            rounds = pe.value_load(rounds_i[0:1, 0:1], min_val=1, max_val=MAXR)
            with pe.Fori(0, rounds) as j:
                turn_rows(j, 0, 0, 0)
                gate_up(j, 0, 0, 0)
                turn_rows(j, 1, 1, 0)
                turn_act(j, 0, 0)
                with pe.Fori(0, NE // 2 - 1) as i:
                    gate_up(j, i * 2 + 1, 1, i)
                    turn_rows(j, i * 2 + 2, 0, i + 1)
                    down(j, i * 2, 0, i)
                    turn_act(j, i * 2 + 1, 1)
                    gate_up(j, i * 2 + 2, 0, i + 1)
                    turn_rows(j, i * 2 + 3, 1, i + 1)
                    down(j, i * 2 + 1, 1, i)
                    turn_act(j, i * 2 + 2, 0)
                gate_up(j, NE - 1, 1, NE // 2 - 1)
                down(j, NE - 2, 0, NE // 2 - 1)
                turn_act(j, NE - 1, 1)
                down(j, NE - 1, 1, NE // 2 - 1)
            pe.wait_ge(d_taken, rounds * 32 + 2)

            for what, t, c in embedding_steps():
                p = TILES[t]
                if what == "product":
                    embedding_product(t, c)
                elif what == "turn":
                    if t < NT - 1:
                        pe.wait_ge(x2_made, rounds * NT + (t + 1))
                    for k in range(2):
                        o = begin(("x2T", t, k))
                        for j in range(4):
                            ins = pe.transpose(o[:, j * P:j * P + p], x[0:p, t, (4 * k + j) * P:(4 * k + j + 1) * P], ident[0:p, 0:p])
                        finish(ins)
                else:
                    o = begin(("pg", t, c))
                    if (t, c) == (NT - 2, 0):
                        pe.wait_ge(x2_made, rounds * NT + NT)
                    pe.wait_ge(*w_need[f"pg{c}"])
                    pe.wait_ge(*emptied(("x2T", t, 1)))
                    finish(product(o[0:p, :], [(hT[:, k, P * t:P * t + p], wk(f"pg{c}", 512)[:, k]) for k in range(KD)]))


        def turn(eng, i, copy, take, empty):
            kind, b = ITEMS[i][0], ITEMS[i][1]
            o = take(("t", i))
            if i > V_LAG - T_LAG:
                eng.wait_ge(s_val, i - (V_LAG - T_LAG))
            q = pt[:, i % (V_LAG - T_LAG + 1)]
            if kind == "s":
                copy(q[:, 0:256], o[:, 0:256])
                empty(copy(q[0:64, 256:384], o[0:64, 256:384]))
            elif kind == "sc":
                empty(copy(q[0:32, 0:P], o[0:32, 0:P]))
            else:
                n = P * len(item_keys(ITEMS[i]))
                empty(copy(q[:, 0:n], o[:, 0:n]))

        def turned_norm(dve, t, key, which, take, empty):
            p = TILES[t]
            for k in range(2):
                o = take(key + (k,))
                empty(dve.tensor_tensor(hT[:, 4 * k:4 * k + 4, P * t:P * t + p], o.rearrange("p (k n) -> p k n", k=4)[:, :, 0:p],
                                        g_cols[:, which, 4 * k:4 * k + 4].unsqueeze(2).broadcast_to([P, 4, p]), ALU.mult))

        def router_logits(dve, t, take, empty):
            p = TILES[t]
            o = take(("rt", t))
            empty(dve.tensor_tensor(lg[0:p, t], o[0:p, 0:20], b_rt[0:p], ALU.add))

        @block.scalar
        def _(act):
            def col(ap, n):
                return ap.rearrange("(k p) -> p k", p=P)

            act.dma_start(g_cols[:, 0], col(I["norm1_g"][0], KD), allow_slow_non_contiguous=True).then_inc(gains_ld, 16)
            act.dma_start(g_cols[:, 1], col(I["norm2_g"][0], KD), allow_slow_non_contiguous=True).then_inc(gains_ld, 16)

            def take(key):
                act.wait_ge(pe_done, PLAN.done(key))
                return bank(key)

            def empty(ins):
                ins.then_inc(drained["act"], 1)

            def copy(key, dst, src):
                empty(act.activation(dst, src, ACT.Copy))

            junk = flat(gluT)
            for t in range(NT):
                act.wait_ge(x_ld[t], 16)
                p = TILES[t]
                act.activation(junk[0:p, 0:D], x_in[0:p, t], ACT.Square, accum_out=stat[0:p, 0, t:t + 1]).then_inc(sq_done, 1)
                act.wait_ge(sq_done, t + 1)
            act.dma_start(ldt[0:64, :], I["ssm_log_dt"].rearrange("o (s g) -> o g s", g=2)[:, 0].broadcast_to([64, NS]),
                          allow_slow_non_contiguous=True).then_inc(par_ld, 16)
            act.dma_start(ldt[64:P, :], I["ssm_log_dt"].rearrange("o (s g) -> o g s", g=2)[:, 1].broadcast_to([64, NS]),
                          allow_slow_non_contiguous=True).then_inc(par_ld, 16)
            for r, name in enumerate(("ssm_lam_re", "ssm_lam_im")):
                act.dma_start(lam_r[:, r, :], I[name][0].rearrange("(s g) n -> s (g n)", g=2)).then_inc(par_ld, 16)
            for r, name in enumerate(("ssm_b_re", "ssm_b_im")):
                act.dma_start(b_r[:, r], I[name][0].rearrange("(s g) n c -> (g n) s c", g=2)).then_inc(par_ld, 16)
            for r, name in enumerate(("ssm_c_re", "ssm_c_im")):
                for u in range(2):
                    act.dma_start(c_r[:, r, :, u], I[name][0].rearrange("(b g) c n -> (g c) b n", b=4)).then_inc(par_ld, 16)
            act.dma_start(h0_r[:], I["state_ssm"][0].rearrange("q (s g) n r -> (q s) (g n r)", g=2)).then_inc(par_ld, 16)
            act.dma_start(d_b[:], I["ssm_d"].broadcast_to([NCH, SSM_W])).then_inc(par_ld, 16)
            act.dma_start(b_glu[:], col(I["b_glu"][0], 4), allow_slow_non_contiguous=True).then_inc(par_ld, 16)
            act.dma_start(ptab[:], I["page_table"].rearrange("(o s) u -> o (s u)", o=1)).then_inc(pt_ld, 16)
            for t in range(NT):
                o = take(("u", t))
                p = TILES[t]
                copy(None, u_rows[0:p, t], o[0:p, :])
            for t in range(NT):
                p = TILES[t]
                for c in range(2):
                    o = take(("kv", t, c))
                    copy(None, kv[0:p, t, 396 * c:396 * c + 396], o[0:p, 0:396])
            act.wait_ge(par_ld, PARS)
            act.activation(sm[:, 2], ldt[:], ACT.Exp).then_inc(dt_done, 1)
            act.wait_ge(drained["act"], PLAN.by[("kv", NT - 1, 1)][1])
            for t in range(NT):
                p = TILES[t]
                act.activation(tgate[0:p, t], kv[0:p, t, 3 * KVW:], ACT.Tanh, scale=0.5).then_inc(gates_made, 1)
            act.wait_ge(angles, 1)
            act.activation(sm[:, 8], sm[:, 3], ACT.Exp)
            act.activation(sm[:, 9], sm[:, 6], ACT.Sin)
            act.activation(sm[:, 10], sm[:, 7], ACT.Sin).then_inc(trig, 1)

            def take_gates(m, stage):
                for h in range(2):
                    n = 2 * m + h
                    if gates_out(n % 4, n):
                        act.wait_ge(tg_out[n % 4], 16 * gates_out(n % 4, n))
                    for w, key in enumerate(("ga", "gb")):
                        o = take((key, m, h))
                        empty(act.activation(stage[:, n % 4, w], o[:, 0:HALF], ACT.Tanh, scale=0.5))
                    act.wait_ge(*emptied(("gb", m, h)))
                    act.dma_start(tg_dram[m][:, :, HALF * h:HALF * h + HALF], stage[:, n % 4]).then_inc(tg_out[n % 4], 16)
            act.wait_ge(u_out, 16 * NT)
            for m in range(KD_A):
                take_gates(m, stage_a)
            for i in range(8):
                o = take(("vt", i))
                copy(None, vt[:, 4 * i:4 * i + 4].rearrange("p a b -> p (a b)"), o)
            for i in range(8):
                o = take(("k", i))
                if i >= 2:
                    act.wait_ge(k_out[i % 2], 16 * (i // 2))
                copy(None, ks[:, i % 2].rearrange("p g n -> p (g n)"), o[0:GRP, :])
            act.wait_ge(*emptied(("h0",)))
            for i in range(6):
                o = take(("d", i))
                s0, s1 = 3 * i, min(3 * i + 3, NS)
                n = s1 - s0
                v = o[:, 0:n * 2 * NCH].rearrange("p (s r c) -> p r s c", s=n, r=2)
                for r in range(2):
                    act.activation(hst[:, r, s0:s1, 1:NPC], v[:, r, :, 0:NPC - 1], ACT.Copy)
                    ins = act.activation(fin[:, r, :, s0:s1].rearrange("p c s -> p s c"), v[:, r, :, NPC - 1:NCH], ACT.Copy)
                empty(ins)
            for m in range(GQA):
                for h in range(2):
                    o = take(("q", m, h))
                    empty(act.activation(qT[:, m, HALF * h:HALF * h + HALF], o[:, 0:HALF], ACT.Copy, scale=SCALE))
            act.wait_ge(pe_done, PLAN.done(("x", 4)))
            for m in range(KD_A, KD):
                take_gates(m, stage_b)
            for i in range(8):
                act.wait_ge(*emptied(("y", i)))
                v = uc.rearrange("p t (b j g c) -> p t b g j c", b=4, j=4, g=2)[:, :, i // 2, i % 2]
                act.activation(v, v, GELU).then_inc(y_gelu, 1)
            o = take(("fin",))
            act.activation(fo.rearrange("p n r -> p r n"), o[:, 0:2 * P].rearrange("p (r n) -> p r n", r=2), ACT.Copy)
            copy(None, fo_p[:].rearrange("p n r -> p r n"), o[0:NS, 2 * P:4 * P].rearrange("p (r n) -> p r n", r=2))
            act.wait_ge(bglu_half, 1)
            for b in range(4):
                act.wait_ge(tg_out[b], 16 * gates_out(b, 2 * KD))
            for m in range(4):
                for h in range(2):
                    o = take(("glu", m, h))
                    empty(act.activation(gluT[:, m, HALF * h:HALF * h + HALF], o[:, 0:HALF], ACT.Tanh,
                                         bias=stat[:, 3, m:m + 1], scale=0.5))
            act.wait_ge(glu_made, 8)
            act.wait_ge(fin_out, 32)
            o = take(("pe",))
            copy(None, kvct[:, :, 0:CL], o[:, 0:2 * CL].rearrange("p (k i) -> p k i", k=2))
            for i in range(10):
                o = take(("ct", i))
                at = CT0 + 2 * P * i
                copy(None, kvct[:, :, at:at + 2 * P].rearrange("p k (u n) -> p u k n", u=2), o.rearrange("p (u k n) -> p u k n", u=2, k=2))
            for r in range(2):
                o = take(("ktp", r))
                copy(None, kt[:, r, 0:NP_], o)
            o = take(("ktn",))
            copy(None, kt[:, :, NP_:ROWS], o[:, 0:P].rearrange("p (r n) -> p r n", r=2))
            for k in range(2):
                act.wait_ge(*emptied(("pre", k)))
                act.activation(cx[:, k, 1], cx[:, k, 0], GELU).then_inc(cmp_g, 1)
            act.activation(cxr[:], cx[:, 1, 0, CJ_P:CJ_P + 32].unsqueeze(1).broadcast_to([P, 4, 32]), GELU).then_inc(cmp_g, 1)
            for what, i in attention_steps():
                if what == "score":
                    kind = ITEMS[i][0]
                    o = take(("s", i))
                    n = sum(item_keys(ITEMS[i]))
                    if i > T_LAG:
                        act.wait_ge(pe_done, PLAN.done(("t", i - T_LAG - 1)))
                    act.wait_ge(s_max, i + 1)
                    if kind == "c":
                        empty(act.activation(pb[:, i % (T_LAG + 1), 0:n], sct[:, 0:n], ACT.Exp))
                    elif kind == "sc":
                        empty(act.activation(pb[:, i % (T_LAG + 1), 0:n], sct[:, 0:n], ACT.Exp, bias=nm[:, i:i + 1], accum_out=rs[:, i:i + 1]))
                    else:
                        empty(act.activation(pb[:, i % (T_LAG + 1), 0:n], o[:, 0:n], ACT.Exp, bias=nm[:, i:i + 1], accum_out=rs[:, i:i + 1]))
                elif what == "cached":
                    o = take(("kts", i // 4, i % 4))
                    copy(None, kts[:, i // 4, 2 * (i % 4):2 * (i % 4) + 2].rearrange("p s n -> p (s n)"), o)
                elif what == "turn" and i % 2 == 0:
                    turn(act, i, lambda d, s: act.activation(d, s, ACT.Copy), take, empty)
            for t in range(NT):
                p = TILES[t]
                act.wait_ge(*emptied(("wo", t, 1)))
                if t == 0:
                    act.wait_ge(pe_done, PLAN.done(("bb", KD - 1, 1)))
                act.activation(junk[0:p, 0:D], x[0:p, t], ACT.Square, accum_out=stat[0:p, 0, t:t + 1]).then_inc(sq_done, 1)
                act.wait_ge(sq_done, NT + t + 1)

            def take_product(t, c):
                if t >= 3:
                    act.wait_ge(pe_done, PLAN.done(("h2T", t, 1)))
                    act.wait_ge(h2_out[t % 2], 16 * (t // 2 + 1))
                o = take(("pp", t, c))
                copy(None, pps[t][0:TILES[t], 512 * c:512 * c + 512], o[0:TILES[t], :])
            for what, t in second_norm_steps():
                p = TILES[t]
                if what == "pT":
                    o = take(("pT", t))
                    copy(None, pT[:, :, P * t:P * t + p], o[:, 0:2 * P].rearrange("p (k n) -> p k n", k=2)[:, :, 0:p])
                elif what == "pp":
                    for c in range(2):
                        take_product(t, c)
                elif what == "rank":
                    act.wait_ge(lg_made, 1)
                    act.activation(r16[:, :, 0:5], r16[:, :, 0:5], ACT.Exp).then_inc(lg_exp, 1)

            act.wait_ge(rounds_made, 1)
            rounds = act.value_load(rounds_i[0:1, 0:1], min_val=1, max_val=MAXR)
            act.wait_ge(pe_done, PLAN.done(("bb", KD - 1, 1)))
            for u in range(2):
                act.sem_inc(ye_out[u], 16)
            act.sem_inc(d_taken, 2)

            def tanh(j, n, u):
                act.wait_ge(g_done, j * 16 + n + 1)
                act.activation(th[:, u], ps[:, 2 + u, 0:FF], ACT.Tanh, scale=0.5).then_inc(th_made, 1)

            def take_act(j, n, u):
                act.wait_ge(ta_done, j * 16 + n + 1)
                act.activation(actT[:, u].rearrange("p f n -> p (f n)"), ps[:, 6 + u, 0:2 * P], ACT.Copy).then_inc(actt_made, 1)

            def take_down(j, n, u, half):
                act.wait_ge(ye_out[u], j * 128 + half * 16 + 16)
                for c in range(2):
                    act.wait_ge(d_done, j * 32 + n * 2 + (c + 1))
                    act.activation(ysb[:, u, 512 * c:512 * c + 512], ps[:, 4 + c, :], ACT.Copy).then_inc(d_taken, 1)
                act.wait_ge(d_taken, j * 32 + n * 2 + 4)
                act.dma_start(ye_dram[bass.ds(n * CAP, CAP), :], ysb[:, u]).then_inc(ye_out[u], 16)

            with act.Fori(0, rounds) as j:
                act.wait_ge(x2_made, j * NT + NT)
                tanh(j, 0, 0)
                take_act(j, 0, 0)
                with act.Fori(0, NE // 2 - 1) as i:
                    tanh(j, i * 2 + 1, 1)
                    take_down(j, i * 2, 0, i)
                    take_act(j, i * 2 + 1, 1)
                    tanh(j, i * 2 + 2, 0)
                    take_down(j, i * 2 + 1, 1, i)
                    take_act(j, i * 2 + 2, 0)
                tanh(j, NE - 1, 1)
                take_down(j, NE - 2, 0, NE // 2 - 1)
                take_act(j, NE - 1, 1)
                take_down(j, NE - 1, 1, NE // 2 - 1)

            def last_squares(t):
                act.wait_ge(x3_made, 2 * t + 2)
                act.activation(yg[0:TILES[t], 0, 0], x[0:TILES[t], t], ACT.Square, accum_out=stat[0:TILES[t], 0, t:t + 1]).then_inc(sq_done, 1)
                act.wait_ge(sq_done, 2 * NT + t + 1)
            for what, t, c in embedding_steps():
                p = TILES[t]
                if what == "product":
                    take_product(t, c)
                elif what == "turn":
                    for k in range(2):
                        o = take(("x2T", t, k))
                        copy(None, hT[:, 4 * k:4 * k + 4, P * t:P * t + p], o.rearrange("p (k n) -> p k n", k=4)[:, :, 0:p])
                else:
                    o = take(("pg", t, c))
                    if 2 * t + c >= 2:
                        act.wait_ge(x3_made, 2 * t + c - 1)
                    empty(act.activation(tpg[0:p, c], o[0:p, :], ACT.Tanh, scale=0.5))
                    if t and c == 0:
                        last_squares(t - 1)
            last_squares(NT - 1)

        @block.vector
        def _(dve):
            count = [0]

            def link(ins):
                count[0] += 1
                ins.then_inc(dve_step, 1)
                dve.wait_ge(dve_step, count[0])

            def tt(out, a, b, op):
                return dve.tensor_tensor(out, a, b, op)

            def take(key):
                dve.wait_ge(pe_done, PLAN.done(key))
                return bank(key)

            def empty(ins):
                ins.then_inc(drained["dve"], 1)

            dve.wait_ge(gains_ld, 32)
            for t in range(NT):
                p = TILES[t]
                dve.wait_ge(rstd_done, t + 1)
                dve.tensor_scalar(x_in[0:p, t], x_in[0:p, t], stat[0:p, 2, t:t + 1], None, ALU.mult).then_inc(hn_made, 1)
            for t in range(NT):
                turned_norm(dve, t, ("hT", t), 0, take, empty)
            dve.wait_ge(pe_done, PLAN.done(("hT", NT - 1, 1)))
            link(dve.memset(stat[:, 3, 0:4], 0.0))
            dve.wait_ge(par_ld, PARS)
            dve.tensor_scalar(stat[:, 3, 0:4], b_glu[:], 0.5, None, ALU.mult).then_inc(bglu_half, 1)
            o = take(("lam",))
            empty(dve.tensor_copy(sm[:, 0:2], o[:, 0:2 * NS].rearrange("p (r s) -> p r s", r=2)))
            lr, li, dt, er, an, kk, ra, rb, mg, sn, cs, den, t0, t1, cr, ci, a1 = (sm[:, j] for j in range(17))
            dve.wait_ge(*emptied(("lam",)))
            dve.wait_ge(dt_done, 1)
            two_pi = 2.0 * math.pi
            hi = 6.28125
            magic = 1.5 * 2.0 ** 23
            tt(er, lr, dt, ALU.mult)
            link(tt(an, li, dt, ALU.mult))
            link(dve.tensor_scalar(kk, an, 1.0 / two_pi, magic, ALU.mult, ALU.add))
            link(dve.tensor_scalar(kk, kk, -magic, None, ALU.add))
            link(dve.scalar_tensor_tensor(ra, kk, -hi, an, ALU.mult, ALU.add))
            link(dve.scalar_tensor_tensor(ra, kk, -(two_pi - hi), ra, ALU.mult, ALU.add))
            link(dve.tensor_scalar(t0, ra, math.pi / 2, -two_pi, ALU.is_gt, ALU.mult))
            link(dve.scalar_tensor_tensor(rb, ra, math.pi / 2, t0, ALU.add, ALU.add))
            link(dve.tensor_scalar(ra, ra, 3.1415925, -3.1415925, ALU.min, ALU.max))
            dve.tensor_scalar(rb, rb, 3.1415925, -3.1415925, ALU.min, ALU.max).then_inc(angles, 1)
            for r in range(2):
                o = take(("c", r))
                v = o.rearrange("p (s g c) -> p s g c", g=2, c=GRP)
                dve.tensor_copy(cst[0:64, r], v[0:64, :, 0])
                empty(dve.tensor_copy(cst[64:P, r], v[64:P, :, 1]))
            o = take(("h0",))
            dve.memset(hst[:, :, :, 0:1], 0.0)
            empty(dve.tensor_copy(hst[:, :, :, NPC:NCH].rearrange("p r s q -> p r q s"),
                                  o[:, 0:2 * P].rearrange("p (r q s) -> p r q s", r=2, q=NSEQ)))
            dve.wait_ge(trig, 1)
            dve.memset(pw[:, 0, 0], 1.0)
            dve.memset(pw[:, 0, 1], 0.0)
            tt(pw[:, 1, 0], mg, cs, ALU.mult)
            link(tt(pw[:, 1, 1], mg, sn, ALU.mult))
            for m in (1, 2, 4):
                a_r, a_i = pw[:, 1:m + 1, 0], pw[:, 1:m + 1, 1]
                b_re = pw[:, m:m + 1, 0].broadcast_to([P, m, NS])
                b_im = pw[:, m:m + 1, 1].broadcast_to([P, m, NS])
                u0 = tmp_v[:, 0:m * NS].rearrange("p (m s) -> p m s", m=m)
                u1 = tmp_v[:, 64:64 + m * NS].rearrange("p (m s) -> p m s", m=m)
                tt(u0, a_i, b_im, ALU.mult)
                tt(u1, a_i, b_re, ALU.mult)
                tt(pw[:, m + 1:2 * m + 1, 0], a_r, b_re, ALU.mult)
                link(tt(pw[:, m + 1:2 * m + 1, 1], a_r, b_im, ALU.mult))
                tt(pw[:, m + 1:2 * m + 1, 0], pw[:, m + 1:2 * m + 1, 0], u0, ALU.subtract)
                link(tt(pw[:, m + 1:2 * m + 1, 1], pw[:, m + 1:2 * m + 1, 1], u1, ALU.add))
            dve.tensor_copy(pwr[:, 0], pw[:, CH - 1]).then_inc(powers, 1)
            for j in range(1, CH):
                dve.tensor_copy(pwr[:, j], pw[:, CH - 1 - j])
            link(dve.tensor_scalar(a1, pw[:, 1, 0], -1.0, None, ALU.add))
            tt(t0, lr, lr, ALU.mult)
            link(tt(t1, li, li, ALU.mult))
            link(tt(den, t0, t1, ALU.add))
            link(dve.reciprocal(den, den))
            tt(t0, a1, lr, ALU.mult)
            link(tt(t1, pw[:, 1, 1], li, ALU.mult))
            link(tt(t0, t0, t1, ALU.add))
            link(tt(cr, t0, den, ALU.mult))
            tt(t0, pw[:, 1, 1], lr, ALU.mult)
            link(tt(t1, a1, li, ALU.mult))
            link(tt(t0, t0, t1, ALU.subtract))
            link(tt(ci, t0, den, ALU.mult))
            sc = [P, NS, GRP]
            crb, cib = cr.unsqueeze(2).broadcast_to(sc), ci.unsqueeze(2).broadcast_to(sc)
            u0 = tmp_v[:, 0:NS * GRP].rearrange("p (s c) -> p s c", s=NS)
            tt(bbar[:, 0], b_r[:, 0], crb, ALU.mult)
            link(tt(u0, b_r[:, 1], cib, ALU.mult))
            tt(bbar[:, 0], bbar[:, 0], u0, ALU.subtract)
            link(tt(bbar[:, 1], b_r[:, 1], crb, ALU.mult))
            link(tt(u0, b_r[:, 0], cib, ALU.mult))
            link(tt(bbar[:, 1], bbar[:, 1], u0, ALU.add))
            n8 = [P, NS, CH, GRP]
            u8 = tmp_v[:, 0:NS * CH * GRP].rearrange("p (s t c) -> p s t c", s=NS, t=CH)
            qr, qi = (pwr[:, :, r].rearrange("p t s -> p s t").unsqueeze(3).broadcast_to(n8) for r in range(2))
            br8, bi8 = (bbar[:, r].unsqueeze(2).broadcast_to(n8) for r in range(2))
            v8 = [vn[:, :, r].rearrange("p s (t c) -> p s t c", t=CH) for r in range(2)]
            tt(v8[0], qr, br8, ALU.mult)
            link(tt(u8, qi, bi8, ALU.mult))
            link(tt(v8[0], v8[0], u8, ALU.subtract))
            tt(v8[1], qr, bi8, ALU.mult)
            link(tt(u8, qi, br8, ALU.mult))
            tt(v8[1], v8[1], u8, ALU.add).then_inc(v_made, 1)
            dve.wait_ge(gates_made, NT)
            dve.tensor_scalar(tgate[:, 0:4], tgate[:, 0:4], 1.0, None, ALU.add).then_inc(gates_made, 1)
            dve.tensor_scalar(tgate[0:64, 4], tgate[0:64, 4], 1.0, None, ALU.add).then_inc(gates_made, 1)
            dve.wait_ge(uc_ld, 16)
            dve.tensor_copy(ucg.rearrange("p g (t c) -> p g t c", t=CH), uc.rearrange("p t (g c) -> p g t c", g=NG)
                            ).then_inc(ucg_made, 1)
            for b in range(4):
                dve.wait_ge(tg_out[b], 16 * gates_out(b, 2 * KD_A))
            for i in range(5):
                o = take(("x", i))
                n = min(7, NG - 7 * i)
                empty(dve.tensor_copy(xg[:, 7 * i:7 * i + n].rearrange("p g n -> p (g n)"), o[:, 0:n * NCH]))
            dve.wait_ge(*emptied(("d", 5)))
            dve.wait_ge(*emptied(("h0",)))
            link(dve.tensor_scalar(walk[:, 0, 0], pw[:, CH, 0], 1.0, None, ALU.mult))
            link(dve.tensor_scalar(walk[:, 0, 1], pw[:, CH, 0], 1.0, None, ALU.mult))
            link(dve.tensor_scalar(walk[:, 1, 0], pw[:, CH, 1], -1.0, None, ALU.mult))
            link(dve.tensor_scalar(walk[:, 1, 1], pw[:, CH, 1], 1.0, None, ALU.mult))
            before = count[0]
            with dve.Fori(0, NPC - 1) as c:
                now, nxt = bass.ds(c, 1), bass.ds(c + 1, 1)
                dve.tensor_tensor(walk[:, 2].unsqueeze(3), walk[:, 0].unsqueeze(3), hst[:, :, :, now], ALU.mult)
                dve.tensor_tensor(walk[:, 3, 0].unsqueeze(2), walk[:, 1, 0].unsqueeze(2), hst[:, 1, :, now], ALU.mult)
                dve.tensor_tensor(walk[:, 3, 1].unsqueeze(2), walk[:, 1, 1].unsqueeze(2), hst[:, 0, :, now], ALU.mult
                                   ).then_inc(dve_step, 1)
                dve.wait_ge(dve_step, c * 3 + (before + 1))
                dve.tensor_tensor(walk[:, 2], walk[:, 2], walk[:, 3], ALU.add).then_inc(dve_step, 1)
                dve.wait_ge(dve_step, c * 3 + (before + 2))
                dve.tensor_tensor(hst[:, :, :, nxt], hst[:, :, :, nxt], walk[:, 2].unsqueeze(3), ALU.add
                                   ).then_inc(dve_step, 1)
                dve.wait_ge(dve_step, c * 3 + (before + 3))
            count[0] = before + 3 * (NPC - 1)
            nine = [P, 1 + NSEQ, NS]
            hv = [hst[:, r, :, NPC - 1:NCH].rearrange("p s c -> p c s") for r in range(2)]
            a8 = [pw[:, CH, r].unsqueeze(1).broadcast_to(nine) for r in range(2)]
            t9 = [tmp9[:, j] for j in range(2)]
            for r, (p0, p1, op) in enumerate(((0, 1, ALU.subtract), (1, 0, ALU.add))):
                dve.tensor_tensor(t9[0], hv[p0], a8[0], ALU.mult)
                link(dve.tensor_tensor(t9[1], hv[p1], a8[1], ALU.mult))
                link(dve.tensor_tensor(t9[0], t9[0], t9[1], op))
                if r == 0:
                    link(dve.tensor_tensor(fin[:, 0], fin[:, 0], t9[0], ALU.add))
                else:
                    dve.tensor_tensor(fin[:, 1], fin[:, 1], t9[0], ALU.add).then_inc(walked, 1)

            dve.wait_ge(ud_made, 1)
            for i in range(8):
                o = take(("y", i))
                v = uc.rearrange("p t (b j g c) -> p t b g j c", b=4, j=4, g=2)[:, :, i // 2, i % 2]
                empty(tt(v, o[0:NCH, :].rearrange("p (g t c) -> p t g c", g=4, t=CH), v, ALU.add))
            for t in range(CH):
                o = take(("zg", t))
                empty(dve.tensor_copy(zgT.rearrange("p k (c t) -> p k c t", t=CH)[:, :, :, t],
                                      o[:, 0:4 * NCH].rearrange("p (k c) -> p k c", k=4)))
            dve.wait_ge(*emptied(("zg", CH - 1)))
            for m in range(4):
                for h in range(2):
                    cut = slice(HALF * h, HALF * h + HALF)
                    dve.wait_ge(*emptied(("glu", m, h)))
                    dve.scalar_tensor_tensor(gluT[:, m, cut], gluT[:, m, cut], 1.0, zgT[:, m, cut], ALU.add, ALU.mult
                                             ).then_inc(glu_made, 1)
            dve.wait_ge(glu_made, 8)
            dve.wait_ge(fin_out, 32)
            dve.wait_ge(masks, 1)
            link(dve.tensor_scalar(rowi[:, 1:2], rowi[:, 0:1], 7, None, ALU.bitwise_and))
            link(dve.tensor_scalar(rowi[:, 2:3], rowi[:, 0:1], 6, None, ALU.logical_shift_right))
            dve.tensor_copy(rowf[:, 0:1], rowi[:, 1:2])
            link(dve.tensor_copy(rowf[:, 1:2], rowi[:, 2:3]))
            dve.tensor_scalar(rowf[:, 2:3], rowf[:, 1:2], 8.0, None, ALU.mult)
            link(dve.tensor_scalar(rowf[:, 3:4], rowf[:, 1:2], 16.0, None, ALU.mult))
            link(dve.scalar_tensor_tensor(rowf[:, 0:1], rowf[:, 1:2], 8.0, rowf[:, 0:1], ALU.mult, ALU.add))
            dve.tensor_scalar(nmk[:, 1], nmk[:, 0], rowf[:, 2:3], NEG, ALU.is_lt, ALU.mult)
            link(dve.tensor_scalar(nmk[:, 2], nmk[:, 0], rowf[:, 0:1], NEG, ALU.is_gt, ALU.mult))
            tt(new_mask[:], nmk[:, 1], nmk[:, 2], ALU.add).then_inc(row_masks, 1)
            dve.tensor_scalar(csneg[:, 1], csneg[:, 0], rowf[:, 3:4], NEG, ALU.is_lt, ALU.mult)
            link(dve.tensor_scalar(csneg[:, 0], csneg[:, 0], rowf[:, 3:4], None, ALU.subtract))
            link(dve.tensor_scalar(csneg[:, 2], csneg[:, 0], float(SJ - 2), NEG, ALU.is_gt, ALU.mult))
            link(tt(csneg[:, 1], csneg[:, 1], csneg[:, 2], ALU.add))
            for k in range(2):
                o = take(("pre", k))
                link(dve.tensor_copy(cc[:, k:k + 1], o[:, 0:1]))
                empty(dve.tensor_scalar(cx[:, k, 0], o[:, 0:NBLK], cc[:, k:k + 1], None, ALU.add))
            o = take(("kc",))
            empty(dve.tensor_copy(kc[:], o[:, 0:NBLK]))
            o = take(("vcp",))
            dve.wait_ge(masks, 2)
            for g in range(4):
                ins = dve.tensor_copy(vcbd[32 * g:32 * g + 32, :, g], o[32 * g:32 * g + 32, 0:P].rearrange("p (k n) -> p k n", k=NKV))
            empty(ins)
            o = take(("vcs",))
            link(dve.memset(vcs[:], 0.0))
            dve.tensor_copy(vcs[:, 0:3], o[0:32, 0:3 * P].rearrange("p (t n) -> p t n", t=3))
            empty(dve.tensor_copy(vcs[0:31, 3], o[0:31, 3 * P:4 * P]))
            dve.wait_ge(gs_ld, 16 * 16)
            dve.wait_ge(gates_made, NT + 2)
            for what, i in attention_steps():
                if what == "score":
                    kind, b, r, h = ITEMS[i]
                    o = take(("s", i))
                    n = sum(item_keys(ITEMS[i]))
                    if kind in "ps":
                        dve.tensor_reduce(nm[:, i:i + 1], o[:, 0:n], axis=X, op=ALU.max, negate=True).then_inc(s_max, 1)
                    elif kind == "c":
                        v = o[:, 0:256].rearrange("p (h j) -> p h j", h=NH)
                        sv = sct[:].rearrange("p (h j) -> p h j", h=NH)
                        pv = pb[:, i % (T_LAG + 1), 0:256].rearrange("p (h j) -> p h j", h=NH)
                        link(tt(sv, v, cmneg[:, b:b + 1].broadcast_to([P, NH, 32]), ALU.add))
                        link(dve.tensor_reduce(mx8[:], sv, axis=X, op=ALU.max))
                        tt(sv, sv, mx8[:].unsqueeze(2).broadcast_to([P, NH, 32]), ALU.subtract).then_inc(s_max, 1)
                        dve.wait_ge(*emptied(("s", i)))
                        link(dve.tensor_reduce(rs8[:], pv, axis=X, op=ALU.add))
                        tt(pv, pv, cm01[:, b:b + 1].broadcast_to([P, NH, 32]), ALU.mult).then_inc(s_prob, 1)
                    else:
                        m = min(32, NBLK - (CJ_S + 2 * SJ * b))
                        if b:
                            dve.wait_ge(*emptied(("s", i - 3)))
                        if m < 32:
                            link(dve.memset(sct[:, 0:32], NEG))
                        link(tt(sct[:, 0:m], o[:, 0:m], csneg[:, 1, 0:m], ALU.add))
                        dve.tensor_reduce(nm[:, i:i + 1], sct[:, 0:32], axis=X, op=ALU.max, negate=True).then_inc(s_max, 1)
                elif what == "turn" and i % 2:
                    turn(dve, i, lambda d, s: dve.tensor_copy(d, s), take, empty)
                elif what == "gather":
                    g = i
                    last = GROUPS[g][-1]
                    kind, b, r, h = ITEMS[last]
                    o = ps[:, RING + g % 2, :]
                    dve.wait_ge(s_val, last + 1)
                    w = w8[:, g % 2]
                    if kind in "cp":
                        src = rs8[:] if kind == "c" else rs[:, GROUPS[g][0]:last + 1]
                        link(dve.reciprocal(w, src))
                        link(tt(w, w, tgate[:, b, r:3 * NH:3], ALU.mult))
                        wb = w.unsqueeze(2).broadcast_to([P, NH, HD])
                        ov = o.rearrange("p (h n) -> p h n", h=NH)
                        dst = ob[:, b % 2] if r == 0 else tmp_o[:]
                        if r == 0 and b >= 2:
                            dve.wait_ge(*emptied(("o", GROUP_OF[ITEMS.index(("p", b - 2, 2, NH - 1))])))
                        ins = tt(dst.rearrange("p (h n) -> p h n", h=NH), ov, wb, ALU.mult)
                        ins.then_inc(s_gath, 1)
                        dve.wait_ge(s_gath, g + 1)
                        if r:
                            ins = tt(ob[:, b % 2], ob[:, b % 2], tmp_o[:], ALU.add)
                            if r == 2:
                                ins.then_inc(osd_made, 1)
                            else:
                                link(ins)
                    else:
                        link(dve.reciprocal(w[:, 0:1], rs[:, last:last + 1]))
                        link(dve.tensor_scalar(w[:, 4:8], sel4[:], w[:, 0:1], tgate_s[:, b, r:r + 1], ALU.mult, ALU.mult))
                        wb = w[:, 4:8].unsqueeze(2).broadcast_to([P, 4, HD])
                        ov = o[:, 0:256].rearrange("p (h n) -> p h n", h=4)
                        dst = ob[:, b % 2, 0:256] if r == 0 else tmp_o[:, 0:256]
                        ins = tt(dst.rearrange("p (h n) -> p h n", h=4), ov, wb, ALU.mult)
                        ins.then_inc(s_gath, 1)
                        dve.wait_ge(s_gath, g + 1)
                        if r:
                            link(tt(ob[:, b % 2, 0:256], ob[:, b % 2, 0:256], tmp_o[:, 0:256], ALU.add))
                        if r == 2:
                            ow = ob[:, b % 2, 0:256].rearrange("p (h n) -> p n h", h=4)
                            if b >= 2:
                                dve.wait_ge(*emptied(("o", GROUP_OF[ITEMS.index(("s", b - 2, 2, 0))])))
                            dve.tensor_reduce(osd[:, b % 2, 0], ow, axis=X, op=ALU.add)
                            dve.tensor_reduce(osd[:, b % 2, 1], ow, axis=X, op=ALU.add).then_inc(osd_made, 1)
                elif what == "out":
                    kind, b, r, h = ITEMS[GROUPS[i][0]]
                    o = take(("o", i))
                    if kind == "p":
                        empty(dve.tensor_copy(onsaT[:, :, P * b:P * b + P], o.rearrange("p (k n) -> p k n", k=4)))
                    else:
                        at = NP_ + 2 * NDEC * b
                        for e in range(2):
                            dv = onsaT[HD * e:HD * e + HD, :, at:at + 2 * NDEC].rearrange("p k (a q) -> p a k q", a=2)
                            sv = o[HD * e:HD * e + HD, 0:P].rearrange("p (a k e q) -> p a k e q", a=2, k=4, e=2)[:, :, :, e]
                            ins = dve.tensor_copy(dv, sv)
                        empty(ins)
            for m in range(KD):
                for h in range(2):
                    dve.wait_ge(tg_ld[m % 4], 16 * (m // 4 + 1))
                    cut = slice(HALF * h, HALF * h + HALF)
                    for w, key in enumerate(("ab", "bb")):
                        o = take((key, m, h))
                        ins = dve.scalar_tensor_tensor(mt[:, w], gates[:, m % 4, w, cut], 1.0, o[:, 0:HALF], ALU.add, ALU.mult)
                        empty(ins)
                        dve.wait_ge(*emptied((key, m, h)))
                    tt(merged[:, m, cut], mt[:, 0], mt[:, 1], ALU.add).then_inc(merged_made, 1)
                    dve.wait_ge(merged_made, 2 * m + h + 1)
            dve.wait_ge(x_res, 16 * NT)
            def add_w_o(t, c):
                o = take(("wo", t, c))
                v = x[0:TILES[t], t, 512 * c:512 * c + 512]
                empty(dve.scalar_tensor_tensor(v, o[0:TILES[t], :], 0.25, v, ALU.mult, ALU.add))

            def norm_rows(t):
                p = TILES[t]
                dve.wait_ge(rstd_done, NT + t + 1)
                if t >= 2:
                    dve.wait_ge(pe_done, PLAN.done(("h2T", t - 2, 1)))
                    dve.wait_ge(h2_out[t % 2], 16 * (t // 2))
                dve.tensor_scalar(hn[0:p, t % 2], x[0:p, t], stat[0:p, 2, t:t + 1], None, ALU.mult).then_inc(hn_made, 1)
            for t in range(NT):
                add_w_o(t, 0)
            dve.wait_ge(rt_ld, 64)
            link(dve.memset(lg[:], 0.0))
            for t in range(NT):
                add_w_o(t, 1)
                norm_rows(t)
                if t >= 2:
                    router_logits(dve, t - 2, take, empty)
                if t >= 1:
                    turned_norm(dve, t - 1, ("h2T", t - 1), 1, take, empty)
            router_logits(dve, NT - 2, take, empty)
            turned_norm(dve, NT - 1, ("h2T", NT - 1), 1, take, empty)
            router_logits(dve, NT - 1, take, empty)
            dve.wait_ge(*emptied(("rt", NT - 1)))

            q = [P, NT, 4]
            G, E1, E2, S1, S2, T5 = (rtmp[:, j] for j in range(6))

            def first_of_largest(sel, v, mx):
                link(dve.tensor_reduce(mx, v, axis=X, op=ALU.max))
                link(tt(sel, v, mx.unsqueeze(2).broadcast_to(q), ALU.is_equal))
                for j in range(4):
                    ins = dve.tensor_scalar(T5[:, :, j:j + 1], sel[:, :, j:j + 1], float(4 - j), None, ALU.mult)
                link(ins)
                link(dve.tensor_reduce(rtmp[:, 7, :, 0], T5, axis=X, op=ALU.max))
                link(tt(sel, T5, rtmp[:, 7, :, 0].unsqueeze(2).broadcast_to(q), ALU.is_equal))

            gl = lg[:, :, 0:4]
            mxg, m1, m2 = rtmp[:, 6, :, 0], rtmp[:, 6, :, 1], rtmp[:, 6, :, 2]
            first_of_largest(G, gl, mxg)
            el = lg[:, :, 4:20].rearrange("p t (g e) -> p t g e", g=4)
            link(tt(picked, el, G.unsqueeze(3).broadcast_to([P, NT, 4, 4]), ALU.mult))
            link(dve.tensor_reduce(E1, picked.rearrange("p t g e -> p t e g"), axis=X, op=ALU.add))
            first_of_largest(S1, E1, m1)
            link(dve.scalar_tensor_tensor(E2, S1, NEG, E1, ALU.mult, ALU.add))
            first_of_largest(S2, E2, m2)
            tt(r16[:, :, 0:4], gl, mxg.unsqueeze(2).broadcast_to(q), ALU.subtract)
            tt(r16[:, :, 4:5], m2.unsqueeze(2), m1.unsqueeze(2), ALU.subtract).then_inc(lg_made, 1)
            n44 = [P, NT, 4, 4]
            for c, S in enumerate((S1, S2)):
                ins = tt(sel[:, c].rearrange("p t (g e) -> p t g e", g=4), G.unsqueeze(3).broadcast_to(n44),
                         S.unsqueeze(2).broadcast_to(n44), ALU.mult)
            link(ins)
            tt(msk_b[:], sel[:, 0], sel[:, 1], ALU.add).then_inc(msk_made, 1)
            link(dve.memset(rk[:], 0.0))
            dve.wait_ge(consts, 3)
            o = take(("rank",))
            dve.tensor_copy(rk[:, 0:4], o[:, 0:4 * NE].rearrange("p (t e) -> p t e", e=NE))
            link(dve.tensor_copy(rk[0:64, 4], o[0:64, 4 * NE:5 * NE]))
            dve.wait_ge(slot_nos, 1)
            link(dve.scalar_tensor_tensor(place[:], rk[:, :, 0:2], 1.0, msk_b[:, :, 0:2], ALU.add, ALU.mult))
            for e in range(2):
                for t in range(NT):
                    ins = dve.tensor_scalar(at_slot[:, e, t], slot_no[:], place[:, t, e:e + 1], None, ALU.is_equal)
            ins.then_inc(at_slots, 1)
            for c in range(2):
                tt(both[:, 0, c], sel[:, c], rk[:], ALU.mult)
                ins = tt(both[:, 1, c], sel[:, c], ebase[:].unsqueeze(1).broadcast_to([P, NT, NE]), ALU.mult)
            link(ins)
            for c in range(2):
                dve.tensor_reduce(rank[:, c], both[:, 0, c], axis=X, op=ALU.add)
                ins = dve.tensor_reduce(base[:, c], both[:, 1, c], axis=X, op=ALU.add)
            link(ins)
            dve.scalar_tensor_tensor(pos_i[:, 0], base[:], float(MAXR), rank[:], ALU.mult, ALU.add).then_inc(pos_made, 1)
            link(dve.tensor_reduce(rnd_f[:, 1:2], o[0:1, NT * NE:NT * NE + NE], axis=X, op=ALU.max))
            for k in range(1, MAXR):
                ins = dve.tensor_scalar(rnd_f[:, 1 + k:2 + k], rnd_f[:, 1:2], float(k * CAP), None, ALU.is_gt)
            link(ins)
            link(dve.tensor_reduce(rnd_f[:, 7:8], rnd_f[:, 2:1 + MAXR], axis=X, op=ALU.add))
            dve.tensor_scalar(rounds_i[:], rnd_f[:, 7:8], 1.0, None, ALU.add).then_inc(rounds_made, 1)
            empty(dve.memset(rnd_f[:, 0:1], 0.0))
            o = take(("first",))
            link(dve.tensor_copy(first_f[:], o[:, 0:4].rearrange("p (e c) -> p e c", e=2)))
            empty(tt(idx[:], first_f[:, :, 0], first_f[:, :, 1], ALU.add))
            dve.wait_ge(lg_exp, 1)
            link(dve.tensor_reduce(rtmp[:, 8, :, 0], r16[:, :, 0:4], axis=X, op=ALU.add))
            link(dve.tensor_scalar(rtmp[:, 8, :, 1], r16[:, :, 4], 1.0, None, ALU.add))
            link(tt(rtmp[:, 8, :, 0], rtmp[:, 8, :, 0], rtmp[:, 8, :, 1], ALU.mult))
            link(dve.reciprocal(rtmp[:, 8, :, 0], rtmp[:, 8, :, 0]))
            link(dve.tensor_scalar(wts[:, 0], rtmp[:, 8, :, 0], 0.5, None, ALU.mult))
            tt(wts[:, 1], wts[:, 0], r16[:, :, 4], ALU.mult)

            dve.sem_inc(hgt_made, 2)
            dve.sem_inc(x2_made, NT)
            for u in range(2):
                dve.sem_inc(hg_free[u], 1)
            dve.wait_ge(pos_made, 1)
            rounds = dve.value_load(rounds_i[0:1, 0:1], min_val=1, max_val=MAXR)

            def take_rows(j, n, u):
                for b in range(2):
                    dve.wait_ge(t_done, j * 32 + n * 2 + (b + 1))
                    ins = tt(hgT[:, u, 4 * b:4 * b + 4], ps[:, b].rearrange("p (k n) -> p k n", k=4),
                             g_cols[:, 1, 4 * b:4 * b + 4].unsqueeze(2).broadcast_to([P, 4, P]), ALU.mult)
                    ins.then_inc(hgt_made, 1)

            def activate(j, n, u):
                dve.wait_ge(th_made, j * 16 + n + 1)
                dve.scalar_tensor_tensor(th[:, u], th[:, u], 1.0, ps[:, 2 + u, 0:FF], ALU.add, ALU.mult).then_inc(si_made, 1)
                dve.wait_ge(si_made, j * 16 + n + 1)
                tt(si[:, u], th[:, u], ps[:, 2 + u, FF:2 * FF], ALU.mult).then_inc(act_made, 1)

            places = 4

            def place_link(j, ins, n):
                ins.then_inc(place_step, 1)
                dve.wait_ge(place_step, j * places + n)

            with dve.Fori(0, rounds) as j:
                dve.tensor_scalar(pos_f[:, 0], rank[:], 0.0, None, ALU.is_ge)
                place_link(j, dve.tensor_scalar(pos_f[:, 1], rank[:], float(CAP), None, ALU.is_lt), 1)
                place_link(j, tt(pos_f[:, 2], pos_f[:, 0], pos_f[:, 1], ALU.mult), 2)
                tt(wt_j[:], wts[:], pos_f[:, 2], ALU.mult)
                place_link(j, tt(pos_f[:, 3], rank[:], pos_f[:, 2], ALU.mult), 3)
                tt(pos_i[:, 1], pos_f[:, 3], base[:], ALU.add).then_inc(pos_made, 1)
                place_link(j, dve.tensor_scalar(rank[:], rank[:], float(CAP), None, ALU.subtract), 4)
                take_rows(j, 0, 0)
                activate(j, 0, 0)
                take_rows(j, 1, 1)
                with dve.Fori(0, NE // 2 - 1) as i:
                    activate(j, i * 2 + 1, 1)
                    take_rows(j, i * 2 + 2, 0)
                    activate(j, i * 2 + 2, 0)
                    take_rows(j, i * 2 + 3, 1)
                activate(j, NE - 1, 1)
                for t in range(NT):
                    p = TILES[t]
                    loaded = j * (16 * (3 - t % 2)) + 16 * (t // 2 + 1)
                    dve.wait_ge(yg_ld[t % 2][0], loaded)
                    dve.scalar_tensor_tensor(x[0:p, t], yg[0:p, t % 2, 0], wt_j[0:p, 0, t:t + 1], x[0:p, t], ALU.mult, ALU.add
                                             ).then_inc(x2_half, 1)
                    dve.wait_ge(yg_ld[t % 2][1], loaded)
                    dve.wait_ge(x2_half, j * NT + (t + 1))
                    dve.scalar_tensor_tensor(x[0:p, t], yg[0:p, t % 2, 1], wt_j[0:p, 1, t:t + 1], x[0:p, t], ALU.mult, ALU.add
                                             ).then_inc(x2_made, 1)

            def result(t):
                p = TILES[t]
                dve.wait_ge(rstd_done, 2 * NT + t + 1)
                dve.wait_ge(x3_made, 2 * t + 2)
                dve.scalar_tensor_tensor(x[0:p, t], x[0:p, t], stat[0:p, 2, t:t + 1], gf[0:p], ALU.mult, ALU.mult
                                         ).then_inc(y_made, 1)
            dve.wait_ge(gf_ld, 16)
            for t in range(NT):
                p = TILES[t]
                for c in range(2):
                    cut = slice(512 * c, 512 * c + 512)
                    dve.wait_ge(*emptied(("pg", t, c)))
                    link(dve.scalar_tensor_tensor(tpg[0:p, c], tpg[0:p, c], 1.0, pps[t][0:p, cut], ALU.add, ALU.mult))
                    dve.scalar_tensor_tensor(x[0:p, t, cut], tpg[0:p, c], 0.5, x[0:p, t, cut], ALU.mult, ALU.add
                                             ).then_inc(x3_made, 1)
                    if t and c == 0:
                        result(t - 1)
            result(NT - 1)


_INS = ["x_prompt", "x_sample", "p_prompt", "p_sample", "cache_cmp_kv", "cache_slc_kv", "cache_win_kv", "state_ssm",
        "page_table", "norm1_g", "w_in", "ssm_lam_re", "ssm_lam_im", "ssm_log_dt", "ssm_b_re", "ssm_b_im", "ssm_c_re",
        "ssm_c_im", "ssm_d", "w_glu", "b_glu", "cmp_pe", "cmp_w1", "cmp_w2", "w_ssm_out", "w_nsa_out", "w_o", "norm2_g",
        "w_route_group", "b_route_group", "w_route_expert", "b_route_expert", "w_exp_gate", "w_exp_up", "w_exp_down",
        "w_ple", "w_ple_gate", "final_norm_g"]
_OUTS = [(1, NP_, D), (NSEQ, NDEC, D), (1, 1, NP_, 2, NKV, HD), (1, 1, NP_, 2, NKV, HD), (1, 1, NP_, 2, NKV, HD),
         (1, 1, NG, NST, 2), (1, NSEQ, NDEC, 2, NKV, HD), (1, NSEQ, NDEC, 2, NKV, HD),
         (1, NSEQ, PAST + NDEC, 2, NKV, HD), (1, NSEQ, NG, NST, 2)]


def kernel(**inputs):
    import concourse.bacc as bacc
    from concourse.bass_utils import run_bass_kernel_spmd

    nc = bacc.Bacc("TRN2", target_bir_lowering=False, num_devices=1)
    arrays, ins, outs = {}, {}, []
    for name in _INS:
        a = np.ascontiguousarray(inputs[name])
        arrays[f"in_{name}"] = a
        ins[name] = nc.dram_tensor(f"in_{name}", a.shape, mybir.dt.from_np(a.dtype), kind="ExternalInput").ap()
    for i, shape in enumerate(_OUTS):
        outs.append(nc.dram_tensor(f"out_{i}", shape, F32, kind="ExternalOutput").ap())
    build(nc, ins, outs)
    r = run_bass_kernel_spmd(nc, [arrays], core_ids=[0])
    return tuple(r.results[0][f"out_{i}"] for i in range(len(_OUTS)))
```
